# Optimizing a Trainium2 kernel written in Bass

```python
import jax, jax.numpy as jnp
from jax import lax
import numpy as np

D_MODEL = 1024
BATCH = 1
SEQ = 256
DEPTH = 2

N_A = DEPTH // 2
N_B = DEPTH - N_A

GLA_HEADS = 4
GLA_QK = D_MODEL // 2
GLA_V = D_MODEL
GLA_HEAD_K = GLA_QK // GLA_HEADS
GLA_HEAD_V = GLA_V // GLA_HEADS
GATE_RANK = 16
GATE_TAU = 16.0
GLA_CHUNK = 64
GLA_IN = 2 * GLA_QK + 2 * GLA_V + GATE_RANK

SB_HEADS = 16
SB_HEAD_DIM = D_MODEL // SB_HEADS
BLOCK_Q = 128

D_FF = 4 * D_MODEL

DEEPNORM_ALPHA = (2.0 * DEPTH) ** 0.25
DEEPNORM_BETA = (8.0 * DEPTH) ** -0.25
LN_EPS = 1e-5
RMS_EPS = 1e-6


def layer_norm(x, g, b):
    xf = x.astype(jnp.float32)
    mu = jnp.mean(xf, axis=-1, keepdims=True)
    var = jnp.mean(jnp.square(xf - mu), axis=-1, keepdims=True)
    y = (xf - mu) * lax.rsqrt(var + LN_EPS)
    return (y * g.astype(jnp.float32) + b.astype(jnp.float32)).astype(x.dtype)

def gla_chunked(q, k, v, log_a):
    B, S, H, dk = q.shape
    dv = v.shape[-1]
    n = S // GLA_CHUNK

    def to_chunks(t):
        return t.astype(jnp.float32).reshape(B, n, GLA_CHUNK, H, t.shape[-1]).transpose(0, 3, 1, 2, 4)

    qc = to_chunks(q) * (dk ** -0.5)
    kc = to_chunks(k)
    vc = to_chunks(v)
    b = jnp.cumsum(to_chunks(log_a), axis=3)
    b_last = b[:, :, :, -1:, :]
    q_dec = qc * jnp.exp(b)
    k_dec = kc * jnp.exp(-b)
    k_end = kc * jnp.exp(b_last - b)

    causal = jnp.tril(jnp.ones((GLA_CHUNK, GLA_CHUNK), dtype=bool))
    att = jnp.where(causal, jnp.einsum('bhncd,bhnsd->bhncs', q_dec, k_dec), 0.0)
    o_intra = jnp.einsum('bhncs,bhnse->bhnce', att, vc)

    u = jnp.einsum('bhnsd,bhnse->bhnde', k_end, vc)
    decay = jnp.exp(b_last[:, :, :, 0, :])

    def step(state, inp):
        d_n, u_n = inp
        return d_n[..., None] * state + u_n, state

    init = jnp.zeros((B, H, dk, dv), jnp.float32)
    _, s_prev = lax.scan(step, init, (jnp.moveaxis(decay, 2, 0), jnp.moveaxis(u, 2, 0)))
    s_prev = jnp.moveaxis(s_prev, 0, 2)
    o_inter = jnp.einsum('bhncd,bhnde->bhnce', q_dec, s_prev)
    o = o_intra + o_inter
    return o.transpose(0, 2, 3, 1, 4).reshape(B, S, H, dv)

def gla_mixer(x, w_in, w_a2, b_a, norm_g, w_o):
    B, S, _ = x.shape
    proj = x @ w_in
    q, k, v, g, a1 = jnp.split(
        proj, [GLA_QK, 2 * GLA_QK, 2 * GLA_QK + GLA_V, 2 * GLA_QK + 2 * GLA_V], axis=-1)
    log_a = jax.nn.log_sigmoid((a1 @ w_a2 + b_a).astype(jnp.float32)) / GATE_TAU
    hk = lambda t: t.reshape(B, S, GLA_HEADS, GLA_HEAD_K)
    o = gla_chunked(hk(q), hk(k), v.reshape(B, S, GLA_HEADS, GLA_HEAD_V), hk(log_a))
    o = o * lax.rsqrt(jnp.mean(jnp.square(o), axis=-1, keepdims=True) + RMS_EPS)
    o = o * norm_g.astype(jnp.float32)
    o = o * jax.nn.silu(g.astype(jnp.float32).reshape(B, S, GLA_HEADS, GLA_HEAD_V))
    return o.reshape(B, S, GLA_V).astype(x.dtype) @ w_o

def stick_breaking_attention(q, k, v):
    S = q.shape[1]
    scale = SB_HEAD_DIM ** -0.5
    outs = []
    for i in range(S // BLOCK_Q):
        kv_len = (i + 1) * BLOCK_Q
        q_blk = q[:, i * BLOCK_Q:kv_len].astype(jnp.float32)
        k_blk = k[:, :kv_len].astype(jnp.float32)
        v_blk = v[:, :kv_len].astype(jnp.float32)
        z = jnp.einsum('bqhd,bkhd->bhqk', q_blk, k_blk) * scale
        t_idx = i * BLOCK_Q + jnp.arange(BLOCK_Q)
        s_idx = jnp.arange(kv_len)
        mask = s_idx[None, :] < t_idx[:, None]
        log_1m = jnp.where(mask, jax.nn.log_sigmoid(-z), 0.0)
        rev = lax.cumsum(log_1m, axis=3, reverse=True)
        log_w = jax.nn.log_sigmoid(z) + (rev - log_1m)
        w = jnp.where(mask, jnp.exp(log_w), 0.0)
        outs.append(jnp.einsum('bhqk,bkhd->bqhd', w, v_blk))
    return jnp.concatenate(outs, axis=1)

def sq_relu_mlp(x, w_up, w_down):
    h = jax.nn.relu(x @ w_up)
    return (h * h) @ w_down

def first_inputs(seed: int = 0) -> dict:
    key = jax.random.key(seed)
    ks = jax.random.split(key, 16)
    nrm = lambda k, shape, s: jax.random.normal(k, shape, jnp.float32) * s
    return {
        "x": nrm(ks[0], (BATCH, SEQ, D_MODEL), 1.0),
        "gla_w_in": nrm(ks[1], (N_A, D_MODEL, GLA_IN), D_MODEL ** -0.5),
        "gla_w_a2": nrm(ks[2], (N_A, GATE_RANK, GLA_QK), GATE_RANK ** -0.5),
        "gla_b_a": nrm(ks[3], (N_A, GLA_QK), 0.1),
        "gla_norm_g": 1.0 + nrm(ks[4], (N_A, GLA_HEAD_V), 0.02),
        "gla_w_o": nrm(ks[5], (N_A, GLA_V, D_MODEL), GLA_V ** -0.5 * DEEPNORM_BETA),
        "kv_w": nrm(ks[6], (D_MODEL, 2 * D_MODEL), D_MODEL ** -0.5),
        "sb_w_q": nrm(ks[7], (N_B, D_MODEL, D_MODEL), D_MODEL ** -0.5),
        "sb_w_o": nrm(ks[8], (N_B, D_MODEL, D_MODEL), D_MODEL ** -0.5 * DEEPNORM_BETA),
        "mlp_w_up": nrm(ks[9], (DEPTH, D_MODEL, D_FF), D_MODEL ** -0.5),
        "mlp_w_down": nrm(ks[10], (DEPTH, D_FF, D_MODEL), D_FF ** -0.5 * DEEPNORM_BETA),
        "ln_g": 1.0 + nrm(ks[11], (DEPTH, 2, D_MODEL), 0.02),
        "ln_b": nrm(ks[12], (DEPTH, 2, D_MODEL), 0.02),
    }

def first_block(x, gla_w_in, gla_w_a2, gla_b_a, gla_norm_g, gla_w_o, kv_w, sb_w_q, sb_w_o,
              mlp_w_up, mlp_w_down, ln_g, ln_b):
    B, S, D = x.shape
    h = x
    k_sh = None
    v_sh = None
    for layer in range(DEPTH):
        if layer < N_A:
            mix = gla_mixer(h, gla_w_in[layer], gla_w_a2[layer], gla_b_a[layer],
                            gla_norm_g[layer], gla_w_o[layer])
        else:
            j = layer - N_A
            if j == 0:
                kv = h @ kv_w
                k_sh = kv[..., :D].reshape(B, S, SB_HEADS, SB_HEAD_DIM)
                v_sh = kv[..., D:].reshape(B, S, SB_HEADS, SB_HEAD_DIM)
            q = (h @ sb_w_q[j]).reshape(B, S, SB_HEADS, SB_HEAD_DIM)
            o = stick_breaking_attention(q, k_sh, v_sh)
            mix = o.reshape(B, S, D).astype(h.dtype) @ sb_w_o[j]
        h = layer_norm(DEEPNORM_ALPHA * h + mix, ln_g[layer, 0], ln_b[layer, 0])
        h = layer_norm(DEEPNORM_ALPHA * h + sq_relu_mlp(h, mlp_w_up[layer], mlp_w_down[layer]),
                       ln_g[layer, 1], ln_b[layer, 1])
    return h


HEAD_DIM = 64
N_FOX_HEADS = D_MODEL // (2 * HEAD_DIM)
N_RET_HEADS = D_MODEL // (2 * HEAD_DIM)
FOX_WIDTH = N_FOX_HEADS * HEAD_DIM
RET_WIDTH = N_RET_HEADS * HEAD_DIM
MIX_WIDTH = FOX_WIDTH + RET_WIDTH
D_FF_2 = -(-8 * D_MODEL // (3 * 128)) * 128
CONV_WIDTH = 3
PLE_DIM = 256
Q_BLOCK = 128
RET_CHUNK = 128
ROPE_BASE = 10000.0
NORM_EPS = 1e-6
GN_EPS = 1e-5
IN_SIZES = (FOX_WIDTH, FOX_WIDTH, FOX_WIDTH, N_FOX_HEADS, RET_WIDTH, RET_WIDTH, RET_WIDTH, RET_WIDTH)
IN_WIDTH = sum(IN_SIZES)
SPLIT_POINTS = tuple(int(v) for v in np.cumsum(IN_SIZES)[:-1])


def rms_norm(x, w):
    xf = x.astype(jnp.float32)
    y = xf * lax.rsqrt(jnp.mean(xf * xf, axis=-1, keepdims=True) + NORM_EPS)
    return (y * w.astype(jnp.float32)).astype(x.dtype)

def split_heads(t, n_heads):
    b, s, _ = t.shape
    return t.reshape(b, s, n_heads, HEAD_DIM)

def rotary_tables(seq):
    inv_freq = ROPE_BASE ** (-jnp.arange(0, HEAD_DIM, 2, dtype=jnp.float32) / HEAD_DIM)
    ang = jnp.arange(seq, dtype=jnp.float32)[:, None] * inv_freq[None, :]
    return jnp.cos(ang), jnp.sin(ang)

def apply_rotary(t, cos, sin):
    half = HEAD_DIM // 2
    t1, t2 = t[..., :half], t[..., half:]
    c = cos[None, :, None, :]
    s = sin[None, :, None, :]
    return jnp.concatenate([t1 * c - t2 * s, t1 * s + t2 * c], axis=-1).astype(t.dtype)

def forgetting_attention(q, k, v, f_logit):
    b, s, h, d = q.shape
    q = q.transpose(0, 2, 1, 3)
    k = k.transpose(0, 2, 1, 3)
    v = v.transpose(0, 2, 1, 3)
    log_f = jax.nn.log_sigmoid(f_logit.astype(jnp.float32))
    cum = jnp.cumsum(log_f, axis=1).transpose(0, 2, 1)
    scale = HEAD_DIM ** -0.5
    kpos = jnp.arange(s)
    n_blocks = s // Q_BLOCK

    def one_block(bi):
        start = bi * Q_BLOCK
        qb = lax.dynamic_slice_in_dim(q, start, Q_BLOCK, axis=2)
        cq = lax.dynamic_slice_in_dim(cum, start, Q_BLOCK, axis=2)
        logits = jnp.einsum('bhqd,bhkd->bhqk', qb, k).astype(jnp.float32) * scale
        logits = logits + cq[..., :, None] - cum[..., None, :]
        qpos = start + jnp.arange(Q_BLOCK)
        logits = jnp.where(kpos[None, :] <= qpos[:, None], logits, -jnp.inf)
        probs = jax.nn.softmax(logits, axis=-1)
        return jnp.einsum('bhqk,bhkd->bhqd', probs.astype(v.dtype), v)

    out = lax.map(one_block, jnp.arange(n_blocks))
    return out.transpose(1, 0, 3, 2, 4).reshape(b, s, h * d)

def chunkwise_retention(q, k, v, log_gamma):
    b, s, h, d = q.shape
    n_chunks = s // RET_CHUNK

    def to_chunks(t):
        return t.reshape(b, n_chunks, RET_CHUNK, h, d).transpose(1, 0, 3, 2, 4)

    idx = jnp.arange(RET_CHUNK, dtype=jnp.float32)
    rel = idx[:, None] - idx[None, :]
    lg = log_gamma[:, None, None]
    intra_decay = jnp.where(rel >= 0, jnp.exp(lg * jnp.maximum(rel, 0.0)), 0.0)
    q_decay = jnp.exp(log_gamma[:, None] * (idx + 1.0))
    k_decay = jnp.exp(log_gamma[:, None] * (RET_CHUNK - 1.0 - idx))
    chunk_decay = jnp.exp(log_gamma * RET_CHUNK)

    def step(state, qkv):
        qc, kc, vc = qkv
        scores = jnp.einsum('bhid,bhjd->bhij', qc, kc) * intra_decay
        inner = jnp.einsum('bhij,bhje->bhie', scores, vc)
        cross = jnp.einsum('bhid,bhde->bhie', qc, state) * q_decay[:, :, None]
        new_state = state * chunk_decay[:, None, None] + jnp.einsum(
            'bhjd,bhje->bhde', kc * k_decay[:, :, None], vc)
        return new_state, inner + cross

    state0 = jnp.zeros((b, h, d, d), jnp.float32)
    _, out = lax.scan(step, state0, (to_chunks(q), to_chunks(k), to_chunks(v)))
    return out.transpose(1, 0, 3, 2, 4).reshape(b, s, h, d)

def head_group_norm(y):
    yf = y.astype(jnp.float32)
    mu = jnp.mean(yf, axis=-1, keepdims=True)
    var = jnp.mean(jnp.square(yf - mu), axis=-1, keepdims=True)
    return (yf - mu) * lax.rsqrt(var + GN_EPS)

def causal_depthwise_conv(a, w, bias):
    s = a.shape[1]
    ap = jnp.pad(a, ((0, 0), (CONV_WIDTH - 1, 0), (0, 0)))
    y = bias
    for j in range(CONV_WIDTH):
        y = y + ap[:, j:j + s, :] * w[j]
    return y

def gated_conv_ffn(u, w_up, conv_w, conv_b, w_down):
    up = u @ w_up
    a, g = up[..., :D_FF_2], up[..., D_FF_2:]
    a = causal_depthwise_conv(a, conv_w, conv_b)
    return (jax.nn.gelu(a, approximate=False) * g) @ w_down

def second_inputs(seed: int = 0) -> dict:
    key = jax.random.key(seed)
    ks = jax.random.split(key, 16)
    nrm = jax.random.normal
    f32 = jnp.float32
    return {
        'x': nrm(ks[0], (BATCH, SEQ, D_MODEL), f32),
        'p': nrm(ks[1], (DEPTH, BATCH, SEQ, PLE_DIM), f32),
        'attn_norm_w': 1.0 + 0.05 * nrm(ks[2], (DEPTH, D_MODEL), f32),
        'w_in': nrm(ks[3], (DEPTH, D_MODEL, IN_WIDTH), f32) * D_MODEL ** -0.5,
        'forget_bias': 2.0 + 0.1 * nrm(ks[4], (DEPTH, N_FOX_HEADS), f32),
        'w_out': nrm(ks[5], (DEPTH, MIX_WIDTH, D_MODEL), f32) * MIX_WIDTH ** -0.5,
        'ffn_norm_w': 1.0 + 0.05 * nrm(ks[6], (DEPTH, D_MODEL), f32),
        'w_up': nrm(ks[7], (DEPTH, D_MODEL, 2 * D_FF_2), f32) * D_MODEL ** -0.5,
        'conv_w': nrm(ks[8], (DEPTH, CONV_WIDTH, D_FF_2), f32) * CONV_WIDTH ** -0.5,
        'conv_b': 0.01 * nrm(ks[9], (DEPTH, D_FF_2), f32),
        'w_down': nrm(ks[10], (DEPTH, D_FF_2, D_MODEL), f32) * D_FF_2 ** -0.5,
        'ple_norm_w': 1.0 + 0.05 * nrm(ks[11], (DEPTH, D_MODEL), f32),
        'w_ple_gate': nrm(ks[12], (DEPTH, D_MODEL, D_MODEL), f32) * D_MODEL ** -0.5,
        'w_ple_proj': nrm(ks[13], (DEPTH, PLE_DIM, D_MODEL), f32) * PLE_DIM ** -0.5,
        'final_norm_w': 1.0 + 0.05 * nrm(ks[14], (D_MODEL,), f32),
    }

def second_block(x, p, attn_norm_w, w_in, forget_bias, w_out, ffn_norm_w, w_up, conv_w, conv_b,
              w_down, ple_norm_w, w_ple_gate, w_ple_proj, final_norm_w):
    seq = x.shape[1]
    cos, sin = rotary_tables(seq)
    log_gamma = jnp.log1p(-jnp.exp2(-5.0 - jnp.arange(N_RET_HEADS, dtype=jnp.float32)))
    h = x
    for i in range(DEPTH):
        u = rms_norm(h, attn_norm_w[i])
        proj = u @ w_in[i]
        fq, fk, fv, f_logit, rq, rk, rv, rg = jnp.split(proj, SPLIT_POINTS, axis=-1)
        fox = forgetting_attention(split_heads(fq, N_FOX_HEADS), split_heads(fk, N_FOX_HEADS),
                                   split_heads(fv, N_FOX_HEADS), f_logit + forget_bias[i])
        rq_h = apply_rotary(split_heads(rq, N_RET_HEADS), cos, sin)
        rk_h = apply_rotary(split_heads(rk, N_RET_HEADS), cos, sin) * (HEAD_DIM ** -0.5)
        ret = chunkwise_retention(rq_h, rk_h, split_heads(rv, N_RET_HEADS), log_gamma)
        ret = head_group_norm(ret).reshape(ret.shape[0], seq, RET_WIDTH)
        ret = (jax.nn.silu(rg.astype(jnp.float32)) * ret).astype(x.dtype)
        mixed = jnp.concatenate([fox.astype(x.dtype), ret], axis=-1)
        h = h + mixed @ w_out[i]
        h = h + gated_conv_ffn(rms_norm(h, ffn_norm_w[i]), w_up[i], conv_w[i], conv_b[i], w_down[i])
        gate = jax.nn.sigmoid(rms_norm(h, ple_norm_w[i]) @ w_ple_gate[i])
        h = h + gate * (p[i] @ w_ple_proj[i])
    return rms_norm(h, final_norm_w)


def setup_inputs(seed=0):
    out = dict(first_inputs(seed))
    for name, value in second_inputs(seed + 1).items():
        if name != "x":
            out[name + "_2"] = value
    return out


def reference(
    x, gla_w_in, gla_w_a2, gla_b_a, gla_norm_g, gla_w_o, kv_w, sb_w_q, sb_w_o, mlp_w_up,
    mlp_w_down, ln_g, ln_b, p_2, attn_norm_w_2, w_in_2, forget_bias_2, w_out_2, ffn_norm_w_2,
    w_up_2, conv_w_2, conv_b_2, w_down_2, ple_norm_w_2, w_ple_gate_2, w_ple_proj_2,
    final_norm_w_2,
):
    x = first_block(
        x, gla_w_in, gla_w_a2, gla_b_a, gla_norm_g, gla_w_o, kv_w, sb_w_q, sb_w_o, mlp_w_up,
        mlp_w_down, ln_g, ln_b,
    )
    return second_block(
        x, p_2, attn_norm_w_2, w_in_2, forget_bias_2, w_out_2, ffn_norm_w_2, w_up_2, conv_w_2,
        conv_b_2, w_down_2, ple_norm_w_2, w_ple_gate_2, w_ple_proj_2, final_norm_w_2,
    )


_drawn_inputs = setup_inputs


def setup_inputs(seed=0):
    import zlib

    import numpy as np

    out = dict(_drawn_inputs(seed))
    spreads = {}
    factors = {'gla_b_a': 4.48,
     'gla_norm_g': 8.0,
     'forget_bias_2': 25.52,
     'conv_b_2': 8.0,
     'ple_norm_w_2': 5.037}
    for name, (base, spread) in spreads.items():
        noise = np.random.default_rng([zlib.crc32(name.encode()), seed]).standard_normal(out[name].shape)
        drawn = base * np.exp(spread * noise) if base else spread * noise
        out[name] = __import__('jax').numpy.asarray(drawn.astype(out[name].dtype))
    for name, factor in factors.items():
        out[name] = (out[name] * factor).astype(out[name].dtype)
    return out
```

```python
import concourse.bass as bass
from concourse import mybir
from contextlib import ExitStack
import numpy as np

S = 256
D = 1024
NT = D // 128
FF = 4096
FF2 = 2816
DEPTH = 2
CW = 2048
N_UP = FF // 256
N_FF = FF2 // 256
FT = FF2 // 128
ALPHA = (2.0 * DEPTH) ** 0.25
LN_EPS, RMS_EPS = 1e-5, 1e-6
GN_EPS = LN_EPS
GLA_H, SB_H, FOX_H, RET_H = 4, 16, 8, 8
GLA_SCALE = 128 ** -0.5

C_GLA_IN = 0
C_GLA_O = C_GLA_IN + 12
C_MLP = [C_GLA_O + 4, 0]
C_SB_IN = C_MLP[0] + 2 * N_UP
C_SB_O = C_SB_IN + 12
C_MLP[1] = C_SB_O + 4
C_B2 = C_MLP[1] + 2 * N_UP
PER_B2 = 14 + 4 + 3 * N_FF + 1 + 4
C_IN = [C_B2 + PER_B2 * n for n in range(DEPTH)]
C_OUT = [c + 14 for c in C_IN]
C_FFN = [c + 18 for c in C_IN]
C_PROJ = [c + 3 * N_FF for c in C_FFN]
C_GATE = [c + 1 for c in C_PROJ]
N_CHUNKS = C_B2 + PER_B2 * DEPTH

RAW, SPLIT = 6, 3
AHEAD = 2

FREE = dict(gla_in=0, mlp0=12, sb_in=12 + N_UP, mlp1=24 + N_UP, in0=24 + 2 * N_UP, in1=38 + 2 * N_UP)
ZERO = dict(mlp0=0, mlp1=1, ffn0=2, ple0=3, ffn1=4, ple1=5)
H_OF = {1: 0, 2: 4, 3: 8, 5: 12, 6: 16, 7: 20, 8: 22, 9: 26, 10: 30, 11: 34, 12: 36, 13: 40}

PV = dict(ln_g=0, ln_b=32, b_a=64, gla_g=68, attn_w=70, ffn_w=86, ple_w=102, fin_w=118, conv_w=126,
          conv_b=126 + 6 * FT)
NPV = 126 + 8 * FT
CONST = dict(ident=0, ones=128, blk=384, tri=512, neg=640, perm=768, scan=896, mask=1152, cos=1536, sin=1792, eps=2048)
NCONST = 2050


def build_program(nc, xT, wstream, wa1, wa2, wf, fbias, pT, params, consts, decay, out):
    f32, f32r = mybir.dt.float32, mybir.dt.float32r
    ALU, ACT = mybir.AluOpType, mybir.ActivationFunctionType
    ctx = ExitStack()
    with ctx:
        def sb(name, shape, dt=f32):
            return ctx.enter_context(nc.sbuf_tensor(name, shape, dt))

        def sem(name):
            return ctx.enter_context(nc.semaphore(name))

        raw = sb("raw", [128, RAW, CW])
        whi = sb("whi", [128, SPLIT, CW], f32r)
        wlo = sb("wlo", [128, SPLIT, CW], f32r)
        hT = sb("hT", [128, NT, S])
        xhi = sb("xhi", [128, NT, S], f32r)
        xlo = sb("xlo", [128, NT, S], f32r)
        y = sb("y", [128, NT, S])
        sq = sb("sq", [128, NT, S])
        qT = sb("qT", [128, NT, S])
        kT = sb("kT", [128, NT, S])
        v = sb("v", [128, 2, D])
        gT = sb("gT", [128, NT, S])
        hhi = sb("hhi", [128, 3, 2, S], f32r)
        hlo = sb("hlo", [128, 3, 2, S], f32r)
        misc = sb("misc", [128, 3072])
        cst = sb("cst", [128, NCONST])
        pv = sb("pv", [128, NPV])
        wa1_sb = sb("wa1_sb", [128, NT, 16])
        wa2_sb = sb("wa2_sb", [16, 512])
        wf_sb = sb("wf_sb", [128, DEPTH, NT, FOX_H])
        fb_sb = sb("fb_sb", [FOX_H, DEPTH])
        low_rank = sb("low_rank", [16, 3, S])
        a1_sb, cum = low_rank[:, 0, :], low_rank[0:FOX_H, :, :]
        stat = sb("stat", [128, 4, 8])

        def const(name, n):
            return cst[:, CONST[name]:CONST[name] + n]

        def par(name, i):
            return pv[:, PV[name] + i:PV[name] + i + 1]

        ident, blk, tri, neg, perm = (const(n, 128) for n in ("ident", "blk", "tri", "neg", "perm"))
        ones = const("ones", 128)
        cosT, sinT, scanm, maskadd = const("cos", S), const("sin", S), const("scan", S), const("mask", 384)

        eps_col = {LN_EPS: const("eps", 1), RMS_EPS: const("eps", 2)[:, 1:2]}

        def flat(t):
            return t[:, :, :].rearrange("p t s -> p (t s)")

        yf, sqf, qf, kf, gf = (flat(t) for t in (y, sq, qT, kT, gT))
        rs = misc[:, 2048:3072]
        rs1 = misc[:, 2048:2304]
        dec = misc[:, 0:2048].rearrange("p (h s) -> p h s", h=RET_H)

        def wide(ap, n):
            return ap.unsqueeze(1).to_broadcast([ap.shape[0], n, ap.shape[1]])

        def pair(t, j):
            return t[:, 2 * j:2 * j + 2, :]

        def two(ap):
            return ap.rearrange("p (t s) -> p t s", t=2)

        acc = ctx.enter_context(nc.psum_tensor("acc", [128, NT, S], f32))
        ring = ctx.enter_context(nc.psum_tensor("ring", [128, 4, 512], f32))

        def bank(i):
            return ring[:, i, :]

        raw_in = [sem(f"raw_in{i}") for i in range(RAW)]
        hi_made, lo_made = sem("hi_made"), sem("lo_made")
        chunk_used = sem("chunk_used")
        gemm_free = sem("gemm_free")
        const_in, x_in, par_in, dec_in, p_in = (sem(n) for n in ("const_in", "x_in", "par_in", "dec_in", "p_in"))
        out_made, out_in = sem("out_made"), sem("out_in")
        acc_zero, acc_done = sem("acc_zero"), sem("acc_done")
        xh_made, x_made, h_made = sem("xh_made"), sem("x_made"), sem("h_made")
        y_made, mean_done, yc_made = sem("y_made"), sem("mean_done"), sem("yc_made")
        sq_made, var_done, rs_made = (sem(n) for n in ("sq_made", "var_done", "rs_made"))
        hid_sq, hid_hi, hid_lo = sem("hid_sq"), sem("hid_hi"), sem("hid_lo")
        a_copied, conv_step, conv_made, gelu_made = (sem(n) for n in ("a_copied", "conv_step", "conv_made", "gelu_made"))
        prod_made, prod_hi, prod_lo = sem("prod_made"), sem("prod_hi"), sem("prod_lo")
        p_hi, p_lo, sig_made = sem("p_hi"), sem("p_lo"), sem("sig_made")
        dve_own, act_own, pool_own = sem("dve_own"), sem("act_own"), sem("pool_own")
        (a1_done, a1_copied, gate_done, g_ln, g_cum, g_exp, g_kend, g_dec, g_attd, g_attc, g_attm, g_ktd, g_ktc,
         g_ud, g_st, g_od, g_sq, g_var, g_rs) = (sem("gla_" + n) for n in (
             "a1_done", "a1_copied", "gate_done", "ln", "cum", "exp", "kend", "dec", "attd", "attc", "attm",
             "ktd", "ktc", "ud", "st", "od", "sq", "var", "rs"))
        s_z, s_ln, s_sp, s_L, s_lw, s_w, s_wm, s_o = (sem("sb_" + n) for n in ("z", "ln", "sp", "L", "lw", "w", "wm", "o"))
        f_log, f_ln, f_cum, f_z, f_mx, f_e, f_p, f_td, f_tc, f_o = (
            sem("fox_" + n) for n in ("log", "lnf", "cum", "z", "mx", "e", "p", "td", "tc", "o"))
        r_rot, r_rdy, r_s, r_m, r_o, r_c, r_mean, r_yc, r_sq, r_var, r_rs = (
            sem("ret_" + n) for n in ("rot", "rdy", "s", "m", "o", "c", "mean", "yc", "sq", "var", "rs"))

        class Own:

            def __init__(self, eng, s):
                self.eng, self.s, self.n = eng, s, 0

            def mark(self, ins):
                self.n += 1
                ins.then_inc(self.s, 1)
                return self.n

            def need(self, n):
                self.eng.wait_ge(self.s, n)

            def sync(self, ins):
                self.need(self.mark(ins))

        block = ctx.enter_context(nc.Block())

        @block.sync
        def _(sp):
            sp.dma_start(hT[:, :, :], xT).then_inc(x_in, 16)
            for c in range(RAW):
                sp.dma_start(raw[:, c, :], wstream[c]).then_inc(raw_in[c], 16)
            with sp.Fori(1, N_CHUNKS // RAW) as m:
                for j in range(RAW):
                    sp.wait_ge(lo_made, m * RAW + (j + 1 - RAW))
                    sp.dma_start(raw[:, j, :], wstream[m * RAW + j]).then_inc(raw_in[j], 16)
            for c in range(N_CHUNKS // RAW * RAW, N_CHUNKS):
                sp.wait_ge(lo_made, c + 1 - RAW)
                sp.dma_start(raw[:, c % RAW, :], wstream[c]).then_inc(raw_in[c % RAW], 16)
            for j in range(4):
                sp.wait_ge(out_made, j + 1)
                sp.dma_start(out[:, 2 * j:2 * j + 2, :], pair(y, j)).then_inc(out_in, 16)
            sp.wait_ge(out_in, 4 * 16)

        def split_hi(act, c, m=0):
            if c >= N_CHUNKS:
                return
            act.wait_ge(raw_in[c % RAW], m * 16 + 16 * (c // RAW + 1))
            if c >= SPLIT:
                act.wait_ge(chunk_used, m * RAW + (c - SPLIT + 1))
            act.copy(whi[:, c % SPLIT, :], raw[:, c % RAW, :]).then_inc(hi_made, 1)

        def split_lo(dve, c, m=0):
            if c >= N_CHUNKS:
                return
            dve.wait_ge(hi_made, m * RAW + (c + 1))
            if c >= SPLIT:
                dve.wait_ge(chunk_used, m * RAW + (c - SPLIT + 1))
            dve.tensor_tensor(wlo[:, c % SPLIT, :], raw[:, c % RAW, :], whi[:, c % SPLIT, :].bitcast(f32),
                              ALU.subtract).then_inc(lo_made, 1)

        @block.tensor
        def _(pe):
            def three(o, l1, l2, r1, r2, start, stop, **kw):
                pe.matmul(o, l1, r1, start=start, stop=False, **kw)
                pe.matmul(o, l1, r2, start=False, stop=False, **kw)
                return pe.matmul(o, l2, r1, start=False, stop=stop, **kw)

            def gemm(c, b, x_need=None, tokens_out=False, m=0):
                pe.wait_ge(lo_made, m * RAW + (c + 1))
                wh, wl = whi[:, c % SPLIT, :], wlo[:, c % SPLIT, :]
                for t in range(2):
                    o = bank(b)[:, t * 256:t * 256 + 256]
                    for k in range(NT):
                        if x_need is not None and t == 0 and k % 2 == 0:
                            pe.wait_ge(x_made, 4 * x_need + k // 2 + 1)
                        if tokens_out:
                            tok, w = slice(t * 128, t * 128 + 128), slice(k * 256, k * 256 + 256)
                            mm = three(o, xhi[:, k, tok], xlo[:, k, tok], wh[:, w], wl[:, w], k == 0, k == NT - 1)
                        else:
                            w = slice(k * 256 + t * 128, k * 256 + t * 128 + 128)
                            mm = three(o, wh[:, w], wl[:, w], xhi[:, k, :], xlo[:, k, :], k == 0, k == NT - 1)
                mm.then_inc(chunk_used, 1)

            def down(c, s, m=0, last=False):
                pe.wait_ge(lo_made, m * RAW + (c + 1))
                for k in range(2):
                    for t in range(NT):
                        w = slice(k * D + t * 128, k * D + t * 128 + 128)
                        mm = three(acc[:, t, :], whi[:, c % SPLIT, w], wlo[:, c % SPLIT, w], hhi[:, s, k, :],
                                   hlo[:, s, k, :], False, False, skip_group_check=True)
                        if last and k == 1 and t % 2 and t < NT - 1:
                            mm.then_inc(acc_done, 1)
                mm.then_inc(chunk_used, 1)

            def sums(src, made, base, o, done):
                for t in range(NT):
                    if t % 2 == 0:
                        pe.wait_ge(made, base + t // 2 + 1)
                    mm = pe.matmul(o, ones, src[:, t, :], start=(t == 0), stop=(t == NT - 1))
                mm.then_inc(done, 1)

            def layer_norm(n):
                sums(y, y_made, 4 * n, bank(0)[:, 0:S], mean_done)
                sums(sq, sq_made, 4 * n, bank(1)[:, 0:S], var_done)

            def rms_norm(n):
                sums(sq, sq_made, 4 * (4 + n), bank(0)[:, 0:S], var_done)

            def product(c, x_need):
                for j in range(4):
                    gemm(c + j, j, x_need if j == 0 else None)

            def wide_product(c, n, free, x_need, tokens, between):
                for j in range(n):
                    if j >= 4:
                        pe.wait_ge(gemm_free, free + j - 3)
                    gemm(c + j, j % 4, x_need if j == 0 else None, j in tokens)
                    if j in between:
                        between[j]()
                pe.wait_ge(gemm_free, free + n)

            def mlp(n, x_need):
                c0, free, h0 = C_MLP[n], FREE[f"mlp{n}"], N_UP * n
                gemm(c0, 0, x_need)
                pe.wait_ge(acc_zero, ZERO[f"mlp{n}"] + 1)
                with pe.Fori(0, (N_UP - 1) // 3) as m:
                    for i in range(1, 4):
                        cu = c0 + 2 * i - 1
                        pe.wait_ge(gemm_free, m * 3 + (free + i - 2))
                        gemm(cu, i % 3, m=m)
                        pe.wait_ge(hid_lo, m * 3 + (h0 + i))
                        down(cu + 1, (i - 1) % 3, m=m)
                pe.wait_ge(hid_lo, h0 + N_UP)
                down(c0 + 2 * N_UP - 1, (N_UP - 1) % 3, last=True)

            def ffn(L, x_need):
                c0, b = C_FFN[L], N_FF * L
                gemm(c0, 0, x_need)
                gemm(c0 + 1, 1)
                pe.wait_ge(acc_zero, ZERO[f"ffn{L}"] + 1)
                with pe.Fori(0, (N_FF - 1) // 2) as m:
                    for i in range(1, 3):
                        ca = c0 + 3 * i - 1
                        pe.wait_ge(a_copied, m * 2 + (b + i))
                        gemm(ca, 2 * (i % 2), m=m)
                        pe.wait_ge(prod_made, m * 2 + (b + i))
                        gemm(ca + 1, 2 * (i % 2) + 1, m=m)
                        pe.wait_ge(prod_lo, m * 2 + (b + i))
                        down(ca + 2, (i - 1) % 2, m=m)
                pe.wait_ge(prod_lo, b + N_FF)
                down(c0 + 3 * N_FF - 1, (N_FF - 1) % 2, last=True)

            def head(h):
                return slice(64 * (h % 2), 64 * (h % 2) + 64)

            def scores(b, l, r):
                pe.matmul(b[:, 0:256], l[:, 0:128], r, start=True, stop=False, skip_group_check=True)
                return pe.matmul(b[:, 256:384], l[:, 128:256], r[:, 128:256], start=False, stop=False,
                                 skip_group_check=True)

            def values(t, h, col, W):
                o = acc[head(h), t, :]
                pe.matmul(o, v[:, 0, col:col + 64], W[:, 0:256], start=True, stop=False, skip_group_check=True)
                return pe.matmul(o[:, 128:256], v[:, 1, col:col + 64], W[:, 256:384], start=False, stop=True,
                                 skip_group_check=True)

            def gate_input():
                pe.wait_ge(x_in, 16)
                pe.wait_ge(par_in, 5 * 16)
                pe.wait_ge(const_in, 16)
                for k in range(NT):
                    mm = pe.matmul(acc[0:16, 0, :], wa1_sb[:, k, :], hT[:, k, :], start=(k == 0), stop=(k == NT - 1))
                mm.then_inc(a1_done, 1)

            def gate_logits():
                pe.wait_ge(a1_copied, 1)
                for h in range(GLA_H):
                    mm = pe.matmul(acc[:, 2 + h, :], wa2_sb[:, h * 128:h * 128 + 128], a1_sb,
                                   start=(h % 2 == 0), stop=True, skip_group_check=True)
                mm.then_inc(gate_done, 1)

            wide_product(C_GLA_IN, 12, FREE["gla_in"], 0, range(4, 8), {0: gate_input, 1: gate_logits})
            for h in range(GLA_H):
                pe.wait_ge(g_kend, h + 1)
                for t in range(2):
                    mm = pe.transpose(ring[:, t, h * 128:h * 128 + 128], kT[:, 4 + h, t * 128:t * 128 + 128], ident)
            mm.then_inc(g_ktd, 1)
            pe.wait_ge(g_dec, 1)
            for t in range(2):
                tok = slice(t * 128, t * 128 + 128)
                for h in range(GLA_H):
                    mm = pe.matmul(ring[:, 2 + t, h * 128:h * 128 + 128], kT[:, h, tok], qT[:, h, tok],
                                   start=True, stop=True)
                mm.then_inc(g_attd, 1)
            pe.wait_ge(g_ktc, 1)
            keT = two(yf[:, 0:1024])
            for n in range(3):
                r = slice(64 * (n % 2), 64 * (n % 2) + 64)
                if n:
                    pe.wait_ge(g_st, n)
                for h in range(GLA_H):
                    mm = pe.matmul(ring[:, h // 2, (h % 2) * 256:(h % 2) * 256 + 256],
                                   keT[r, n // 2, h * 128:h * 128 + 128], v[r, n // 2, h * 256:h * 256 + 256],
                                   start=True, stop=True)
                mm.then_inc(g_ud, 1)
            pe.wait_ge(g_attm, 2)
            pe.wait_ge(g_st, 3)
            attm = two(sqf[:, 1024:2048])
            for h in range(GLA_H):
                for e in range(2):
                    ec = h * 256 + e * 128
                    for t in range(2):
                        pe.matmul(acc[:, 2 * h + e, t * 128:t * 128 + 128], v[:, t, ec:ec + 128],
                                  attm[:, t, h * 128:h * 128 + 128], start=True, stop=False, skip_group_check=True)
                        for n in (2 * t, 2 * t + 1):
                            if n:
                                sc = (n - 1) * 1024 + ec
                                mm = pe.matmul(acc[:, 2 * h + e, n * 64:n * 64 + 64], misc[:, sc:sc + 128],
                                               qT[:, h, n * 64:n * 64 + 64], start=False, stop=True,
                                               skip_group_check=True)
                mm.then_inc(g_od, 1)
            for h in range(GLA_H):
                pe.wait_ge(g_sq, h + 1)
                for e in range(2):
                    mm = pe.matmul(ring[:, 2 + h // 2, (h % 2) * 256:(h % 2) * 256 + 256], ones, sq[:, 2 * h + e, :],
                                   start=(e == 0), stop=(e == 1))
                if h % 2:
                    mm.then_inc(g_var, 1)
            product(C_GLA_O, 1)
            layer_norm(0)
            mlp(0, 2)
            layer_norm(1)

            wide_product(C_SB_IN, 12, FREE["sb_in"], 3, range(4, 8), {})
            for i in range(SB_H + 3):
                if i < SB_H:
                    h = i
                    if h >= 4:
                        pe.wait_ge(s_w, h - 3)
                    scores(bank(h % 4), kT[head(h), h // 2, :], qT[head(h), h // 2, :]).then_inc(s_z, 1)
                if 0 <= i - 1 < SB_H:
                    h = i - 1
                    b, L = bank(h % 4), yf[:, (h % 2) * 384:(h % 2) * 384 + 384]
                    pe.wait_ge(s_L, h + 1)
                    pe.matmul(b[:, 0:256], tri, L[:, 0:256], start=False, stop=False, skip_group_check=True)
                    pe.matmul(b[:, 128:256], neg, L[:, 256:384], start=False, stop=False, skip_group_check=True)
                    pe.matmul(b[:, 256:384], tri, L[:, 256:384], start=False, stop=True,
                              skip_group_check=True).then_inc(s_lw, 1)
                if 0 <= i - 3:
                    h = i - 3
                    pe.wait_ge(s_wm, h + 1)
                    values(h // 2, h, h * 64, sqf[:, (h % 3) * 384:(h % 3) * 384 + 384]).then_inc(s_o, 1)
            product(C_SB_O, 4)
            layer_norm(2)
            mlp(1, 5)
            layer_norm(3)

            for L in range(DEPTH):
                X = 6 + 4 * L
                rms_norm(3 * L)
                for k in range(NT):
                    if k % 2 == 0:
                        pe.wait_ge(x_made, 4 * X + k // 2 + 1)
                    mm = pe.matmul(acc[0:FOX_H, 0, :], wf_sb[:, L, k, :], y[:, k, :], start=(k == 0), stop=(k == NT - 1))
                mm.then_inc(f_log, 1)

                def rotate():
                    pe.wait_ge(f_cum, L + 1)
                    pe.wait_ge(gemm_free, FREE[f"in{L}"] + 4)
                    for t in range(NT):
                        mm = pe.matmul(acc[:, t, :], perm, (qT if t < 4 else kT)[:, 4 + t % 4, :], start=(t % 2 == 0),
                                       stop=True, skip_group_check=True)
                    mm.then_inc(r_rot, 1)

                wide_product(C_IN[L], 14, FREE[f"in{L}"], X, (8, 9, 10, 11), {6: rotate})
                for i in range(FOX_H + 4):
                    if i < FOX_H:
                        h, b = i, bank(i % 2)
                        if h >= 2:
                            pe.wait_ge(f_mx, FOX_H * L + h - 1)
                        q, k, nc_h = qT[head(h), h // 2, :], kT[head(h), h // 2, :], y[0:FOX_H, h, :]
                        pe.matmul(b[:, 0:128], q[:, 0:128], k[:, 0:128], start=True, stop=False, skip_group_check=True)
                        pe.matmul(b[:, 128:384], q[:, 128:256], k, start=False, stop=False, skip_group_check=True)
                        pe.matmul(b[:, 0:128], ones[0:FOX_H, :], nc_h[:, 0:128], start=False, stop=False,
                                  skip_group_check=True)
                        pe.matmul(b[:, 128:384], ones[0:FOX_H, :], nc_h, start=False, stop=True,
                                  skip_group_check=True).then_inc(f_z, 1)
                    if 0 <= i - 2 < FOX_H:
                        h = i - 2
                        b, P = bank(2 + h % 2), sqf[:, (h % 3) * 384:(h % 3) * 384 + 384]
                        pe.wait_ge(f_p, FOX_H * L + h + 1)
                        if h >= 2:
                            pe.wait_ge(f_tc, FOX_H * L + h - 1)
                        pe.transpose(b[:, 0:128], P[:, 0:128], ident)
                        pe.transpose(b[:, 128:256], P[:, 128:256], ident)
                        pe.transpose(b[:, 256:384], P[:, 256:384], ident).then_inc(f_td, 1)
                    if 0 <= i - 4:
                        h = i - 4
                        pe.wait_ge(f_tc, FOX_H * L + h + 1)
                        if h == 0:
                            pe.wait_ge(r_rdy, 2 * L + 2)
                        values(h // 2, h, h * 64,
                               sqf[:, 1152 + (h % 2) * 384:1536 + (h % 2) * 384]).then_inc(f_o, 1)
                for i in range(RET_H + 1):
                    if i < RET_H:
                        h, t = i, 4 + i // 2
                        if h >= 2:
                            pe.wait_ge(r_m, RET_H * L + h - 1)
                        scores(bank(h % 2), kT[head(h), t, :], qT[head(h), t, :]).then_inc(r_s, 1)
                    if i >= 1:
                        h = i - 1
                        pe.wait_ge(r_m, RET_H * L + h + 1)
                        values(4 + h // 2, h, 512 + h * 64, yf[:, (h % 2) * 384:(h % 2) * 384 + 384]).then_inc(r_o, 1)
                for j in range(2):
                    pe.wait_ge(r_c, 2 * L + j + 1)
                    pe.matmul(bank(j), blk, yf[:, 1024 + j * 512:1536 + j * 512], start=True, stop=True).then_inc(r_mean, 1)
                for j in range(2):
                    pe.wait_ge(r_sq, 2 * L + j + 1)
                    pe.matmul(bank(2 + j), blk, sqf[:, j * 512:j * 512 + 512], start=True, stop=True).then_inc(r_var, 1)
                product(C_OUT[L], X + 1)
                rms_norm(3 * L + 1)
                ffn(L, X + 2)
                pe.wait_ge(acc_zero, ZERO[f"ple{L}"] + 1)
                pe.wait_ge(p_lo, L + 1)
                down(C_PROJ[L], 2, last=True)
                rms_norm(3 * L + 2)
                product(C_GATE[L], X + 3)
            rms_norm(6)

        @block.scalar
        def _(act):
            own = Own(act, act_own)
            for dst, src in ((pv[:, :], params), (wa1_sb[:, :, :], wa1), (wa2_sb[:, :], wa2), (wf_sb[:, :, :, :], wf),
                             (fb_sb[:, :], fbias)):
                act.dma_start(dst, src).then_inc(par_in, 16)
            act.dma_start(cst[:, :], consts).then_inc(const_in, 16)

            def x_high(X, src, waits):
                for j in range(4):
                    act.wait_ge(*waits(j))
                    act.copy(pair(xhi, j), src(j)).then_inc(xh_made, 1)

            def from_h(X):
                return lambda j: (h_made, H_OF[X] + j + 1)

            def squares(n, src, made, base):
                for j in range(4):
                    act.wait_ge(made, base + j + 1)
                    act.activation(pair(sq, j), pair(src, j), ACT.Square).then_inc(sq_made, 1)

            def power(r, psum, scale, eps):
                own.sync(act.activation(r, psum, ACT.Ln, bias=eps_col[eps], scale=scale))
                return act.activation(r, r, ACT.Exp, scale=-0.5)

            def inverse_root(n, psum, eps):
                act.wait_ge(var_done, n + 1)
                power(rs1, psum, 1 / D, eps).then_inc(rs_made, 1)

            def ln_part(n):
                squares(n, y, yc_made, 4 * n)
                inverse_root(n, bank(1)[:, 0:S], LN_EPS)

            def rms_part(n):
                squares(4 + n, hT, y_made, 4 * (4 + n))
                inverse_root(4 + n, bank(0)[:, 0:S], RMS_EPS)

            def evacuate(c, n, dest, between):
                for j in range(n):
                    split_hi(act, c + j + AHEAD)
                    act.wait_ge(chunk_used, c + j + 1)
                    d, func, scale = dest(j)
                    if func is None:
                        act.copy(d, two(bank(j % 4))).then_inc(gemm_free, 1)
                    else:
                        act.activation(d, two(bank(j % 4)), func, scale=scale).then_inc(gemm_free, 1)
                    if j in between:
                        between[j]()

            def v_part(j):
                return v[:, :, j * 256:j * 256 + 256]

            def ahead(c, n):
                for j in range(n):
                    split_hi(act, c + j + AHEAD)

            def mlp(n):
                c0, free, h0 = C_MLP[n], FREE[f"mlp{n}"], N_UP * n

                def hidden(c, i, m=0):
                    s = i % 3
                    act.wait_ge(chunk_used, m * RAW + (c + 1))
                    act.activation(pair(qT, s), two(bank(s)), ACT.Relu).then_inc(gemm_free, 1)
                    act.wait_ge(gemm_free, m * 3 + (free + i + 1))
                    act.activation(hhi[:, s, :, :], pair(qT, s), ACT.Square).then_inc(hid_hi, 1)

                split_hi(act, c0 + AHEAD)
                hidden(c0, 0)
                with act.Fori(0, (N_UP - 1) // 3) as m:
                    for i in range(1, 4):
                        cu = c0 + 2 * i - 1
                        split_hi(act, cu + AHEAD, m)
                        hidden(cu, i, m)
                        split_hi(act, cu + 1 + AHEAD, m)
                split_hi(act, c0 + 2 * N_UP - 1 + AHEAD)

            def ffn(L):
                c0, b = C_FFN[L], N_FF * L

                def a_part(c, i, m=0):
                    s = i % 2
                    act.wait_ge(chunk_used, m * RAW + (c + 1))
                    pad = qf[:, s * 516:s * 516 + 516].rearrange("p (t s) -> p t s", t=2)
                    act.copy(pad[:, :, 2:258], two(bank(2 * s))).then_inc(a_copied, 1)

                def gelu(i, m=0):
                    s = i % 2
                    act.wait_ge(conv_made, m * 2 + (b + i + 1))
                    act.activation(kf[:, 1024 + s * 512:1536 + s * 512], kf[:, s * 512:s * 512 + 512],
                                   ACT.Gelu).then_inc(gelu_made, 1)

                def high(i, m=0):
                    s = i % 2
                    act.wait_ge(prod_made, m * 2 + (b + i + 1))
                    act.copy(hhi[:, s, :, :], two(gf[:, s * 512:s * 512 + 512])).then_inc(prod_hi, 1)

                split_hi(act, c0 + AHEAD)
                a_part(c0, 0)
                split_hi(act, c0 + 1 + AHEAD)
                gelu(0)
                high(0)
                with act.Fori(0, (N_FF - 1) // 2) as m:
                    for i in range(1, 3):
                        ca = c0 + 3 * i - 1
                        split_hi(act, ca + AHEAD, m)
                        a_part(ca, i, m)
                        split_hi(act, ca + 1 + AHEAD, m)
                        gelu(i, m)
                        split_hi(act, ca + 2 + AHEAD, m)
                        high(i, m)
                split_hi(act, c0 + 3 * N_FF - 1 + AHEAD)

            def load_exp_ln():
                act.preload_act_table_set("natural_log_exp_and_others")

            load_exp_ln()
            x_high(0, lambda j: pair(hT, j), lambda j: (x_in, 16))
            for c in range(AHEAD):
                split_hi(act, c)

            def a1_copy():
                act.wait_ge(a1_done, 1)
                act.copy(a1_sb, acc[0:16, 0, :]).then_inc(a1_copied, 1)

            def gate_ln():
                act.wait_ge(gate_done, 1)
                act.wait_ge(par_in, 5 * 16)
                for h in range(GLA_H):
                    n = own.mark(act.activation(sqf[:, h * 256:h * 256 + 256], acc[:, 2 + h, :], ACT.Abs,
                                                bias=par("b_a", h)))
                own.need(n)
                own.sync(act.activation(sqf[:, 0:1024], sqf[:, 0:1024], ACT.Exp, scale=-1.0))
                act.activation(sqf[:, 0:1024], sqf[:, 0:1024], ACT.Ln, bias=1.0).then_inc(g_ln, 1)

            def gate_exp():
                act.wait_ge(g_cum, 2)
                act.activation(yf[:, 0:1024], yf[:, 0:1024], ACT.Exp, scale=1 / 16).then_inc(g_exp, 1)
                act.activation(sqf[:, 0:1024], yf[:, 1024:2048], ACT.Exp, scale=1 / 16).then_inc(g_exp, 1)
                act.activation(sqf[:, 1024:2048], yf[:, 1024:2048], ACT.Exp, scale=-1 / 16).then_inc(g_exp, 1)

            def gla_dest(j):
                if j < 4:
                    return pair(qT if j < 2 else kT, j % 2), None, None
                if j < 8:
                    return v_part(j - 4), None, None
                return pair(gT, j - 8), ACT.Silu, 1.0

            evacuate(C_GLA_IN, 12, gla_dest, {0: a1_copy, 1: gate_ln, 4: gate_exp})
            load_exp_ln()
            act.wait_ge(g_ktd, 1)
            own.mark(act.copy(yf[:, 0:512], ring[:, 0, :]))
            act.copy(yf[:, 512:1024], ring[:, 1, :]).then_inc(g_ktc, 1)
            for t in range(2):
                act.wait_ge(g_attd, t + 1)
                act.copy(sqf[:, 1024 + t * 512:1536 + t * 512], ring[:, 2 + t, :]).then_inc(g_attc, 1)
            for h in range(GLA_H):
                act.wait_ge(g_od, h + 1 if h < 2 else GLA_H)
                act.activation(pair(sq, h), pair(acc, h), ACT.Square).then_inc(g_sq, 1)
            for j in range(2):
                act.wait_ge(g_var, j + 1)
                power(rs[:, j * 512:j * 512 + 512], bank(2 + j), 1 / 256, RMS_EPS).then_inc(g_rs, 1)
            x_high(1, lambda j: pair(y, j), from_h(1))
            ahead(C_GLA_O, 4)
            ln_part(0)
            x_high(2, lambda j: pair(hT, j), from_h(2))
            act.dma_start(misc[:, 0:2048], decay).then_inc(dec_in, 16)
            mlp(0)
            ln_part(1)
            x_high(3, lambda j: pair(hT, j), from_h(3))

            def sb_dest(j):
                if j < 4:
                    return pair(kT, j), None, None
                if j < 8:
                    return v_part(j - 4), None, None
                return pair(qT, j - 8), ACT.Copy, 0.125

            evacuate(C_SB_IN, 12, sb_dest, {})
            for i in range(SB_H + 1):
                if i < SB_H:
                    h = i
                    a, b = gf[:, (h % 2) * 384:(h % 2) * 384 + 384], bank(h % 4)[:, 0:384]
                    act.wait_ge(s_z, h + 1)
                    if h >= 2:
                        act.wait_ge(s_sp, h - 1)
                    own.sync(act.activation(a, b, ACT.Abs))
                    own.sync(act.activation(a, a, ACT.Exp, scale=-1.0))
                    act.activation(a, a, ACT.Ln, bias=1.0).then_inc(s_ln, 1)
                if i >= 1:
                    h = i - 1
                    act.wait_ge(s_lw, h + 1)
                    if h >= 3:
                        act.wait_ge(s_o, h - 2)
                    act.activation(sqf[:, (h % 3) * 384:(h % 3) * 384 + 384], bank(h % 4)[:, 0:384],
                                   ACT.Exp).then_inc(s_w, 1)
            x_high(4, lambda j: pair(acc, j), lambda j: (s_o, 4 * j + 4))
            ahead(C_SB_O, 4)
            ln_part(2)
            x_high(5, lambda j: pair(hT, j), from_h(5))
            mlp(1)
            ln_part(3)

            for L in range(DEPTH):
                X = 6 + 4 * L
                if L:
                    act.wait_ge(p_lo, L)
                act.dma_start(two(gf[:, 1024:1536]), pT[L]).then_inc(p_in, 16)
                rms_part(3 * L)
                x_high(X, lambda j: pair(y, j), from_h(X))

                def forget_ln():
                    act.wait_ge(f_log, L + 1)
                    own.sync(act.activation(cum[:, 0, :], acc[0:FOX_H, 0, :], ACT.Abs, bias=fb_sb[:, L:L + 1]))
                    own.sync(act.activation(cum[:, 0, :], cum[:, 0, :], ACT.Exp, scale=-1.0))
                    act.activation(cum[:, 0, :], cum[:, 0, :], ACT.Ln, bias=1.0).then_inc(f_ln, 1)

                def p_high():
                    act.wait_ge(p_in, 16 * (L + 1))
                    act.copy(hhi[:, 2, :, :], two(gf[:, 1024:1536])).then_inc(p_hi, 1)

                def in_dest(j):
                    if j < 2:
                        return pair(qT, 2 + j), None, None
                    if j < 4:
                        return pair(kT, j), ACT.Copy, 0.125
                    if j < 6:
                        return pair(qT, j - 4), ACT.Copy, 0.125
                    if j < 8:
                        return pair(kT, j - 6), None, None
                    if j < 12:
                        return v_part(j - 8), None, None
                    return pair(gT, j - 12), ACT.Silu, 1.0

                forget_ln()
                evacuate(C_IN[L], 14, in_dest, {9: p_high})
                load_exp_ln()
                for i in range(FOX_H + 2):
                    if i < FOX_H:
                        h = i
                        P = sqf[:, (h % 3) * 384:(h % 3) * 384 + 384]
                        act.wait_ge(f_mx, FOX_H * L + h + 1)
                        act.activation(P[:, 0:128], P[:, 0:128], ACT.Exp, bias=stat[:, h % 4, 2:3],
                                       accum_out=stat[:, h % 4, 4:5])
                        act.activation(P[:, 128:384], P[:, 128:384], ACT.Exp, bias=stat[:, h % 4, 3:4],
                                       accum_out=stat[:, h % 4, 5:6]).then_inc(f_e, 1)
                    if i >= 2:
                        h = i - 2
                        act.wait_ge(f_td, FOX_H * L + h + 1)
                        if h >= 2:
                            act.wait_ge(f_o, FOX_H * L + h - 1)
                        act.copy(sqf[:, 1152 + (h % 2) * 384:1536 + (h % 2) * 384], bank(2 + h % 2)[:, 0:384]).then_inc(f_tc, 1)
                for j in range(2):
                    act.wait_ge(f_o, FOX_H * L + 4 * j + 4)
                    act.copy(pair(xhi, j), pair(acc, j)).then_inc(xh_made, 1)
                for j in range(2):
                    act.wait_ge(r_o, RET_H * L + 4 * j + 4)
                    act.copy(pair(y, 2 + j), pair(acc, 2 + j)).then_inc(r_c, 1)
                for j in range(2):
                    act.wait_ge(r_yc, 2 * L + j + 1)
                    act.activation(pair(sq, j), pair(y, 2 + j), ACT.Square).then_inc(r_sq, 1)
                for j in range(2):
                    act.wait_ge(r_var, 2 * L + j + 1)
                    power(rs[:, j * 512:j * 512 + 512], bank(2 + j), 1 / 64, GN_EPS).then_inc(r_rs, 1)
                for j in range(2):
                    act.wait_ge(h_made, H_OF[X + 1] + j + 1)
                    act.copy(pair(xhi, 2 + j), pair(y, 2 + j)).then_inc(xh_made, 1)
                ahead(C_OUT[L], 4)
                rms_part(3 * L + 1)
                x_high(X + 2, lambda j: pair(y, j), from_h(X + 2))
                ffn(L)
                load_exp_ln()
                ahead(C_PROJ[L], 1)
                rms_part(3 * L + 2)
                x_high(X + 3, lambda j: pair(y, j), from_h(X + 3))
                for j in range(4):
                    split_hi(act, C_GATE[L] + j + AHEAD)
                    act.wait_ge(chunk_used, C_GATE[L] + j + 1)
                    act.activation(kf[:, j * 512:j * 512 + 512], bank(j), ACT.Sigmoid).then_inc(sig_made, 1)
                load_exp_ln()
            rms_part(6)

        @block.vector
        def _(dve):
            own = Own(dve, dve_own)

            def x_low(X, src, js=range(4)):
                for j in js:
                    dve.wait_ge(xh_made, 4 * X + j + 1)
                    dve.tensor_tensor(pair(xlo, j), src(j), pair(xhi, j).bitcast(f32), ALU.subtract).then_inc(x_made, 1)

            def ahead(c, n):
                for j in range(n):
                    split_lo(dve, c + j + AHEAD)

            def zero_acc(s, n):
                dve.wait_ge(s, n)
                dve.memset(acc[:, :, :], 0.0).then_inc(acc_zero, 1)

            def residual(j, psum):
                dve.scalar_tensor_tensor(pair(y, j), pair(hT, j), ALPHA, psum, ALU.mult, ALU.add).then_inc(y_made, 1)

            def layer_norm(n, X):
                dve.wait_ge(y_made, 4 * n + 4)
                dve.wait_ge(mean_done, n + 1)
                for j in range(4):
                    dve.scalar_tensor_tensor(pair(y, j), wide(bank(0)[:, 0:S], 2), -1 / D, pair(y, j), ALU.mult,
                                             ALU.add).then_inc(yc_made, 1)
                dve.wait_ge(yc_made, 4 * n + 4)
                dve.wait_ge(rs_made, n + 1)
                marks = [own.mark(dve.tensor_tensor(pair(y, 0), pair(y, 0), wide(rs1, 2), ALU.mult))]
                for j in range(4):
                    if j < 3:
                        marks.append(own.mark(dve.tensor_tensor(pair(y, j + 1), pair(y, j + 1), wide(rs1, 2), ALU.mult)))
                    own.need(marks[j])
                    for t in (2 * j, 2 * j + 1):
                        ins = dve.tensor_scalar(hT[:, t, :], y[:, t, :], par("ln_g", 8 * n + t), par("ln_b", 8 * n + t),
                                                ALU.mult, ALU.add)
                    ins.then_inc(y_made if X is None else h_made, 1)
                    if X is not None and j:
                        x_low(X, lambda i: pair(hT, i), [j - 1])
                if X is not None:
                    x_low(X, lambda i: pair(hT, i), [3])

            def rms_norm(n, X, w, i0):
                dve.wait_ge(rs_made, 4 + n + 1)
                for j in range(4):
                    for t in (2 * j, 2 * j + 1):
                        ins = dve.scalar_tensor_tensor(y[:, t, :], hT[:, t, :], par(w, i0 + t), rs1, ALU.mult, ALU.mult)
                    ins.then_inc(out_made if X is None else h_made, 1)
                    if X is not None and j:
                        x_low(X, lambda i: pair(y, i), [j - 1])
                if X is not None:
                    x_low(X, lambda i: pair(y, i), [3])

            def mlp(n):
                c0, free, h0 = C_MLP[n], FREE[f"mlp{n}"], N_UP * n

                def hidden(i, m=0):
                    s = i % 3
                    dve.wait_ge(gemm_free, m * 3 + (free + i + 1))
                    dve.tensor_tensor(pair(kT, s), pair(qT, s), pair(qT, s), ALU.mult).then_inc(hid_sq, 1)
                    dve.wait_ge(hid_sq, m * 3 + (h0 + i + 1))
                    dve.wait_ge(hid_hi, m * 3 + (h0 + i + 1))
                    dve.tensor_tensor(hlo[:, s, :, :], pair(kT, s), hhi[:, s, :, :].bitcast(f32),
                                      ALU.subtract).then_inc(hid_lo, 1)

                split_lo(dve, c0 + AHEAD)
                hidden(0)
                with dve.Fori(0, (N_UP - 1) // 3) as m:
                    for i in range(1, 4):
                        cu = c0 + 2 * i - 1
                        split_lo(dve, cu + AHEAD, m)
                        hidden(i, m)
                        split_lo(dve, cu + 1 + AHEAD, m)
                split_lo(dve, c0 + 2 * N_UP - 1 + AHEAD)

            def acc_ready(inst, c, j):
                if j < 3:
                    dve.wait_ge(acc_done, 3 * inst + j + 1)
                else:
                    dve.wait_ge(chunk_used, c + 1)

            def ffn(L):
                c0, b = C_FFN[L], N_FF * L
                pads = qf[:, 0:1032].rearrange("p (a s) -> p a s", a=4)[:, :, 0:2]
                own.sync(dve.memset(pads, 0.0))

                def conv(i, m=0):
                    s = i % 2
                    dve.wait_ge(a_copied, m * 2 + (b + i + 1))
                    for step in range(3):
                        for t in range(2):
                            o = kf[:, s * 512 + t * 256:s * 512 + t * 256 + 256]
                            at = s * 516 + t * 258 + 2 - step
                            tile = m * 4 + (2 * i + t)
                            w = pv[:, bass.ds(tile + (PV["conv_w"] + (3 * L + 2 - step) * FT), 1)]
                            if step == 0:
                                bias = pv[:, bass.ds(tile + (PV["conv_b"] + L * FT), 1)]
                                ins = dve.tensor_scalar(o, qf[:, at:at + 256], w, bias, ALU.mult, ALU.add)
                            else:
                                ins = dve.scalar_tensor_tensor(o, qf[:, at:at + 256], w, o, ALU.mult, ALU.add)
                        ins.then_inc(conv_step if step < 2 else conv_made, 1)
                        if step < 2:
                            dve.wait_ge(conv_step, m * 4 + (2 * (b + i) + step + 1))

                def gated(c, i, m=0):
                    s = i % 2
                    dve.wait_ge(gelu_made, m * 2 + (b + i + 1))
                    dve.wait_ge(chunk_used, m * RAW + (c + 1))
                    dve.tensor_tensor(gf[:, s * 512:s * 512 + 512], kf[:, 1024 + s * 512:1536 + s * 512],
                                      bank(2 * s + 1), ALU.mult).then_inc(prod_made, 1)

                def low(i, m=0):
                    s = i % 2
                    dve.wait_ge(prod_made, m * 2 + (b + i + 1))
                    dve.wait_ge(prod_hi, m * 2 + (b + i + 1))
                    dve.tensor_tensor(hlo[:, s, :, :], two(gf[:, s * 512:s * 512 + 512]), hhi[:, s, :, :].bitcast(f32),
                                      ALU.subtract).then_inc(prod_lo, 1)

                split_lo(dve, c0 + AHEAD)
                conv(0)
                split_lo(dve, c0 + 1 + AHEAD)
                gated(c0 + 1, 0)
                low(0)
                with dve.Fori(0, (N_FF - 1) // 2) as m:
                    for i in range(1, 3):
                        ca = c0 + 3 * i - 1
                        split_lo(dve, ca + AHEAD, m)
                        conv(i, m)
                        split_lo(dve, ca + 1 + AHEAD, m)
                        gated(ca + 1, i, m)
                        split_lo(dve, ca + 2 + AHEAD, m)
                        low(i, m)
                split_lo(dve, c0 + 3 * N_FF - 1 + AHEAD)

            x_low(0, lambda j: pair(hT, j))
            for c in range(AHEAD + 2):
                split_lo(dve, c)
            b4 = yf[:, 1024:2048]
            dve.wait_ge(g_ln, 1)
            dve.wait_ge(par_in, 5 * 16)
            dve.wait_ge(const_in, 16)
            for h in range(GLA_H):
                n = own.mark(dve.tensor_scalar(yf[:, h * 256:h * 256 + 256], acc[:, 2 + h, :], par("b_a", h), 0.0,
                                               ALU.add, ALU.min))
            own.need(n)
            own.sync(dve.tensor_tensor(yf[:, 0:1024], yf[:, 0:1024], sqf[:, 0:1024], ALU.subtract))
            split_lo(dve, 2 + AHEAD)
            for h in range(GLA_H):
                s = slice(h * 256, h * 256 + 256)
                last = dve.tensor_tensor_scan(b4[:, s], scanm, yf[:, s], 0.0, ALU.mult, ALU.add)
            last.then_inc(g_cum, 1)
            dve.wait_ge(g_cum, 1)
            b3 = b4.rearrange("p (a c) -> p a c", c=64)
            dve.tensor_tensor(yf[:, 0:1024].rearrange("p (a c) -> p a c", c=64), b3[:, :, 63:64].to_broadcast([128, 16, 64]),
                              b3, ALU.subtract).then_inc(g_cum, 1)
            for c in (3, 4, 5):
                split_lo(dve, c + AHEAD)
            dve.wait_ge(gemm_free, 4)
            dve.wait_ge(g_exp, 1)
            for h in range(GLA_H):
                dve.tensor_tensor(kT[:, 4 + h, :], kT[:, h, :], y[:, h, :], ALU.mult).then_inc(g_kend, 1)
            split_lo(dve, 6 + AHEAD)
            dve.wait_ge(g_exp, 3)
            dve.wait_ge(g_kend, GLA_H)
            own.mark(dve.scalar_tensor_tensor(qf[:, 0:1024], qf[:, 0:1024], GLA_SCALE, sqf[:, 0:1024], ALU.mult, ALU.mult))
            dve.tensor_tensor(kf[:, 0:1024], kf[:, 0:1024], sqf[:, 1024:2048], ALU.mult).then_inc(g_dec, 1)
            for c in range(7, 12):
                split_lo(dve, c + AHEAD)
            for n in range(3):
                dve.wait_ge(g_ud, n + 1)
                for h in range(GLA_H):
                    u = ring[:, h // 2, (h % 2) * 256:(h % 2) * 256 + 256]
                    at = n * 1024 + h * 256
                    if n == 0:
                        ins = dve.tensor_copy(misc[:, at:at + 256], u)
                    else:
                        d = sqf[:, h * 256 + n * 64 + 63:h * 256 + n * 64 + 64]
                        ins = dve.scalar_tensor_tensor(misc[:, at:at + 256], misc[:, at - 1024:at - 768], d, u,
                                                       ALU.mult, ALU.add)
                ins.then_inc(g_st, 1)
                dve.wait_ge(g_st, n + 1)
            for j in range(2):
                dve.wait_ge(g_rs, j + 1)
                for h in (2 * j, 2 * j + 1):
                    own.sync(dve.tensor_tensor(pair(y, h), pair(acc, h), wide(rs[:, h * 256:h * 256 + 256], 2), ALU.mult))
                    for e in range(2):
                        t = 2 * h + e
                        ins = dve.scalar_tensor_tensor(y[:, t, :], y[:, t, :], par("gla_g", e), gT[:, t, :],
                                                       ALU.mult, ALU.mult)
                    ins.then_inc(h_made, 1)
                    x_low(1, lambda i: pair(y, i), [h])
            zero_acc(x_made, 8)

            def after_product(c, n):
                for j in range(4):
                    split_lo(dve, c + j + AHEAD)
                    dve.wait_ge(chunk_used, c + j + 1)
                    residual(j, two(bank(j)))

            def after_mlp(n):
                for j in range(4):
                    acc_ready(ZERO[f"mlp{n}"], C_MLP[n] + 2 * N_UP - 1, j)
                    residual(j, pair(acc, j))

            dve.wait_ge(x_made, 8)
            after_product(C_GLA_O, 0)
            layer_norm(0, 2)
            mlp(0)
            after_mlp(0)
            layer_norm(1, 3)

            ahead(C_SB_IN, 12)
            for h in range(SB_H):
                s = (h % 2) * 384
                dve.wait_ge(s_ln, h + 1)
                if h >= 2:
                    dve.wait_ge(s_lw, h - 1)
                dve.scalar_tensor_tensor(yf[:, s:s + 384], bank(h % 4)[:, 0:384], 0.0, gf[:, s:s + 384], ALU.max,
                                         ALU.add).then_inc(s_sp, 1)
            x_low(4, lambda j: pair(acc, j))
            zero_acc(x_made, 20)
            after_product(C_SB_O, 2)
            layer_norm(2, 5)
            mlp(1)
            after_mlp(1)
            layer_norm(3, None)

            def add_to_h(j, psum):
                dve.tensor_tensor(pair(hT, j), pair(hT, j), psum, ALU.add).then_inc(y_made, 1)

            for L in range(DEPTH):
                X = 6 + 4 * L
                rms_norm(3 * L, X, "attn_w", 8 * L)
                split_lo(dve, C_IN[L] + AHEAD)
                dve.wait_ge(f_ln, L + 1)
                own.sync(dve.tensor_scalar(cum[:, 1, :], acc[0:FOX_H, 0, :], fb_sb[:, L:L + 1], 0.0, ALU.add, ALU.min))
                own.sync(dve.tensor_tensor(cum[:, 1, :], cum[:, 1, :], cum[:, 0, :], ALU.subtract))
                own.sync(dve.tensor_tensor_scan(cum[:, 2, :], cst[0:FOX_H, CONST["ones"]:CONST["ones"] + S], cum[:, 1, :],
                                                0.0, ALU.mult, ALU.add))
                dve.scalar_tensor_tensor(y[0:FOX_H, :, :], wide(cum[:, 2, :], FOX_H), -1.0,
                                         ident[0:FOX_H, 0:FOX_H].unsqueeze(2).to_broadcast([FOX_H, FOX_H, S]),
                                         ALU.mult, ALU.mult).then_inc(f_cum, 1)
                for j in range(1, 7):
                    split_lo(dve, C_IN[L] + j + AHEAD)
                dve.wait_ge(r_rot, L + 1)
                for n, t in enumerate((qT, kT)):
                    own.mark(dve.tensor_tensor(sq[:, 0:4, :], t[:, 4:8, :], wide(cosT, 4), ALU.mult))
                    own.sync(dve.tensor_tensor(sq[:, 4:8, :], acc[:, 4 * n:4 * n + 4, :], wide(sinT, 4), ALU.mult))
                    dve.tensor_tensor(t[:, 4:8, :], sq[:, 0:4, :], sq[:, 4:8, :], ALU.add).then_inc(r_rdy, 1)
                    dve.wait_ge(r_rdy, 2 * L + n + 1)
                    split_lo(dve, C_IN[L] + 7 + n + AHEAD)
                dve.wait_ge(p_hi, L + 1)
                dve.tensor_tensor(hlo[:, 2, :, :], two(gf[:, 1024:1536]), hhi[:, 2, :, :].bitcast(f32),
                                  ALU.subtract).then_inc(p_lo, 1)
                for j in range(9, 14):
                    split_lo(dve, C_IN[L] + j + AHEAD)
                for i in range(FOX_H + 1):
                    if i < FOX_H:
                        h, st = i, stat[:, i % 4, :]
                        b, P = bank(h % 2), sqf[:, (h % 3) * 384:(h % 3) * 384 + 384]
                        dve.wait_ge(f_z, FOX_H * L + h + 1)
                        if h >= 3:
                            dve.wait_ge(f_td, FOX_H * L + h - 2)
                        own.mark(dve.tensor_tensor_reduce(P[:, 0:128], b[:, 0:128], maskadd[:, 0:128], 1.0, -3.0e38,
                                                          ALU.add, ALU.max, st[:, 0:1]))
                        own.sync(dve.tensor_tensor_reduce(P[:, 128:384], b[:, 128:384], maskadd[:, 128:384], 1.0, -3.0e38,
                                                          ALU.add, ALU.max, st[:, 1:2]))
                        dve.tensor_scalar(st[:, 2:4], st[:, 0:2], -1.0, None, ALU.mult).then_inc(f_mx, 1)
                    if i >= 1:
                        h, st = i - 1, stat[:, (i - 1) % 4, :]
                        P = sqf[:, (h % 3) * 384:(h % 3) * 384 + 384]
                        dve.wait_ge(f_e, FOX_H * L + h + 1)
                        own.sync(dve.reciprocal(st[:, 6:8], st[:, 4:6]))
                        dve.tensor_scalar(P[:, 0:128], P[:, 0:128], st[:, 6:7], None, ALU.mult)
                        dve.tensor_scalar(P[:, 128:384], P[:, 128:384], st[:, 7:8], None, ALU.mult).then_inc(f_p, 1)
                dve.wait_ge(dec_in, 16)
                x_low(X + 1, lambda j: pair(acc, j), range(2))
                for h in range(RET_H):
                    s = (h % 2) * 384
                    dve.wait_ge(r_s, RET_H * L + h + 1)
                    if h >= 2:
                        dve.wait_ge(r_o, RET_H * L + h - 1)
                    dve.tensor_tensor(yf[:, s:s + 256], bank(h % 2)[:, 0:256], dec[:, h, :], ALU.mult)
                    dve.tensor_tensor(yf[:, s + 256:s + 384], bank(h % 2)[:, 256:384], dec[:, h, 0:128],
                                      ALU.mult).then_inc(r_m, 1)
                for j in range(2):
                    dve.wait_ge(r_mean, 2 * L + j + 1)
                    dve.scalar_tensor_tensor(pair(y, 2 + j), two(bank(j)), -1 / 64, pair(y, 2 + j), ALU.mult,
                                             ALU.add).then_inc(r_yc, 1)
                dve.wait_ge(r_yc, 2 * L + 2)
                for j in range(2):
                    r, t = rs[:, j * 512:j * 512 + 512], yf[:, 1024 + j * 512:1536 + j * 512]
                    dve.wait_ge(r_rs, 2 * L + j + 1)
                    own.sync(dve.tensor_tensor(t, t, r, ALU.mult))
                    dve.tensor_tensor(t, t, gf[:, j * 512:j * 512 + 512], ALU.mult).then_inc(h_made, 1)
                    x_low(X + 1, lambda i: pair(y, i), [2 + j])
                zero_acc(x_made, 4 * (X + 1) + 4)
                for j in range(4):
                    split_lo(dve, C_OUT[L] + j + AHEAD)
                    dve.wait_ge(chunk_used, C_OUT[L] + j + 1)
                    add_to_h(j, two(bank(j)))
                rms_norm(3 * L + 1, X + 2, "ffn_w", 8 * L)
                ffn(L)
                for j in range(4):
                    acc_ready(ZERO[f"ffn{L}"], C_FFN[L] + 3 * N_FF - 1, j)
                    add_to_h(j, pair(acc, j))
                zero_acc(y_made, 4 * (6 + 3 * L) + 4)
                split_lo(dve, C_PROJ[L] + AHEAD)
                rms_norm(3 * L + 2, X + 3, "ple_w", 8 * L)
                for j in range(4):
                    split_lo(dve, C_GATE[L] + j + AHEAD)
                    if j == 0:
                        dve.wait_ge(chunk_used, C_PROJ[L] + 1)
                    dve.wait_ge(sig_made, 4 * L + j + 1)
                    own.sync(dve.tensor_tensor(pair(kT, j), pair(kT, j), pair(acc, j), ALU.mult))
                    add_to_h(j, pair(kT, j))
            rms_norm(6, None, "fin_w", 0)

        @block.gpsimd
        def _(pool):
            own = Own(pool, pool_own)
            for t in range(2):
                pool.wait_ge(g_attc, t + 1)
                a = sqf[:, 1024 + t * 512:1536 + t * 512]
                own.sync(pool.affine_select(out=a, in_=a, compare_op=ALU.is_ge, fill=0.0, base=0,
                                            pattern=[[0, 4], [1, 128]], channel_multiplier=-1))
                b = a.rearrange("p (h c) -> p h c", h=4)[:, :, 64:128]
                pool.affine_select(out=b, in_=b, compare_op=ALU.is_ge, fill=0.0, base=-64,
                                   pattern=[[0, 4], [0, 64]], channel_multiplier=1).then_inc(g_attm, 1)

            def strict(buf):
                d = buf.rearrange("p (b s) -> p b s", b=3)[:, 0:3:2, :]
                return pool.affine_select(out=d, in_=d, compare_op=ALU.is_gt, fill=0.0, base=0,
                                          pattern=[[0, 2], [1, 128]], channel_multiplier=-1)

            for i in range(SB_H + 1):
                if i < SB_H:
                    pool.wait_ge(s_sp, i + 1)
                    strict(yf[:, (i % 2) * 384:(i % 2) * 384 + 384]).then_inc(s_L, 1)
                if i >= 1:
                    h = i - 1
                    pool.wait_ge(s_w, h + 1)
                    strict(sqf[:, (h % 3) * 384:(h % 3) * 384 + 384]).then_inc(s_wm, 1)


def _tiles(a, n=None):
    return np.ascontiguousarray(a.reshape(-1, 128, a.shape[-1]).transpose(1, 0, 2))


def _cols(w):
    n = w.shape[1] // 256
    return w.reshape(NT, 128, n, 256).transpose(2, 1, 0, 3).reshape(n, 128, CW)


def _rows(w):
    n = w.shape[0] // 256
    return w.reshape(n, 2, 128, D).transpose(0, 2, 1, 3).reshape(n, 128, CW)


def _stream(i):
    w = i["gla_w_in"][0]
    parts = [_cols(w[:, 0:3072]), _cols(i["gla_w_o"][0])]

    def mlp(n):
        up, down = _cols(i["mlp_w_up"][n]), _rows(i["mlp_w_down"][n])
        parts.append(up[0:1])
        for s in range(1, N_UP):
            parts.extend([up[s:s + 1], down[s - 1:s]])
        parts.append(down[N_UP - 1:])

    mlp(0)
    parts.extend([_cols(i["kv_w"]), _cols(i["sb_w_q"][0]), _cols(i["sb_w_o"][0])])
    mlp(1)
    for n in range(DEPTH):
        w = i["w_in_2"][n]
        fq, fk, fv, rq, rk, rv, rg = (w[:, a:a + 512] for a in (0, 512, 1024, 1544, 2056, 2568, 3080))
        parts.extend(_cols(p) for p in (rq, rk, fq, fk, fv, rv, rg))
        parts.append(_cols(i["w_out_2"][n]))
        up, down = i["w_up_2"][n], _rows(i["w_down_2"][n])
        a, g = _cols(up[:, :FF2]), _cols(up[:, FF2:])
        parts.extend([a[0:1], g[0:1]])
        for s in range(1, N_FF):
            parts.extend([a[s:s + 1], g[s:s + 1], down[s - 1:s]])
        parts.append(down[N_FF - 1:])
        parts.extend([_rows(i["w_ple_proj_2"][n]), _cols(i["w_ple_gate_2"][n])])
    return np.concatenate(parts, axis=0)


def _params(i):
    def c(a):
        return np.asarray(a).reshape(-1, 128).T

    return np.ascontiguousarray(np.concatenate([
        c(i["ln_g"]), c(i["ln_b"]), c(i["gla_b_a"]), c(i["gla_norm_g"]), c(i["attn_norm_w_2"]), c(i["ffn_norm_w_2"]),
        c(i["ple_norm_w_2"]), c(i["final_norm_w_2"]), c(i["conv_w_2"]), c(i["conv_b_2"])], axis=1))


def _constants():
    p, f = np.arange(128)[:, None], np.arange(128)[None, :]
    causal = np.where(f > p, -3.0e38, 0.0)
    d = p % 64
    source = np.where(d < 32, p + 32, p - 32)
    perm = np.where(f == source, np.where(d < 32, -1.0, 1.0), 0.0).T
    inv = (np.float32(10000.0) ** (-np.arange(0, 64, 2, dtype=np.float32) / np.float32(64))).astype(np.float32)
    ang = (np.arange(S, dtype=np.float32)[None, :] * inv[np.arange(128) % 32][:, None]).astype(np.float32)
    scan = np.where(np.arange(S) % 64 == 0, 0.0, 1.0)[None, :] * np.ones((128, 1))
    parts = dict(ident=p == f, ones=np.ones((128, 256)), blk=p // 64 == f // 64, tri=-(p >= f).astype(float),
                 neg=-np.ones((128, 128)), perm=perm, scan=scan,
                 mask=np.concatenate([causal, np.zeros((128, 128)), causal], axis=1), cos=np.cos(ang), sin=np.sin(ang),
                 eps=np.tile([LN_EPS, RMS_EPS], (128, 1)))
    assert list(parts) == list(CONST)
    return np.concatenate([np.asarray(a, np.float32) for a in parts.values()], axis=1)


def _decays():
    gamma = 1.0 - np.exp2(-5.0 - np.arange(RET_H))
    i, j = np.arange(S)[None, None, :], np.arange(128)[:, None, None]
    lg = np.log1p(-np.exp2(-5.0 - np.arange(RET_H)))[None, :, None]
    t = np.where(i >= j, np.exp(lg * np.maximum(i - j, 0)), 0.0)
    return t.reshape(128, RET_H * S).astype(np.float32)


def kernel(**inputs):
    import concourse.bacc as bacc
    from concourse.bass_utils import run_bass_kernel_spmd

    i = {k: np.asarray(a) for k, a in inputs.items()}
    arrays = dict(
        xT=_tiles(i["x"][0].T),
        wstream=_stream(i),
        wa1=_tiles(i["gla_w_in"][0][:, 3072:3088]),
        wa2=np.ascontiguousarray(i["gla_w_a2"][0]),
        wf=np.ascontiguousarray(np.stack([_tiles(i["w_in_2"][n][:, 1536:1544]) for n in range(DEPTH)], axis=1)),
        fbias=np.ascontiguousarray(i["forget_bias_2"].T),
        pT=np.stack([_tiles(i["p_2"][n, 0].T) for n in range(DEPTH)]),
        params=_params(i),
        consts=_constants(),
        decay=_decays(),
    )
    nc = bacc.Bacc("TRN2", target_bir_lowering=False, num_devices=1)
    aps = {n: nc.dram_tensor(n, a.shape, mybir.dt.from_np(a.dtype), kind="ExternalInput").ap() for n, a in arrays.items()}
    aps["out"] = nc.dram_tensor("out", (128, NT, S), mybir.dt.float32, kind="ExternalOutput").ap()
    build_program(nc, **aps)
    got = run_bass_kernel_spmd(nc, [arrays], core_ids=[0]).results[0]["out"]
    return np.ascontiguousarray(got.transpose(2, 1, 0).reshape(1, S, D))
```

```python
import concourse.bass as bass
from concourse import mybir
from contextlib import ExitStack
import numpy as np

S = 256
D = 1024
NT = D // 128
FF = 4096
FF2 = 2816
DEPTH = 2
CW = 2048
N_UP = FF // 256
N_FF = FF2 // 256
FT = FF2 // 128
ALPHA = (2.0 * DEPTH) ** 0.25
LN_EPS, RMS_EPS = 1e-5, 1e-6
GN_EPS = LN_EPS
GLA_H, SB_H, FOX_H, RET_H = 4, 16, 8, 8
GLA_SCALE = 128 ** -0.5

C_GLA_IN = 0
C_GLA_O = C_GLA_IN + 12
C_MLP = [C_GLA_O + 4, 0]
C_SB_IN = C_MLP[0] + 2 * N_UP
C_SB_O = C_SB_IN + 12
C_MLP[1] = C_SB_O + 4
C_B2 = C_MLP[1] + 2 * N_UP
PER_B2 = 14 + 4 + 3 * N_FF + 1 + 4
C_IN = [C_B2 + PER_B2 * n for n in range(DEPTH)]
C_OUT = [c + 14 for c in C_IN]
C_FFN = [c + 18 for c in C_IN]
C_PROJ = [c + 3 * N_FF for c in C_FFN]
C_GATE = [c + 1 for c in C_PROJ]
N_CHUNKS = C_B2 + PER_B2 * DEPTH

RAW, SPLIT = 6, 3
AHEAD = 2

FREE = dict(gla_in=0, mlp0=12, sb_in=12 + N_UP, mlp1=24 + N_UP, in0=24 + 2 * N_UP, in1=38 + 2 * N_UP)
ZERO = dict(mlp0=0, mlp1=1, ffn0=2, ffn1=3)
H_OF = {1: 0, 2: 4, 3: 8, 5: 12, 7: 16, 11: 18}

PV = dict(ln_g=0, ln_b=32, b_a=64, gla_g=68, attn_w=70, ffn_w=86, ple_w=102, fin_w=118, conv_w=126,
          conv_b=126 + 6 * FT)
NPV = 126 + 8 * FT
CONST = dict(ident=0, ones=128, blk=384, tri=512, neg=640, perm=768, scan=896, mask=1152, cos=1536, sin=1792, eps=2048)
NCONST = 2050


def build_program(nc, xT, wstream, wa1, wa2, wf, fbias, pT, params, consts, decay, out):
    f32, f32r = mybir.dt.float32, mybir.dt.float32r
    ALU, ACT = mybir.AluOpType, mybir.ActivationFunctionType
    ctx = ExitStack()
    with ctx:
        def sb(name, shape, dt=f32):
            return ctx.enter_context(nc.sbuf_tensor(name, shape, dt))

        def sem(name):
            return ctx.enter_context(nc.semaphore(name))

        raw = sb("raw", [128, RAW, CW])
        whi = sb("whi", [128, SPLIT, CW], f32r)
        wlo = sb("wlo", [128, SPLIT, CW], f32r)
        hT = sb("hT", [128, NT, S])
        xhi = sb("xhi", [128, NT, S], f32r)
        xlo = sb("xlo", [128, NT, S], f32r)
        y = sb("y", [128, NT, S])
        sq = sb("sq", [128, NT, S])
        qT = sb("qT", [128, NT, S])
        kT = sb("kT", [128, NT, S])
        v = sb("v", [128, 2, D])
        gT = sb("gT", [128, NT, S])
        hhi = sb("hhi", [128, 3, 2, S], f32r)
        hlo = sb("hlo", [128, 3, 2, S], f32r)
        misc = sb("misc", [128, 3072])
        cst = sb("cst", [128, NCONST])
        pv = sb("pv", [128, NPV])
        wa1_sb = sb("wa1_sb", [128, NT, 16])
        wa2_sb = sb("wa2_sb", [16, 512])
        wf_sb = sb("wf_sb", [128, DEPTH, NT, FOX_H])
        fb_sb = sb("fb_sb", [FOX_H, DEPTH])
        low_rank = sb("low_rank", [16, 3, S])
        a1_sb, cum = low_rank[:, 0, :], low_rank[0:FOX_H, :, :]
        r_col = sb("r_col", [128, 2])
        stat = sb("stat", [128, 4, 8])

        def const(name, n):
            return cst[:, CONST[name]:CONST[name] + n]

        def par(name, i):
            return pv[:, PV[name] + i:PV[name] + i + 1]

        ident, blk, tri, neg, perm = (const(n, 128) for n in ("ident", "blk", "tri", "neg", "perm"))
        ones = const("ones", 128)
        cosT, sinT, scanm, maskadd = const("cos", S), const("sin", S), const("scan", S), const("mask", 384)

        eps_col = {LN_EPS: const("eps", 1), RMS_EPS: const("eps", 2)[:, 1:2]}

        def flat(t):
            return t[:, :, :].rearrange("p t s -> p (t s)")

        yf, sqf, qf, kf, gf = (flat(t) for t in (y, sq, qT, kT, gT))
        rs = misc[:, 2048:3072]
        rs1 = misc[:, 2048:2304]
        dec = misc[:, 0:2048].rearrange("p (h s) -> p h s", h=RET_H)

        def wide(ap, n):
            return ap.unsqueeze(1).to_broadcast([ap.shape[0], n, ap.shape[1]])

        def pair(t, j):
            return t[:, 2 * j:2 * j + 2, :]

        def two(ap):
            return ap.rearrange("p (t s) -> p t s", t=2)

        acc = ctx.enter_context(nc.psum_tensor("acc", [128, NT, S], f32))
        ring = ctx.enter_context(nc.psum_tensor("ring", [128, 4, 512], f32))

        def bank(i):
            return ring[:, i, :]

        raw_in = [sem(f"raw_in{i}") for i in range(RAW)]
        hi_made, lo_made = sem("hi_made"), sem("lo_made")
        chunk_used = sem("chunk_used")
        gemm_free = sem("gemm_free")
        const_in, x_in, par_in, dec_in, p_in = (sem(n) for n in ("const_in", "x_in", "par_in", "dec_in", "p_in"))
        out_made, out_in = sem("out_made"), sem("out_in")
        acc_zero, acc_done = sem("acc_zero"), sem("acc_done")
        xh_made, x_made, h_made = sem("xh_made"), sem("x_made"), sem("h_made")
        y_made, mean_done, yc_made = sem("y_made"), sem("mean_done"), sem("yc_made")
        sq_made, var_done, rs_made = (sem(n) for n in ("sq_made", "var_done", "rs_made"))
        hid_sq, hid_hi, hid_lo = sem("hid_sq"), sem("hid_hi"), sem("hid_lo")
        a_copied, conv_step, conv_made, gelu_made = (sem(n) for n in ("a_copied", "conv_step", "conv_made", "gelu_made"))
        prod_made, prod_hi, prod_lo = sem("prod_made"), sem("prod_hi"), sem("prod_lo")
        p_hi, p_lo, sig_made = sem("p_hi"), sem("p_lo"), sem("sig_made")
        wf_made, r_col_done, r_col_copied = sem("wf_made"), sem("r_col_done"), sem("r_col_copied")
        silu_made = sem("silu_made")
        z_scaled, gelu_scaled = sem("z_scaled"), sem("gelu_scaled")
        dve_own, act_own, pool_own = sem("dve_own"), sem("act_own"), sem("pool_own")
        (a1_done, a1_copied, gate_done, g_ln, g_cum, g_exp, g_kend, g_dec, g_attd, g_attc, g_attm, g_ktd, g_ktc,
         g_ud, g_st, g_od, g_sq, g_var, g_rs) = (sem("gla_" + n) for n in (
             "a1_done", "a1_copied", "gate_done", "ln", "cum", "exp", "kend", "dec", "attd", "attc", "attm",
             "ktd", "ktc", "ud", "st", "od", "sq", "var", "rs"))
        s_z, s_ln, s_sp, s_L, s_lw, s_w, s_wm, s_o = (sem("sb_" + n) for n in ("z", "ln", "sp", "L", "lw", "w", "wm", "o"))
        f_log, f_logit, f_ln, f_cum, f_z, f_mx, f_e, f_p, f_td, f_tc, f_o = (
            sem("fox_" + n) for n in ("log", "logit", "lnf", "cum", "z", "mx", "e", "p", "td", "tc", "o"))
        r_rot, r_rdy, r_s, r_m, r_o, r_c, r_mean, r_yc, r_sq, r_var, r_rs = (
            sem("ret_" + n) for n in ("rot", "rdy", "s", "m", "o", "c", "mean", "yc", "sq", "var", "rs"))

        class Own:

            def __init__(self, eng, s):
                self.eng, self.s, self.n = eng, s, 0

            def mark(self, ins):
                self.n += 1
                ins.then_inc(self.s, 1)
                return self.n

            def need(self, n):
                self.eng.wait_ge(self.s, n)

            def sync(self, ins):
                self.need(self.mark(ins))

        block = ctx.enter_context(nc.Block())

        @block.sync
        def _(sp):
            sp.dma_start(hT[:, :, :], xT).then_inc(x_in, 16)
            for c in range(RAW):
                sp.dma_start(raw[:, c, :], wstream[c]).then_inc(raw_in[c], 16)
            with sp.Fori(1, N_CHUNKS // RAW) as m:
                for j in range(RAW):
                    sp.wait_ge(lo_made, m * RAW + (j + 1 - RAW))
                    sp.dma_start(raw[:, j, :], wstream[m * RAW + j]).then_inc(raw_in[j], 16)
            for c in range(N_CHUNKS // RAW * RAW, N_CHUNKS):
                sp.wait_ge(lo_made, c + 1 - RAW)
                sp.dma_start(raw[:, c % RAW, :], wstream[c]).then_inc(raw_in[c % RAW], 16)
            for j in range(4):
                sp.wait_ge(out_made, j + 1)
                sp.dma_start(out[:, 2 * j:2 * j + 2, :], pair(y, j)).then_inc(out_in, 16)
            sp.wait_ge(out_in, 4 * 16)

        def split_hi(act, c, m=0):
            if c >= N_CHUNKS:
                return
            act.wait_ge(raw_in[c % RAW], m * 16 + 16 * (c // RAW + 1))
            if c >= SPLIT:
                act.wait_ge(chunk_used, m * RAW + (c - SPLIT + 1))
            act.copy(whi[:, c % SPLIT, :], raw[:, c % RAW, :]).then_inc(hi_made, 1)

        def split_lo(dve, c, m=0):
            if c >= N_CHUNKS:
                return
            dve.wait_ge(hi_made, m * RAW + (c + 1))
            if c >= SPLIT:
                dve.wait_ge(chunk_used, m * RAW + (c - SPLIT + 1))
            dve.tensor_tensor(wlo[:, c % SPLIT, :], raw[:, c % RAW, :], whi[:, c % SPLIT, :].bitcast(f32),
                              ALU.subtract).then_inc(lo_made, 1)

        @block.tensor
        def _(pe):
            def three(o, l1, l2, r1, r2, start, stop, **kw):
                pe.matmul(o, l1, r1, start=start, stop=False, **kw)
                pe.matmul(o, l1, r2, start=False, stop=False, **kw)
                return pe.matmul(o, l2, r1, start=False, stop=stop, **kw)

            def gemm(c, b, x_need=None, tokens_out=False, m=0):
                pe.wait_ge(lo_made, m * RAW + (c + 1))
                wh, wl = whi[:, c % SPLIT, :], wlo[:, c % SPLIT, :]
                outs = [bank(b)[:, t * 256:t * 256 + 256] for t in range(2)]
                if x_need is not None:
                    for k in range(NT):
                        if k % 2 == 0:
                            pe.wait_ge(x_made, 4 * x_need + k // 2 + 1)
                        for t in range(2):
                            w = slice(k * 256 + t * 128, k * 256 + t * 128 + 128)
                            mm = three(outs[t], wh[:, w], wl[:, w], xhi[:, k, :], xlo[:, k, :], k == 0 and t == 0,
                                       k == NT - 1, skip_group_check=True)
                    mm.then_inc(chunk_used, 1)
                    return
                for t in range(2):
                    for k in range(NT):
                        if tokens_out:
                            tok, w = slice(t * 128, t * 128 + 128), slice(k * 256, k * 256 + 256)
                            mm = three(outs[t], xhi[:, k, tok], xlo[:, k, tok], wh[:, w], wl[:, w], k == 0, k == NT - 1)
                        else:
                            w = slice(k * 256 + t * 128, k * 256 + t * 128 + 128)
                            mm = three(outs[t], wh[:, w], wl[:, w], xhi[:, k, :], xlo[:, k, :], k == 0, k == NT - 1)
                mm.then_inc(chunk_used, 1)

            def down(c, s, m=0, last=False):
                pe.wait_ge(lo_made, m * RAW + (c + 1))
                for k in range(2):
                    for t in range(NT):
                        w = slice(k * D + t * 128, k * D + t * 128 + 128)
                        mm = three(acc[:, t, :], whi[:, c % SPLIT, w], wlo[:, c % SPLIT, w], hhi[:, s, k, :],
                                   hlo[:, s, k, :], False, False, skip_group_check=True)
                        if last and k == 1 and t % 2 and t < NT - 1:
                            mm.then_inc(acc_done, 1)
                mm.then_inc(chunk_used, 1)

            def sums(src, made, base, o, done):
                for t in range(NT):
                    if t % 2 == 0:
                        pe.wait_ge(made, base + t // 2 + 1)
                    mm = pe.matmul(o, ones, src[:, t, :], start=(t == 0), stop=(t == NT - 1))
                mm.then_inc(done, 1)

            def layer_norm(n):
                sums(y, y_made, 4 * n, bank(0)[:, 0:S], mean_done)
                sums(sq, sq_made, 4 * n, bank(1)[:, 0:S], var_done)

            def squares_sum(n, o):
                sums(sq, sq_made, 4 * (4 + n), o, var_done)

            def ple_projection(c, L):
                pe.wait_ge(lo_made, c + 1)
                pe.wait_ge(p_lo, L + 1)
                for j in range(4):
                    pe.wait_ge(y_made, 4 * (6 + 3 * L) + j + 1)
                    for k in range(2):
                        for t in (2 * j, 2 * j + 1):
                            w = slice(k * D + t * 128, k * D + t * 128 + 128)
                            mm = three(acc[:, t, :], whi[:, c % SPLIT, w], wlo[:, c % SPLIT, w], hhi[:, 2, k, :],
                                       hlo[:, 2, k, :], k == 0 and t % 2 == 0, k == 1, skip_group_check=True)
                mm.then_inc(chunk_used, 1)

            def product(c, x_need):
                for j in range(4):
                    gemm(c + j, j, x_need if j == 0 else None)

            def wide_product(c, n, free, x_need, tokens, between):
                for j in range(n):
                    if j >= 4:
                        pe.wait_ge(gemm_free, free + j - 3)
                    gemm(c + j, j % 4, x_need if j == 0 else None, j in tokens)
                    if j in between:
                        between[j]()
                pe.wait_ge(gemm_free, free + n)

            def mlp(n, x_need):
                c0, free, h0 = C_MLP[n], FREE[f"mlp{n}"], N_UP * n
                gemm(c0, 0, x_need)
                pe.wait_ge(acc_zero, ZERO[f"mlp{n}"] + 1)
                with pe.Fori(0, (N_UP - 1) // 3) as m:
                    for i in range(1, 4):
                        cu = c0 + 2 * i - 1
                        pe.wait_ge(gemm_free, m * 3 + (free + i - 2))
                        gemm(cu, i % 3, m=m)
                        pe.wait_ge(hid_lo, m * 3 + (h0 + i))
                        down(cu + 1, (i - 1) % 3, m=m)
                pe.wait_ge(hid_lo, h0 + N_UP)
                down(c0 + 2 * N_UP - 1, (N_UP - 1) % 3, last=True)

            def ffn(L, x_need):
                c0, b = C_FFN[L], N_FF * L
                gemm(c0, 0, x_need)
                squares_sum(3 * L + 1, bank(3)[:, 0:S])
                gemm(c0 + 1, 1)
                pe.wait_ge(acc_zero, ZERO[f"ffn{L}"] + 1)
                pe.wait_ge(rs_made, 4 + 3 * L + 2)
                with pe.Fori(0, (N_FF - 1) // 2) as m:
                    for i in range(1, 3):
                        ca = c0 + 3 * i - 1
                        pe.wait_ge(a_copied, m * 2 + (b + i))
                        gemm(ca, 2 * (i % 2), m=m)
                        pe.wait_ge(prod_made, m * 2 + (b + i))
                        gemm(ca + 1, 2 * (i % 2) + 1, m=m)
                        pe.wait_ge(prod_lo, m * 2 + (b + i))
                        down(ca + 2, (i - 1) % 2, m=m)
                pe.wait_ge(prod_lo, b + N_FF)
                down(c0 + 3 * N_FF - 1, (N_FF - 1) % 2, last=True)

            def head(h):
                return slice(64 * (h % 2), 64 * (h % 2) + 64)

            def scores(b, l, r):
                pe.matmul(b[:, 0:256], l[:, 0:128], r, start=True, stop=False, skip_group_check=True)
                return pe.matmul(b[:, 256:384], l[:, 128:256], r[:, 128:256], start=False, stop=False,
                                 skip_group_check=True)

            def values(t, h, col, W):
                o = acc[head(h), t, :]
                pe.matmul(o, v[:, 0, col:col + 64], W[:, 0:256], start=True, stop=False, skip_group_check=True)
                return pe.matmul(o[:, 128:256], v[:, 1, col:col + 64], W[:, 256:384], start=False, stop=True,
                                 skip_group_check=True)

            def gate_input():
                pe.wait_ge(x_in, 16)
                pe.wait_ge(par_in, 5 * 16)
                pe.wait_ge(const_in, 16)
                for k in range(NT):
                    mm = pe.matmul(acc[0:16, 0, :], wa1_sb[:, k, :], hT[:, k, :], start=(k == 0), stop=(k == NT - 1))
                mm.then_inc(a1_done, 1)

            def gate_logits():
                pe.wait_ge(a1_copied, 1)
                for h in range(GLA_H):
                    mm = pe.matmul(acc[:, 2 + h, :], wa2_sb[:, h * 128:h * 128 + 128], a1_sb,
                                   start=(h % 2 == 0), stop=True, skip_group_check=True)
                mm.then_inc(gate_done, 1)

            wide_product(C_GLA_IN, 12, FREE["gla_in"], 0, range(4, 8), {0: gate_input, 1: gate_logits})
            for h in range(GLA_H):
                pe.wait_ge(g_kend, h + 1)
                for t in range(2):
                    mm = pe.transpose(ring[:, t, h * 128:h * 128 + 128], kT[:, 4 + h, t * 128:t * 128 + 128], ident)
            mm.then_inc(g_ktd, 1)
            pe.wait_ge(g_dec, 1)
            for t in range(2):
                tok = slice(t * 128, t * 128 + 128)
                for h in range(GLA_H):
                    mm = pe.matmul(ring[:, 2 + t, h * 128:h * 128 + 128], kT[:, h, tok], qT[:, h, tok],
                                   start=True, stop=True)
                mm.then_inc(g_attd, 1)
            pe.wait_ge(g_ktc, 1)
            keT = two(yf[:, 0:1024])
            for n in range(3):
                r = slice(64 * (n % 2), 64 * (n % 2) + 64)
                if n:
                    pe.wait_ge(g_st, n)
                for h in range(GLA_H):
                    mm = pe.matmul(ring[:, h // 2, (h % 2) * 256:(h % 2) * 256 + 256],
                                   keT[r, n // 2, h * 128:h * 128 + 128], v[r, n // 2, h * 256:h * 256 + 256],
                                   start=True, stop=True)
                mm.then_inc(g_ud, 1)
            pe.wait_ge(g_attm, 2)
            pe.wait_ge(g_st, 3)
            attm = two(sqf[:, 1024:2048])
            for h in range(GLA_H):
                for e in range(2):
                    ec = h * 256 + e * 128
                    for t in range(2):
                        pe.matmul(acc[:, 2 * h + e, t * 128:t * 128 + 128], v[:, t, ec:ec + 128],
                                  attm[:, t, h * 128:h * 128 + 128], start=True, stop=False, skip_group_check=True)
                        for n in (2 * t, 2 * t + 1):
                            if n:
                                sc = (n - 1) * 1024 + ec
                                mm = pe.matmul(acc[:, 2 * h + e, n * 64:n * 64 + 64], misc[:, sc:sc + 128],
                                               qT[:, h, n * 64:n * 64 + 64], start=False, stop=True,
                                               skip_group_check=True)
                mm.then_inc(g_od, 1)
            for h in range(GLA_H):
                pe.wait_ge(g_sq, h + 1)
                for e in range(2):
                    mm = pe.matmul(ring[:, 2 + h // 2, (h % 2) * 256:(h % 2) * 256 + 256], ones, sq[:, 2 * h + e, :],
                                   start=(e == 0), stop=(e == 1))
                if h % 2:
                    mm.then_inc(g_var, 1)
            product(C_GLA_O, 1)
            layer_norm(0)
            mlp(0, 2)
            layer_norm(1)

            wide_product(C_SB_IN, 12, FREE["sb_in"], 3, range(4, 8), {})
            for i in range(SB_H + 3):
                if i < SB_H:
                    h = i
                    if h >= 4:
                        pe.wait_ge(s_w, h - 3)
                    scores(bank(h % 4), kT[head(h), h // 2, :], qT[head(h), h // 2, :]).then_inc(s_z, 1)
                if 0 <= i - 1 < SB_H:
                    h = i - 1
                    b, L = bank(h % 4), yf[:, (h % 2) * 384:(h % 2) * 384 + 384]
                    pe.wait_ge(s_L, h + 1)
                    pe.matmul(b[:, 0:256], tri, L[:, 0:256], start=False, stop=False, skip_group_check=True)
                    pe.matmul(b[:, 128:256], neg, L[:, 256:384], start=False, stop=False, skip_group_check=True)
                    pe.matmul(b[:, 256:384], tri, L[:, 256:384], start=False, stop=True,
                              skip_group_check=True).then_inc(s_lw, 1)
                if 0 <= i - 3:
                    h = i - 3
                    pe.wait_ge(s_wm, h + 1)
                    values(h // 2, h, h * 64, sqf[:, (h % 3) * 384:(h % 3) * 384 + 384]).then_inc(s_o, 1)
            product(C_SB_O, 4)
            layer_norm(2)
            mlp(1, 5)
            layer_norm(3)

            for L in range(DEPTH):
                X = 6 + 4 * L

                def norm_and_forget():
                    squares_sum(3 * L, acc[:, 7, :])
                    if L == 0:
                        pe.wait_ge(wf_made, 1)
                    for k in range(NT):
                        mm = pe.matmul(acc[0:FOX_H, 0, :], wf_sb[:, L, k, :], hT[:, k, :], start=(k == 0),
                                       stop=(k == NT - 1))
                    mm.then_inc(f_log, 1)

                def scale_column():
                    pe.wait_ge(rs_made, 4 + 3 * L + 1)
                    for t in range(2):
                        mm = pe.matmul(acc[:, 4, t:t + 1], rs1[:, t * 128:t * 128 + 128], ident[:, 0:1],
                                       start=(t == 0), stop=True, skip_group_check=True)
                    mm.then_inc(r_col_done, 1)

                def rotate():
                    pe.wait_ge(r_col_copied, L + 1)
                    pe.wait_ge(f_cum, L + 1)
                    pe.wait_ge(gemm_free, FREE[f"in{L}"] + 4)
                    for t in range(NT):
                        mm = pe.matmul(acc[:, t, :], perm, (qT if t < 4 else kT)[:, 4 + t % 4, :], start=(t % 2 == 0),
                                       stop=True, skip_group_check=True)
                    mm.then_inc(r_rot, 1)

                wide_product(C_IN[L], 14, FREE[f"in{L}"], X, (8, 9, 10, 11),
                             {0: norm_and_forget, 2: scale_column, 6: rotate})
                for i in range(FOX_H + 4):
                    if i < FOX_H:
                        h, b = i, bank(i % 2)
                        if h >= 2:
                            pe.wait_ge(f_mx, FOX_H * L + h - 1)
                        q, k, nc_h = qT[head(h), h // 2, :], kT[head(h), h // 2, :], y[0:FOX_H, h, :]
                        pe.matmul(b[:, 0:128], q[:, 0:128], k[:, 0:128], start=True, stop=False, skip_group_check=True)
                        pe.matmul(b[:, 128:384], q[:, 128:256], k, start=False, stop=False, skip_group_check=True)
                        pe.matmul(b[:, 0:128], ones[0:FOX_H, :], nc_h[:, 0:128], start=False, stop=False,
                                  skip_group_check=True)
                        pe.matmul(b[:, 128:384], ones[0:FOX_H, :], nc_h, start=False, stop=True,
                                  skip_group_check=True).then_inc(f_z, 1)
                    if 0 <= i - 2 < FOX_H:
                        h = i - 2
                        b, P = bank(2 + h % 2), sqf[:, (h % 3) * 384:(h % 3) * 384 + 384]
                        pe.wait_ge(f_p, FOX_H * L + h + 1)
                        if h >= 2:
                            pe.wait_ge(f_tc, FOX_H * L + h - 1)
                        pe.transpose(b[:, 0:128], P[:, 0:128], ident)
                        pe.transpose(b[:, 128:256], P[:, 128:256], ident)
                        pe.transpose(b[:, 256:384], P[:, 256:384], ident).then_inc(f_td, 1)
                    if 0 <= i - 4:
                        h = i - 4
                        pe.wait_ge(f_tc, FOX_H * L + h + 1)
                        if h == 0:
                            pe.wait_ge(r_rdy, 2 * L + 2)
                        values(h // 2, h, h * 64,
                               sqf[:, 1152 + (h % 2) * 384:1536 + (h % 2) * 384]).then_inc(f_o, 1)
                for i in range(RET_H + 1):
                    if i < RET_H:
                        h, t = i, 4 + i // 2
                        if h >= 2:
                            pe.wait_ge(r_m, RET_H * L + h - 1)
                        scores(bank(h % 2), kT[head(h), t, :], qT[head(h), t, :]).then_inc(r_s, 1)
                    if i >= 1:
                        h = i - 1
                        pe.wait_ge(r_m, RET_H * L + h + 1)
                        values(4 + h // 2, h, 512 + h * 64, yf[:, (h % 2) * 384:(h % 2) * 384 + 384]).then_inc(r_o, 1)
                for j in range(2):
                    pe.wait_ge(r_c, 2 * L + j + 1)
                    pe.matmul(bank(j), blk, yf[:, 1024 + j * 512:1536 + j * 512], start=True, stop=True).then_inc(r_mean, 1)
                for j in range(2):
                    pe.wait_ge(r_sq, 2 * L + j + 1)
                    pe.matmul(bank(2 + j), blk, sqf[:, j * 512:j * 512 + 512], start=True, stop=True).then_inc(r_var, 1)
                product(C_OUT[L], X + 1)
                ffn(L, X + 2)
                ple_projection(C_PROJ[L], L)
                for j in range(4):
                    if j == 3:
                        pe.wait_ge(rs_made, 4 + 3 * L + 3)
                    gemm(C_GATE[L] + j, j, X + 3 if j == 0 else None)
                    if j == 0:
                        squares_sum(3 * L + 2, bank(3)[:, 0:S])
            squares_sum(6, bank(0)[:, 0:S])

        @block.scalar
        def _(act):
            own = Own(act, act_own)
            for dst, src in ((pv[:, :], params), (wa1_sb[:, :, :], wa1), (wa2_sb[:, :], wa2), (wf_sb[:, :, :, :], wf),
                             (fb_sb[:, :], fbias)):
                act.dma_start(dst, src).then_inc(par_in, 16)
            act.dma_start(cst[:, :], consts).then_inc(const_in, 16)

            def x_high(X, src, waits):
                for j in range(4):
                    act.wait_ge(*waits(j))
                    act.copy(pair(xhi, j), src(j)).then_inc(xh_made, 1)

            def from_h(X):
                return lambda j: (h_made, H_OF[X] + j + 1)

            def squares(n, src, made, base):
                for j in range(4):
                    act.wait_ge(made, base + j + 1)
                    act.activation(pair(sq, j), pair(src, j), ACT.Square).then_inc(sq_made, 1)

            def power(r, psum, scale, eps):
                own.sync(act.activation(r, psum, ACT.Ln, bias=eps_col[eps], scale=scale))
                return act.activation(r, r, ACT.Exp, scale=-0.5)

            def inverse_root(n, psum, eps):
                act.wait_ge(var_done, n + 1)
                power(rs1, psum, 1 / D, eps).then_inc(rs_made, 1)

            def ln_part(n):
                squares(n, y, yc_made, 4 * n)
                inverse_root(n, bank(1)[:, 0:S], LN_EPS)

            def weighted_high(n, w, i0, j):
                act.wait_ge(y_made, 4 * (4 + n) + j + 1)
                for t in (2 * j, 2 * j + 1):
                    ins = act.activation(xhi[:, t, :], hT[:, t, :], ACT.Copy, scale=par(w, i0 + t))
                ins.then_inc(xh_made, 1)

            def squares_of_h(n):
                squares(4 + n, hT, y_made, 4 * (4 + n))

            def evacuate(c, n, dest, between):
                for j in range(n):
                    split_hi(act, c + j + AHEAD)
                    act.wait_ge(chunk_used, c + j + 1)
                    d, func, scale = dest(j)
                    if func is None:
                        act.copy(d, two(bank(j % 4))).then_inc(gemm_free, 1)
                    else:
                        act.activation(d, two(bank(j % 4)), func, scale=scale).then_inc(gemm_free, 1)
                    if j in between:
                        between[j]()

            def v_part(j):
                return v[:, :, j * 256:j * 256 + 256]

            def ahead(c, n):
                for j in range(n):
                    split_hi(act, c + j + AHEAD)

            def mlp(n):
                c0, free, h0 = C_MLP[n], FREE[f"mlp{n}"], N_UP * n

                def hidden(c, i, m=0):
                    s = i % 3
                    act.wait_ge(chunk_used, m * RAW + (c + 1))
                    act.activation(pair(qT, s), two(bank(s)), ACT.Relu).then_inc(gemm_free, 1)
                    act.wait_ge(gemm_free, m * 3 + (free + i + 1))
                    act.activation(hhi[:, s, :, :], pair(qT, s), ACT.Square).then_inc(hid_hi, 1)

                split_hi(act, c0 + AHEAD)
                hidden(c0, 0)
                with act.Fori(0, (N_UP - 1) // 3) as m:
                    for i in range(1, 4):
                        cu = c0 + 2 * i - 1
                        split_hi(act, cu + AHEAD, m)
                        hidden(cu, i, m)
                        split_hi(act, cu + 1 + AHEAD, m)
                split_hi(act, c0 + 2 * N_UP - 1 + AHEAD)

            def ffn(L):
                c0, b = C_FFN[L], N_FF * L

                def gelu(i, m=0):
                    s = i % 2
                    act.wait_ge(conv_made, m * 2 + (b + i + 1))
                    act.activation(kf[:, 1024 + s * 512:1536 + s * 512], kf[:, s * 512:s * 512 + 512],
                                   ACT.Gelu).then_inc(gelu_made, 1)

                def high(i, m=0):
                    s = i % 2
                    act.wait_ge(prod_made, m * 2 + (b + i + 1))
                    act.copy(hhi[:, s, :, :], two(gf[:, s * 512:s * 512 + 512])).then_inc(prod_hi, 1)

                split_hi(act, c0 + AHEAD)
                inverse_root(4 + 3 * L + 1, bank(3)[:, 0:S], RMS_EPS)
                split_hi(act, c0 + 1 + AHEAD)
                gelu(0)
                high(0)
                with act.Fori(0, (N_FF - 1) // 2) as m:
                    for i in range(1, 3):
                        ca = c0 + 3 * i - 1
                        split_hi(act, ca + AHEAD, m)
                        split_hi(act, ca + 1 + AHEAD, m)
                        gelu(i, m)
                        split_hi(act, ca + 2 + AHEAD, m)
                        high(i, m)
                split_hi(act, c0 + 3 * N_FF - 1 + AHEAD)

            def load_exp_ln():
                act.preload_act_table_set("natural_log_exp_and_others")

            load_exp_ln()
            x_high(0, lambda j: pair(hT, j), lambda j: (x_in, 16))
            for c in range(AHEAD):
                split_hi(act, c)

            def a1_copy():
                act.wait_ge(a1_done, 1)
                act.copy(a1_sb, acc[0:16, 0, :]).then_inc(a1_copied, 1)

            def gate_ln():
                act.wait_ge(gate_done, 1)
                act.wait_ge(par_in, 5 * 16)
                for h in range(GLA_H):
                    n = own.mark(act.activation(sqf[:, h * 256:h * 256 + 256], acc[:, 2 + h, :], ACT.Abs,
                                                bias=par("b_a", h)))
                own.need(n)
                own.sync(act.activation(sqf[:, 0:1024], sqf[:, 0:1024], ACT.Exp, scale=-1.0))
                act.activation(sqf[:, 0:1024], sqf[:, 0:1024], ACT.Ln, bias=1.0).then_inc(g_ln, 1)

            def gate_exp():
                act.wait_ge(g_cum, 2)
                act.activation(yf[:, 0:1024], yf[:, 0:1024], ACT.Exp, scale=1 / 16).then_inc(g_exp, 1)
                act.activation(sqf[:, 0:1024], yf[:, 1024:2048], ACT.Exp, scale=1 / 16).then_inc(g_exp, 1)
                act.activation(sqf[:, 1024:2048], yf[:, 1024:2048], ACT.Exp, scale=-1 / 16).then_inc(g_exp, 1)

            def gla_dest(j):
                if j < 4:
                    return pair(qT if j < 2 else kT, j % 2), None, None
                if j < 8:
                    return v_part(j - 4), None, None
                return pair(gT, j - 8), ACT.Silu, 1.0

            evacuate(C_GLA_IN, 12, gla_dest, {0: a1_copy, 1: gate_ln, 4: gate_exp})
            load_exp_ln()
            act.wait_ge(g_ktd, 1)
            own.mark(act.copy(yf[:, 0:512], ring[:, 0, :]))
            act.copy(yf[:, 512:1024], ring[:, 1, :]).then_inc(g_ktc, 1)
            for t in range(2):
                act.wait_ge(g_attd, t + 1)
                act.copy(sqf[:, 1024 + t * 512:1536 + t * 512], ring[:, 2 + t, :]).then_inc(g_attc, 1)
            for h in range(GLA_H):
                act.wait_ge(g_od, h + 1 if h < 2 else GLA_H)
                act.activation(pair(sq, h), pair(acc, h), ACT.Square).then_inc(g_sq, 1)
            for j in range(2):
                act.wait_ge(g_var, j + 1)
                power(rs[:, j * 512:j * 512 + 512], bank(2 + j), 1 / 256, RMS_EPS).then_inc(g_rs, 1)
            x_high(1, lambda j: pair(y, j), from_h(1))
            ahead(C_GLA_O, 4)
            ln_part(0)
            x_high(2, lambda j: pair(hT, j), from_h(2))
            act.dma_start(misc[:, 0:2048], decay).then_inc(dec_in, 16)
            mlp(0)
            ln_part(1)
            x_high(3, lambda j: pair(hT, j), from_h(3))

            def sb_dest(j):
                if j < 4:
                    return pair(kT, j), None, None
                if j < 8:
                    return v_part(j - 4), None, None
                return pair(qT, j - 8), ACT.Copy, 0.125

            evacuate(C_SB_IN, 12, sb_dest, {})
            for i in range(SB_H + 1):
                if i < SB_H:
                    h = i
                    a, b = gf[:, (h % 2) * 384:(h % 2) * 384 + 384], bank(h % 4)[:, 0:384]
                    act.wait_ge(s_z, h + 1)
                    if h >= 2:
                        act.wait_ge(s_sp, h - 1)
                    own.sync(act.activation(a, b, ACT.Abs))
                    own.sync(act.activation(a, a, ACT.Exp, scale=-1.0))
                    act.activation(a, a, ACT.Ln, bias=1.0).then_inc(s_ln, 1)
                if i >= 1:
                    h = i - 1
                    act.wait_ge(s_lw, h + 1)
                    if h >= 3:
                        act.wait_ge(s_o, h - 2)
                    act.activation(sqf[:, (h % 3) * 384:(h % 3) * 384 + 384], bank(h % 4)[:, 0:384],
                                   ACT.Exp).then_inc(s_w, 1)
            x_high(4, lambda j: pair(acc, j), lambda j: (s_o, 4 * j + 4))
            ahead(C_SB_O, 4)
            ln_part(2)
            x_high(5, lambda j: pair(hT, j), from_h(5))
            mlp(1)
            ln_part(3)

            for L in range(DEPTH):
                X = 6 + 4 * L
                if L:
                    act.wait_ge(p_lo, L)
                act.dma_start(two(gf[:, 1024:1536]), pT[L]).then_inc(p_in, 16)
                if L == 0:
                    for j in range(4):
                        weighted_high(0, "attn_w", 0, j)
                squares_of_h(3 * L)
                split_hi(act, C_IN[L] + AHEAD)
                inverse_root(4 + 3 * L, acc[:, 7, :], RMS_EPS)
                split_hi(act, C_IN[L] + 1 + AHEAD)

                def forget_ln():
                    act.wait_ge(f_logit, L + 1)
                    own.sync(act.activation(cum[:, 0, :], cum[:, 1, :], ACT.Abs, bias=fb_sb[:, L:L + 1]))
                    own.sync(act.activation(cum[:, 0, :], cum[:, 0, :], ACT.Exp, scale=-1.0))
                    act.activation(cum[:, 0, :], cum[:, 0, :], ACT.Ln, bias=1.0).then_inc(f_ln, 1)

                def p_high():
                    act.wait_ge(p_in, 16 * (L + 1))
                    act.copy(hhi[:, 2, :, :], two(gf[:, 1024:1536])).then_inc(p_hi, 1)

                forget_ln()
                split_hi(act, C_IN[L] + 2 + AHEAD)
                act.wait_ge(r_col_done, L + 1)
                act.copy(r_col[:, :], acc[:, 4, 0:2]).then_inc(r_col_copied, 1)
                for j in range(3, 14):
                    split_hi(act, C_IN[L] + j + AHEAD)
                    if 8 <= j < 12:
                        act.wait_ge(chunk_used, C_IN[L] + j + 1)
                        act.wait_ge(gemm_free, FREE[f"in{L}"] + 8)
                        act.wait_ge(r_col_copied, L + 1)
                        own.mark(act.activation(v_part(j - 8)[:, 0, :], bank(j % 4)[:, 0:256], ACT.Copy, scale=r_col[:, 0:1]))
                        act.activation(v_part(j - 8)[:, 1, :], bank(j % 4)[:, 256:512], ACT.Copy,
                                       scale=r_col[:, 1:2]).then_inc(gemm_free, 1)
                    if j == 9:
                        p_high()
                    if j >= 12:
                        act.wait_ge(gemm_free, FREE[f"in{L}"] + j + 1)
                        act.activation(pair(gT, j - 12), pair(gT, j - 12), ACT.Silu).then_inc(silu_made, 1)
                load_exp_ln()
                for i in range(FOX_H + 2):
                    if i < FOX_H:
                        h = i
                        P = sqf[:, (h % 3) * 384:(h % 3) * 384 + 384]
                        act.wait_ge(f_mx, FOX_H * L + h + 1)
                        act.activation(P[:, 0:128], P[:, 0:128], ACT.Exp, bias=stat[:, h % 4, 2:3],
                                       accum_out=stat[:, h % 4, 4:5])
                        act.activation(P[:, 128:384], P[:, 128:384], ACT.Exp, bias=stat[:, h % 4, 3:4],
                                       accum_out=stat[:, h % 4, 5:6]).then_inc(f_e, 1)
                    if i >= 2:
                        h = i - 2
                        act.wait_ge(f_td, FOX_H * L + h + 1)
                        if h >= 2:
                            act.wait_ge(f_o, FOX_H * L + h - 1)
                        act.copy(sqf[:, 1152 + (h % 2) * 384:1536 + (h % 2) * 384], bank(2 + h % 2)[:, 0:384]).then_inc(f_tc, 1)
                for j in range(2):
                    act.wait_ge(f_o, FOX_H * L + 4 * j + 4)
                    act.copy(pair(xhi, j), pair(acc, j)).then_inc(xh_made, 1)
                for j in range(2):
                    act.wait_ge(r_o, RET_H * L + 4 * j + 4)
                    act.copy(pair(y, 2 + j), pair(acc, 2 + j)).then_inc(r_c, 1)
                for j in range(2):
                    act.wait_ge(r_yc, 2 * L + j + 1)
                    act.activation(pair(sq, j), pair(y, 2 + j), ACT.Square).then_inc(r_sq, 1)
                for j in range(2):
                    act.wait_ge(r_var, 2 * L + j + 1)
                    power(rs[:, j * 512:j * 512 + 512], bank(2 + j), 1 / 64, GN_EPS).then_inc(r_rs, 1)
                for j in range(2):
                    act.wait_ge(h_made, H_OF[X + 1] + j + 1)
                    act.copy(pair(xhi, 2 + j), pair(y, 2 + j)).then_inc(xh_made, 1)
                ahead(C_OUT[L], 4)
                act.wait_ge(chunk_used, C_OUT[L] + 4)
                for j in range(4):
                    weighted_high(3 * L + 1, "ffn_w", 8 * L, j)
                squares_of_h(3 * L + 1)
                ffn(L)
                load_exp_ln()
                for j in range(4):
                    weighted_high(3 * L + 2, "ple_w", 8 * L, j)
                ahead(C_PROJ[L], 1)
                squares_of_h(3 * L + 2)
                split_hi(act, C_GATE[L] + AHEAD)
                inverse_root(4 + 3 * L + 2, bank(3)[:, 0:S], RMS_EPS)
                for j in range(4):
                    if j:
                        split_hi(act, C_GATE[L] + j + AHEAD)
                    if j == 3 and L + 1 < DEPTH:
                        act.wait_ge(chunk_used, C_GATE[L] + 4)
                        weighted_high(3 * L + 3, "attn_w", 8 * L + 8, 0)
                    act.wait_ge(z_scaled, 4 * L + j + 1)
                    z = kf[:, j * 512:j * 512 + 512]
                    act.activation(z, z, ACT.Sigmoid).then_inc(sig_made, 1)
                load_exp_ln()
                if L + 1 < DEPTH:
                    for j in range(1, 4):
                        weighted_high(3 * L + 3, "attn_w", 8 * L + 8, j)
            squares_of_h(6)
            inverse_root(4 + 6, bank(0)[:, 0:S], RMS_EPS)

        @block.vector
        def _(dve):
            own = Own(dve, dve_own)

            def x_low(X, src, js=range(4)):
                for j in js:
                    dve.wait_ge(xh_made, 4 * X + j + 1)
                    dve.tensor_tensor(pair(xlo, j), src(j), pair(xhi, j).bitcast(f32), ALU.subtract).then_inc(x_made, 1)

            def ahead(c, n):
                for j in range(n):
                    split_lo(dve, c + j + AHEAD)

            def zero_acc(s, n):
                dve.wait_ge(s, n)
                dve.memset(acc[:, :, :], 0.0).then_inc(acc_zero, 1)

            def residual(j, psum):
                dve.scalar_tensor_tensor(pair(y, j), pair(hT, j), ALPHA, psum, ALU.mult, ALU.add).then_inc(y_made, 1)

            def layer_norm(n, X):
                dve.wait_ge(y_made, 4 * n + 4)
                dve.wait_ge(mean_done, n + 1)
                for j in range(4):
                    dve.scalar_tensor_tensor(pair(y, j), wide(bank(0)[:, 0:S], 2), -1 / D, pair(y, j), ALU.mult,
                                             ALU.add).then_inc(yc_made, 1)
                dve.wait_ge(yc_made, 4 * n + 4)
                dve.wait_ge(rs_made, n + 1)
                marks = [own.mark(dve.tensor_tensor(pair(y, 0), pair(y, 0), wide(rs1, 2), ALU.mult))]
                for j in range(4):
                    if j < 3:
                        marks.append(own.mark(dve.tensor_tensor(pair(y, j + 1), pair(y, j + 1), wide(rs1, 2), ALU.mult)))
                    own.need(marks[j])
                    for t in (2 * j, 2 * j + 1):
                        ins = dve.tensor_scalar(hT[:, t, :], y[:, t, :], par("ln_g", 8 * n + t), par("ln_b", 8 * n + t),
                                                ALU.mult, ALU.add)
                    ins.then_inc(y_made if X is None else h_made, 1)
                    if X is not None and j:
                        x_low(X, lambda i: pair(hT, i), [j - 1])
                if X is not None:
                    x_low(X, lambda i: pair(hT, i), [3])

            def weighted_low(X, w, i0):
                for j in range(4):
                    dve.wait_ge(xh_made, 4 * X + j + 1)
                    for t in (2 * j, 2 * j + 1):
                        ins = dve.scalar_tensor_tensor(xlo[:, t, :], hT[:, t, :], par(w, i0 + t),
                                                       xhi[:, t, :].bitcast(f32), ALU.mult, ALU.subtract)
                    ins.then_inc(x_made, 1)

            def final_norm():
                dve.wait_ge(rs_made, 4 + 6 + 1)
                for j in range(4):
                    for t in (2 * j, 2 * j + 1):
                        ins = dve.scalar_tensor_tensor(y[:, t, :], hT[:, t, :], par("fin_w", t), rs1, ALU.mult, ALU.mult)
                    ins.then_inc(out_made, 1)

            def mlp(n):
                c0, free, h0 = C_MLP[n], FREE[f"mlp{n}"], N_UP * n

                def hidden(i, m=0):
                    s = i % 3
                    dve.wait_ge(gemm_free, m * 3 + (free + i + 1))
                    dve.tensor_tensor(pair(kT, s), pair(qT, s), pair(qT, s), ALU.mult).then_inc(hid_sq, 1)
                    dve.wait_ge(hid_sq, m * 3 + (h0 + i + 1))
                    dve.wait_ge(hid_hi, m * 3 + (h0 + i + 1))
                    dve.tensor_tensor(hlo[:, s, :, :], pair(kT, s), hhi[:, s, :, :].bitcast(f32),
                                      ALU.subtract).then_inc(hid_lo, 1)

                split_lo(dve, c0 + AHEAD)
                hidden(0)
                with dve.Fori(0, (N_UP - 1) // 3) as m:
                    for i in range(1, 4):
                        cu = c0 + 2 * i - 1
                        split_lo(dve, cu + AHEAD, m)
                        hidden(i, m)
                        split_lo(dve, cu + 1 + AHEAD, m)
                split_lo(dve, c0 + 2 * N_UP - 1 + AHEAD)

            def acc_ready(inst, c, j):
                if j < 3:
                    dve.wait_ge(acc_done, 3 * inst + j + 1)
                else:
                    dve.wait_ge(chunk_used, c + 1)

            def ffn(L):
                c0, b = C_FFN[L], N_FF * L
                pads = qf[:, 0:1032].rearrange("p (a s) -> p a s", a=4)[:, :, 0:2]
                own.sync(dve.memset(pads, 0.0))

                def a_part(c, i, m=0):
                    s = i % 2
                    dve.wait_ge(chunk_used, m * RAW + (c + 1))
                    pad = qf[:, s * 516:s * 516 + 516].rearrange("p (t s) -> p t s", t=2)
                    dve.tensor_tensor(pad[:, :, 2:258], two(bank(2 * s)), wide(rs1, 2), ALU.mult).then_inc(a_copied, 1)

                def conv(i, m=0):
                    s = i % 2
                    dve.wait_ge(a_copied, m * 2 + (b + i + 1))
                    for step in range(3):
                        for t in range(2):
                            o = kf[:, s * 512 + t * 256:s * 512 + t * 256 + 256]
                            at = s * 516 + t * 258 + 2 - step
                            tile = m * 4 + (2 * i + t)
                            w = pv[:, bass.ds(tile + (PV["conv_w"] + (3 * L + 2 - step) * FT), 1)]
                            if step == 0:
                                bias = pv[:, bass.ds(tile + (PV["conv_b"] + L * FT), 1)]
                                ins = dve.tensor_scalar(o, qf[:, at:at + 256], w, bias, ALU.mult, ALU.add)
                            else:
                                ins = dve.scalar_tensor_tensor(o, qf[:, at:at + 256], w, o, ALU.mult, ALU.add)
                        ins.then_inc(conv_step if step < 2 else conv_made, 1)
                        if step < 2:
                            dve.wait_ge(conv_step, m * 4 + (2 * (b + i) + step + 1))

                def gated(c, i, m=0):
                    s = i % 2
                    dve.wait_ge(gelu_made, m * 2 + (b + i + 1))
                    a = two(kf[:, 1024 + s * 512:1536 + s * 512])
                    dve.tensor_tensor(a, a, wide(rs1, 2), ALU.mult).then_inc(gelu_scaled, 1)
                    dve.wait_ge(gelu_scaled, m * 2 + (b + i + 1))
                    dve.wait_ge(chunk_used, m * RAW + (c + 1))
                    dve.tensor_tensor(gf[:, s * 512:s * 512 + 512], kf[:, 1024 + s * 512:1536 + s * 512],
                                      bank(2 * s + 1), ALU.mult).then_inc(prod_made, 1)

                def low(i, m=0):
                    s = i % 2
                    dve.wait_ge(prod_made, m * 2 + (b + i + 1))
                    dve.wait_ge(prod_hi, m * 2 + (b + i + 1))
                    dve.tensor_tensor(hlo[:, s, :, :], two(gf[:, s * 512:s * 512 + 512]), hhi[:, s, :, :].bitcast(f32),
                                      ALU.subtract).then_inc(prod_lo, 1)

                split_lo(dve, c0 + AHEAD)
                dve.wait_ge(rs_made, 4 + 3 * L + 2)
                a_part(c0, 0)
                conv(0)
                split_lo(dve, c0 + 1 + AHEAD)
                gated(c0 + 1, 0)
                low(0)
                with dve.Fori(0, (N_FF - 1) // 2) as m:
                    for i in range(1, 3):
                        ca = c0 + 3 * i - 1
                        split_lo(dve, ca + AHEAD, m)
                        a_part(ca, i, m)
                        conv(i, m)
                        split_lo(dve, ca + 1 + AHEAD, m)
                        gated(ca + 1, i, m)
                        split_lo(dve, ca + 2 + AHEAD, m)
                        low(i, m)
                split_lo(dve, c0 + 3 * N_FF - 1 + AHEAD)

            x_low(0, lambda j: pair(hT, j))
            for c in range(AHEAD + 2):
                split_lo(dve, c)
            b4 = yf[:, 1024:2048]
            dve.wait_ge(g_ln, 1)
            dve.wait_ge(par_in, 5 * 16)
            dve.wait_ge(const_in, 16)
            for L in range(DEPTH):
                w = pv[:, PV["attn_w"] + 8 * L:PV["attn_w"] + 8 * L + 8].unsqueeze(2).to_broadcast([128, NT, FOX_H])
                ins = dve.tensor_tensor(wf_sb[:, L, :, :], wf_sb[:, L, :, :], w, ALU.mult)
            ins.then_inc(wf_made, 1)
            for h in range(GLA_H):
                n = own.mark(dve.tensor_scalar(yf[:, h * 256:h * 256 + 256], acc[:, 2 + h, :], par("b_a", h), 0.0,
                                               ALU.add, ALU.min))
            own.need(n)
            own.sync(dve.tensor_tensor(yf[:, 0:1024], yf[:, 0:1024], sqf[:, 0:1024], ALU.subtract))
            split_lo(dve, 2 + AHEAD)
            for h in range(GLA_H):
                s = slice(h * 256, h * 256 + 256)
                last = dve.tensor_tensor_scan(b4[:, s], scanm, yf[:, s], 0.0, ALU.mult, ALU.add)
            last.then_inc(g_cum, 1)
            dve.wait_ge(g_cum, 1)
            b3 = b4.rearrange("p (a c) -> p a c", c=64)
            dve.tensor_tensor(yf[:, 0:1024].rearrange("p (a c) -> p a c", c=64), b3[:, :, 63:64].to_broadcast([128, 16, 64]),
                              b3, ALU.subtract).then_inc(g_cum, 1)
            for c in (3, 4, 5):
                split_lo(dve, c + AHEAD)
            dve.wait_ge(gemm_free, 4)
            dve.wait_ge(g_exp, 1)
            for h in range(GLA_H):
                dve.tensor_tensor(kT[:, 4 + h, :], kT[:, h, :], y[:, h, :], ALU.mult).then_inc(g_kend, 1)
            split_lo(dve, 6 + AHEAD)
            dve.wait_ge(g_exp, 3)
            dve.wait_ge(g_kend, GLA_H)
            own.mark(dve.scalar_tensor_tensor(qf[:, 0:1024], qf[:, 0:1024], GLA_SCALE, sqf[:, 0:1024], ALU.mult, ALU.mult))
            dve.tensor_tensor(kf[:, 0:1024], kf[:, 0:1024], sqf[:, 1024:2048], ALU.mult).then_inc(g_dec, 1)
            for c in range(7, 12):
                split_lo(dve, c + AHEAD)
            for n in range(3):
                dve.wait_ge(g_ud, n + 1)
                for h in range(GLA_H):
                    u = ring[:, h // 2, (h % 2) * 256:(h % 2) * 256 + 256]
                    at = n * 1024 + h * 256
                    if n == 0:
                        ins = dve.tensor_copy(misc[:, at:at + 256], u)
                    else:
                        d = sqf[:, h * 256 + n * 64 + 63:h * 256 + n * 64 + 64]
                        ins = dve.scalar_tensor_tensor(misc[:, at:at + 256], misc[:, at - 1024:at - 768], d, u,
                                                       ALU.mult, ALU.add)
                ins.then_inc(g_st, 1)
                dve.wait_ge(g_st, n + 1)
            for j in range(2):
                dve.wait_ge(g_rs, j + 1)
                for h in (2 * j, 2 * j + 1):
                    own.sync(dve.tensor_tensor(pair(y, h), pair(acc, h), wide(rs[:, h * 256:h * 256 + 256], 2), ALU.mult))
                    for e in range(2):
                        t = 2 * h + e
                        ins = dve.scalar_tensor_tensor(y[:, t, :], y[:, t, :], par("gla_g", e), gT[:, t, :],
                                                       ALU.mult, ALU.mult)
                    ins.then_inc(h_made, 1)
                    x_low(1, lambda i: pair(y, i), [h])
            zero_acc(x_made, 8)

            def after_product(c, n):
                for j in range(4):
                    split_lo(dve, c + j + AHEAD)
                    dve.wait_ge(chunk_used, c + j + 1)
                    residual(j, two(bank(j)))

            def after_mlp(n):
                for j in range(4):
                    acc_ready(ZERO[f"mlp{n}"], C_MLP[n] + 2 * N_UP - 1, j)
                    residual(j, pair(acc, j))

            dve.wait_ge(x_made, 8)
            after_product(C_GLA_O, 0)
            layer_norm(0, 2)
            mlp(0)
            after_mlp(0)
            layer_norm(1, 3)

            ahead(C_SB_IN, 12)
            for h in range(SB_H):
                s = (h % 2) * 384
                dve.wait_ge(s_ln, h + 1)
                if h >= 2:
                    dve.wait_ge(s_lw, h - 1)
                dve.scalar_tensor_tensor(yf[:, s:s + 384], bank(h % 4)[:, 0:384], 0.0, gf[:, s:s + 384], ALU.max,
                                         ALU.add).then_inc(s_sp, 1)
            x_low(4, lambda j: pair(acc, j))
            zero_acc(x_made, 20)
            after_product(C_SB_O, 2)
            layer_norm(2, 5)
            mlp(1)
            after_mlp(1)
            layer_norm(3, None)

            def add_to_h(j, psum):
                dve.tensor_tensor(pair(hT, j), pair(hT, j), psum, ALU.add).then_inc(y_made, 1)

            for L in range(DEPTH):
                X = 6 + 4 * L
                weighted_low(X, "attn_w", 8 * L)
                split_lo(dve, C_IN[L] + AHEAD)
                split_lo(dve, C_IN[L] + 1 + AHEAD)
                dve.wait_ge(rs_made, 4 + 3 * L + 1)
                dve.wait_ge(f_log, L + 1)
                dve.tensor_tensor(cum[:, 1, :], acc[0:FOX_H, 0, :], rs1[0:FOX_H, :], ALU.mult).then_inc(f_logit, 1)

                def scaled(j, dest, scale=1.0):
                    dve.wait_ge(chunk_used, C_IN[L] + j + 1)
                    if j == 12:
                        dve.wait_ge(gemm_free, FREE[f"in{L}"] + 12)
                    dve.scalar_tensor_tensor(dest, two(bank(j % 4)), scale, wide(rs1, 2), ALU.mult,
                                             ALU.mult).then_inc(gemm_free, 1)

                scaled(0, pair(qT, 2))
                dve.wait_ge(f_ln, L + 1)
                own.sync(dve.tensor_scalar(cum[:, 1, :], cum[:, 1, :], fb_sb[:, L:L + 1], 0.0, ALU.add, ALU.min))
                own.sync(dve.tensor_tensor(cum[:, 1, :], cum[:, 1, :], cum[:, 0, :], ALU.subtract))
                own.sync(dve.tensor_tensor_scan(cum[:, 2, :], cst[0:FOX_H, CONST["ones"]:CONST["ones"] + S], cum[:, 1, :],
                                                0.0, ALU.mult, ALU.add))
                dve.scalar_tensor_tensor(y[0:FOX_H, :, :], wide(cum[:, 2, :], FOX_H), -1.0,
                                         ident[0:FOX_H, 0:FOX_H].unsqueeze(2).to_broadcast([FOX_H, FOX_H, S]),
                                         ALU.mult, ALU.mult).then_inc(f_cum, 1)
                scaled(1, pair(qT, 3))
                for j in range(2, 7):
                    split_lo(dve, C_IN[L] + j + AHEAD)
                    if j < 4:
                        scaled(j, pair(kT, j), 0.125)
                    elif j < 6:
                        scaled(j, pair(qT, j - 4), 0.125)
                    else:
                        scaled(j, pair(kT, j - 6))
                dve.wait_ge(r_rot, L + 1)
                for n, t in enumerate((qT, kT)):
                    own.mark(dve.tensor_tensor(sq[:, 0:4, :], t[:, 4:8, :], wide(cosT, 4), ALU.mult))
                    own.sync(dve.tensor_tensor(sq[:, 4:8, :], acc[:, 4 * n:4 * n + 4, :], wide(sinT, 4), ALU.mult))
                    dve.tensor_tensor(t[:, 4:8, :], sq[:, 0:4, :], sq[:, 4:8, :], ALU.add).then_inc(r_rdy, 1)
                    dve.wait_ge(r_rdy, 2 * L + n + 1)
                    split_lo(dve, C_IN[L] + 7 + n + AHEAD)
                    if n == 0:
                        scaled(7, pair(kT, 1))
                dve.wait_ge(p_hi, L + 1)
                dve.tensor_tensor(hlo[:, 2, :, :], two(gf[:, 1024:1536]), hhi[:, 2, :, :].bitcast(f32),
                                  ALU.subtract).then_inc(p_lo, 1)
                for j in range(9, 14):
                    split_lo(dve, C_IN[L] + j + AHEAD)
                    if j >= 12:
                        scaled(j, pair(gT, j - 12))
                for i in range(FOX_H + 1):
                    if i < FOX_H:
                        h, st = i, stat[:, i % 4, :]
                        b, P = bank(h % 2), sqf[:, (h % 3) * 384:(h % 3) * 384 + 384]
                        dve.wait_ge(f_z, FOX_H * L + h + 1)
                        if h >= 3:
                            dve.wait_ge(f_td, FOX_H * L + h - 2)
                        own.mark(dve.tensor_tensor_reduce(P[:, 0:128], b[:, 0:128], maskadd[:, 0:128], 1.0, -3.0e38,
                                                          ALU.add, ALU.max, st[:, 0:1]))
                        own.sync(dve.tensor_tensor_reduce(P[:, 128:384], b[:, 128:384], maskadd[:, 128:384], 1.0, -3.0e38,
                                                          ALU.add, ALU.max, st[:, 1:2]))
                        dve.tensor_scalar(st[:, 2:4], st[:, 0:2], -1.0, None, ALU.mult).then_inc(f_mx, 1)
                    if i >= 1:
                        h, st = i - 1, stat[:, (i - 1) % 4, :]
                        P = sqf[:, (h % 3) * 384:(h % 3) * 384 + 384]
                        dve.wait_ge(f_e, FOX_H * L + h + 1)
                        own.sync(dve.reciprocal(st[:, 6:8], st[:, 4:6]))
                        dve.tensor_scalar(P[:, 0:128], P[:, 0:128], st[:, 6:7], None, ALU.mult)
                        dve.tensor_scalar(P[:, 128:384], P[:, 128:384], st[:, 7:8], None, ALU.mult).then_inc(f_p, 1)
                dve.wait_ge(dec_in, 16)
                x_low(X + 1, lambda j: pair(acc, j), range(2))
                for h in range(RET_H):
                    s = (h % 2) * 384
                    dve.wait_ge(r_s, RET_H * L + h + 1)
                    if h >= 2:
                        dve.wait_ge(r_o, RET_H * L + h - 1)
                    dve.tensor_tensor(yf[:, s:s + 256], bank(h % 2)[:, 0:256], dec[:, h, :], ALU.mult)
                    dve.tensor_tensor(yf[:, s + 256:s + 384], bank(h % 2)[:, 256:384], dec[:, h, 0:128],
                                      ALU.mult).then_inc(r_m, 1)
                for j in range(2):
                    dve.wait_ge(r_mean, 2 * L + j + 1)
                    dve.scalar_tensor_tensor(pair(y, 2 + j), two(bank(j)), -1 / 64, pair(y, 2 + j), ALU.mult,
                                             ALU.add).then_inc(r_yc, 1)
                dve.wait_ge(r_yc, 2 * L + 2)
                for j in range(2):
                    r, t = rs[:, j * 512:j * 512 + 512], yf[:, 1024 + j * 512:1536 + j * 512]
                    dve.wait_ge(r_rs, 2 * L + j + 1)
                    own.sync(dve.tensor_tensor(t, t, r, ALU.mult))
                    dve.wait_ge(silu_made, 2 * L + j + 1)
                    dve.tensor_tensor(t, t, gf[:, j * 512:j * 512 + 512], ALU.mult).then_inc(h_made, 1)
                    x_low(X + 1, lambda i: pair(y, i), [2 + j])
                zero_acc(x_made, 4 * (X + 1) + 4)
                for j in range(4):
                    split_lo(dve, C_OUT[L] + j + AHEAD)
                    dve.wait_ge(chunk_used, C_OUT[L] + j + 1)
                    add_to_h(j, two(bank(j)))
                weighted_low(X + 2, "ffn_w", 8 * L)
                ffn(L)
                for j in range(4):
                    acc_ready(ZERO[f"ffn{L}"], C_FFN[L] + 3 * N_FF - 1, j)
                    add_to_h(j, pair(acc, j))
                weighted_low(X + 3, "ple_w", 8 * L)
                split_lo(dve, C_PROJ[L] + AHEAD)
                for j in range(4):
                    split_lo(dve, C_GATE[L] + j + AHEAD)
                    if j == 0:
                        dve.wait_ge(rs_made, 4 + 3 * L + 3)
                    dve.wait_ge(chunk_used, C_GATE[L] + j + 1)
                    dve.tensor_tensor(pair(kT, j), two(bank(j)), wide(rs1, 2), ALU.mult).then_inc(z_scaled, 1)
                    dve.wait_ge(sig_made, 4 * L + j + 1)
                    own.sync(dve.tensor_tensor(pair(kT, j), pair(kT, j), pair(acc, j), ALU.mult))
                    add_to_h(j, pair(kT, j))
            final_norm()

        @block.gpsimd
        def _(pool):
            own = Own(pool, pool_own)
            for t in range(2):
                pool.wait_ge(g_attc, t + 1)
                a = sqf[:, 1024 + t * 512:1536 + t * 512]
                own.sync(pool.affine_select(out=a, in_=a, compare_op=ALU.is_ge, fill=0.0, base=0,
                                            pattern=[[0, 4], [1, 128]], channel_multiplier=-1))
                b = a.rearrange("p (h c) -> p h c", h=4)[:, :, 64:128]
                pool.affine_select(out=b, in_=b, compare_op=ALU.is_ge, fill=0.0, base=-64,
                                   pattern=[[0, 4], [0, 64]], channel_multiplier=1).then_inc(g_attm, 1)

            def strict(buf):
                d = buf.rearrange("p (b s) -> p b s", b=3)[:, 0:3:2, :]
                return pool.affine_select(out=d, in_=d, compare_op=ALU.is_gt, fill=0.0, base=0,
                                          pattern=[[0, 2], [1, 128]], channel_multiplier=-1)

            for i in range(SB_H + 1):
                if i < SB_H:
                    pool.wait_ge(s_sp, i + 1)
                    strict(yf[:, (i % 2) * 384:(i % 2) * 384 + 384]).then_inc(s_L, 1)
                if i >= 1:
                    h = i - 1
                    pool.wait_ge(s_w, h + 1)
                    strict(sqf[:, (h % 3) * 384:(h % 3) * 384 + 384]).then_inc(s_wm, 1)


def _tiles(a, n=None):
    return np.ascontiguousarray(a.reshape(-1, 128, a.shape[-1]).transpose(1, 0, 2))


def _cols(w):
    n = w.shape[1] // 256
    return w.reshape(NT, 128, n, 256).transpose(2, 1, 0, 3).reshape(n, 128, CW)


def _rows(w):
    n = w.shape[0] // 256
    return w.reshape(n, 2, 128, D).transpose(0, 2, 1, 3).reshape(n, 128, CW)


def _stream(i):
    w = i["gla_w_in"][0]
    parts = [_cols(w[:, 0:3072]), _cols(i["gla_w_o"][0])]

    def mlp(n):
        up, down = _cols(i["mlp_w_up"][n]), _rows(i["mlp_w_down"][n])
        parts.append(up[0:1])
        for s in range(1, N_UP):
            parts.extend([up[s:s + 1], down[s - 1:s]])
        parts.append(down[N_UP - 1:])

    mlp(0)
    parts.extend([_cols(i["kv_w"]), _cols(i["sb_w_q"][0]), _cols(i["sb_w_o"][0])])
    mlp(1)
    for n in range(DEPTH):
        w = i["w_in_2"][n]
        fq, fk, fv, rq, rk, rv, rg = (w[:, a:a + 512] for a in (0, 512, 1024, 1544, 2056, 2568, 3080))
        parts.extend(_cols(p) for p in (rq, rk, fq, fk, fv, rv, rg))
        parts.append(_cols(i["w_out_2"][n]))
        up, down = i["w_up_2"][n], _rows(i["w_down_2"][n])
        a, g = _cols(up[:, :FF2]), _cols(up[:, FF2:])
        parts.extend([a[0:1], g[0:1]])
        for s in range(1, N_FF):
            parts.extend([a[s:s + 1], g[s:s + 1], down[s - 1:s]])
        parts.append(down[N_FF - 1:])
        parts.extend([_rows(i["w_ple_proj_2"][n]), _cols(i["w_ple_gate_2"][n])])
    return np.concatenate(parts, axis=0)


def _params(i):
    def c(a):
        return np.asarray(a).reshape(-1, 128).T

    return np.ascontiguousarray(np.concatenate([
        c(i["ln_g"]), c(i["ln_b"]), c(i["gla_b_a"]), c(i["gla_norm_g"]), c(i["attn_norm_w_2"]), c(i["ffn_norm_w_2"]),
        c(i["ple_norm_w_2"]), c(i["final_norm_w_2"]), c(i["conv_w_2"]), c(i["conv_b_2"])], axis=1))


def _constants():
    p, f = np.arange(128)[:, None], np.arange(128)[None, :]
    causal = np.where(f > p, -3.0e38, 0.0)
    d = p % 64
    source = np.where(d < 32, p + 32, p - 32)
    perm = np.where(f == source, np.where(d < 32, -1.0, 1.0), 0.0).T
    inv = (np.float32(10000.0) ** (-np.arange(0, 64, 2, dtype=np.float32) / np.float32(64))).astype(np.float32)
    ang = (np.arange(S, dtype=np.float32)[None, :] * inv[np.arange(128) % 32][:, None]).astype(np.float32)
    scan = np.where(np.arange(S) % 64 == 0, 0.0, 1.0)[None, :] * np.ones((128, 1))
    parts = dict(ident=p == f, ones=np.ones((128, 256)), blk=p // 64 == f // 64, tri=-(p >= f).astype(float),
                 neg=-np.ones((128, 128)), perm=perm, scan=scan,
                 mask=np.concatenate([causal, np.zeros((128, 128)), causal], axis=1), cos=np.cos(ang), sin=np.sin(ang),
                 eps=np.tile([LN_EPS, RMS_EPS], (128, 1)))
    assert list(parts) == list(CONST)
    return np.concatenate([np.asarray(a, np.float32) for a in parts.values()], axis=1)


def _decays():
    gamma = 1.0 - np.exp2(-5.0 - np.arange(RET_H))
    i, j = np.arange(S)[None, None, :], np.arange(128)[:, None, None]
    lg = np.log1p(-np.exp2(-5.0 - np.arange(RET_H)))[None, :, None]
    t = np.where(i >= j, np.exp(lg * np.maximum(i - j, 0)), 0.0)
    return t.reshape(128, RET_H * S).astype(np.float32)


def kernel(**inputs):
    import concourse.bacc as bacc
    from concourse.bass_utils import run_bass_kernel_spmd

    i = {k: np.asarray(a) for k, a in inputs.items()}
    arrays = dict(
        xT=_tiles(i["x"][0].T),
        wstream=_stream(i),
        wa1=_tiles(i["gla_w_in"][0][:, 3072:3088]),
        wa2=np.ascontiguousarray(i["gla_w_a2"][0]),
        wf=np.ascontiguousarray(np.stack([_tiles(i["w_in_2"][n][:, 1536:1544]) for n in range(DEPTH)], axis=1)),
        fbias=np.ascontiguousarray(i["forget_bias_2"].T),
        pT=np.stack([_tiles(i["p_2"][n, 0].T) for n in range(DEPTH)]),
        params=_params(i),
        consts=_constants(),
        decay=_decays(),
    )
    nc = bacc.Bacc("TRN2", target_bir_lowering=False, num_devices=1)
    aps = {n: nc.dram_tensor(n, a.shape, mybir.dt.from_np(a.dtype), kind="ExternalInput").ap() for n, a in arrays.items()}
    aps["out"] = nc.dram_tensor("out", (128, NT, S), mybir.dt.float32, kind="ExternalOutput").ap()
    build_program(nc, **aps)
    got = run_bass_kernel_spmd(nc, [arrays], core_ids=[0]).results[0]["out"]
    return np.ascontiguousarray(got.transpose(2, 1, 0).reshape(1, S, D))
```

```python
import concourse.bass as bass
from concourse import mybir
from contextlib import ExitStack
import numpy as np

S = 256
D = 1024
NT = D // 128
FF = 4096
FF2 = 2816
DEPTH = 2
CW = 2048
N_UP = FF // 256
N_FF = FF2 // 256
FT = FF2 // 128
ALPHA = (2.0 * DEPTH) ** 0.25
LN_EPS, RMS_EPS = 1e-5, 1e-6
GN_EPS = LN_EPS
GLA_H, SB_H, FOX_H, RET_H = 4, 16, 8, 8
GLA_SCALE = 128 ** -0.5

C_GLA_IN = 0
C_GLA_O = C_GLA_IN + 12
C_MLP = [C_GLA_O + 4, 0]
C_SB_IN = C_MLP[0] + 2 * N_UP
C_SB_O = C_SB_IN + 12
C_MLP[1] = C_SB_O + 4
C_B2 = C_MLP[1] + 2 * N_UP
PER_B2 = 14 + 4 + 3 * N_FF + 1 + 4
C_IN = [C_B2 + PER_B2 * n for n in range(DEPTH)]
C_OUT = [c + 14 for c in C_IN]
C_FFN = [c + 18 for c in C_IN]
C_PROJ = [c + 3 * N_FF for c in C_FFN]
C_GATE = [c + 1 for c in C_PROJ]
N_CHUNKS = C_B2 + PER_B2 * DEPTH

RAW, SPLIT = 6, 3
AHEAD = 2

FREE = dict(gla_in=0, mlp0=12, sb_in=12 + N_UP, mlp1=24 + N_UP, in0=24 + 2 * N_UP, in1=38 + 2 * N_UP)
ZERO = dict(mlp0=0, mlp1=1, ffn0=2, ffn1=3)
H_OF = {1: 0, 2: 4, 3: 8, 5: 12, 7: 16, 11: 18}

PV = dict(ln_g=0, ln_b=32, b_a=64, gla_g=68, attn_w=70, ffn_w=86, ple_w=102, fin_w=118, conv_w=126,
          conv_b=126 + 6 * FT)
NPV = 126 + 8 * FT
CONST = dict(ident=0, ones=128, blk=384, tri=512, neg=640, perm=768, scan=896, mask=1152, cos=1536, sin=1792, eps=2048)
NCONST = 2050


def build_program(nc, xT, wstream, wa1, wa2, wf, fbias, pT, params, consts, decay, out):
    f32, f32r = mybir.dt.float32, mybir.dt.float32r
    ALU, ACT = mybir.AluOpType, mybir.ActivationFunctionType
    ctx = ExitStack()
    with ctx:
        def sb(name, shape, dt=f32):
            return ctx.enter_context(nc.sbuf_tensor(name, shape, dt))

        def sem(name):
            return ctx.enter_context(nc.semaphore(name))

        raw = sb("raw", [128, RAW, CW])
        whi = sb("whi", [128, SPLIT, CW], f32r)
        wlo = sb("wlo", [128, SPLIT, CW], f32r)
        hT = sb("hT", [128, NT, S])
        xhi = sb("xhi", [128, NT, S], f32r)
        xlo = sb("xlo", [128, NT, S], f32r)
        y = sb("y", [128, NT, S])
        sq = sb("sq", [128, NT, S])
        qT = sb("qT", [128, NT, S])
        kT = sb("kT", [128, NT, S])
        v = sb("v", [128, 2, D])
        gT = sb("gT", [128, NT, S])
        hhi = sb("hhi", [128, 3, 2, S], f32r)
        hlo = sb("hlo", [128, 3, 2, S], f32r)
        misc = sb("misc", [128, 3072])
        cst = sb("cst", [128, NCONST])
        pv = sb("pv", [128, NPV])
        wa1_sb = sb("wa1_sb", [128, NT, 16])
        wa2_sb = sb("wa2_sb", [16, 512])
        wf_sb = sb("wf_sb", [128, DEPTH, NT, FOX_H])
        fb_sb = sb("fb_sb", [FOX_H, DEPTH])
        low_rank = sb("low_rank", [16, 3, S])
        a1_sb, cum = low_rank[:, 0, :], low_rank[0:FOX_H, :, :]
        r_col = sb("r_col", [128, 2])
        stat = sb("stat", [128, 4, 8])

        def const(name, n):
            return cst[:, CONST[name]:CONST[name] + n]

        def par(name, i):
            return pv[:, PV[name] + i:PV[name] + i + 1]

        ident, blk, tri, neg, perm = (const(n, 128) for n in ("ident", "blk", "tri", "neg", "perm"))
        ones = const("ones", 128)
        cosT, sinT, scanm, maskadd = const("cos", S), const("sin", S), const("scan", S), const("mask", 384)

        eps_col = {LN_EPS: const("eps", 1), RMS_EPS: const("eps", 2)[:, 1:2]}

        def flat(t):
            return t[:, :, :].rearrange("p t s -> p (t s)")

        yf, sqf, qf, kf, gf = (flat(t) for t in (y, sq, qT, kT, gT))
        rs = misc[:, 2048:3072]
        rs1 = misc[:, 2048:2304]
        dec = misc[:, 0:2048].rearrange("p (h s) -> p h s", h=RET_H)

        def wide(ap, n):
            return ap.unsqueeze(1).to_broadcast([ap.shape[0], n, ap.shape[1]])

        def pair(t, j):
            return t[:, 2 * j:2 * j + 2, :]

        def two(ap):
            return ap.rearrange("p (t s) -> p t s", t=2)

        acc = ctx.enter_context(nc.psum_tensor("acc", [128, NT, S], f32))
        ring = ctx.enter_context(nc.psum_tensor("ring", [128, 4, 512], f32))

        def bank(i):
            return ring[:, i, :]

        def acc_bank(i):
            return acc[:, 2 * i:2 * i + 2, :].rearrange("p t s -> p (t s)")

        def in_bank(j):
            return j if j < 4 else j % 2

        raw_in = [sem(f"raw_in{i}") for i in range(RAW)]
        hi_made, lo_made = sem("hi_made"), sem("lo_made")
        chunk_used = sem("chunk_used")
        gemm_free = sem("gemm_free")
        const_in, x_in, par_in, dec_in, p_in = (sem(n) for n in ("const_in", "x_in", "par_in", "dec_in", "p_in"))
        out_made, out_in = sem("out_made"), sem("out_in")
        acc_zero, acc_done, out_done = sem("acc_zero"), sem("acc_done"), sem("out_done")
        xh_made, x_made, h_made = sem("xh_made"), sem("x_made"), sem("h_made")
        y_made, mean_done, yc_made = sem("y_made"), sem("mean_done"), sem("yc_made")
        sq_made, var_done, rs_made = (sem(n) for n in ("sq_made", "var_done", "rs_made"))
        hid_sq, hid_hi, hid_lo = sem("hid_sq"), sem("hid_hi"), sem("hid_lo")
        a_copied, conv_step, conv_made, gelu_made = (sem(n) for n in ("a_copied", "conv_step", "conv_made", "gelu_made"))
        prod_made, prod_hi, prod_lo = sem("prod_made"), sem("prod_hi"), sem("prod_lo")
        p_hi, p_lo, sig_made = sem("p_hi"), sem("p_lo"), sem("sig_made")
        wf_made, r_col_done, r_col_copied = sem("wf_made"), sem("r_col_done"), sem("r_col_copied")
        silu_made = sem("silu_made")
        z_scaled, gelu_scaled = sem("z_scaled"), sem("gelu_scaled")
        dve_own, act_own, pool_own = sem("dve_own"), sem("act_own"), sem("pool_own")
        (a1_done, a1_copied, gate_done, g_ln, g_cum, g_exp, g_kend, g_dec, g_attd, g_attc, g_attm, g_ktd, g_ktc,
         g_ud, g_st, g_od, g_sq, g_var, g_rs) = (sem("gla_" + n) for n in (
             "a1_done", "a1_copied", "gate_done", "ln", "cum", "exp", "kend", "dec", "attd", "attc", "attm",
             "ktd", "ktc", "ud", "st", "od", "sq", "var", "rs"))
        s_z, s_ln, s_sp, s_L, s_lw, s_w, s_wm, s_o = (sem("sb_" + n) for n in ("z", "ln", "sp", "L", "lw", "w", "wm", "o"))
        f_log, f_logit, f_ln, f_cum, f_z, f_mx, f_e, f_p, f_td, f_tc, f_o = (
            sem("fox_" + n) for n in ("log", "logit", "lnf", "cum", "z", "mx", "e", "p", "td", "tc", "o"))
        r_rot, r_rdy, r_s, r_m, r_o, r_c, r_mean, r_yc, r_sq, r_var, r_rs = (
            sem("ret_" + n) for n in ("rot", "rdy", "s", "m", "o", "c", "mean", "yc", "sq", "var", "rs"))

        class Own:

            def __init__(self, eng, s):
                self.eng, self.s, self.n = eng, s, 0

            def mark(self, ins):
                self.n += 1
                ins.then_inc(self.s, 1)
                return self.n

            def need(self, n):
                self.eng.wait_ge(self.s, n)

            def sync(self, ins):
                self.need(self.mark(ins))

        block = ctx.enter_context(nc.Block())

        @block.sync
        def _(sp):
            sp.dma_start(hT[:, :, :], xT).then_inc(x_in, 16)
            for c in range(RAW):
                sp.dma_start(raw[:, c, :], wstream[c]).then_inc(raw_in[c], 16)
            with sp.Fori(1, N_CHUNKS // RAW) as m:
                for j in range(RAW):
                    sp.wait_ge(lo_made, m * RAW + (j + 1 - RAW))
                    sp.dma_start(raw[:, j, :], wstream[m * RAW + j]).then_inc(raw_in[j], 16)
            for c in range(N_CHUNKS // RAW * RAW, N_CHUNKS):
                sp.wait_ge(lo_made, c + 1 - RAW)
                sp.dma_start(raw[:, c % RAW, :], wstream[c]).then_inc(raw_in[c % RAW], 16)
            for j in range(4):
                sp.wait_ge(out_made, j + 1)
                sp.dma_start(out[:, 2 * j:2 * j + 2, :], pair(y, j)).then_inc(out_in, 16)
            sp.wait_ge(out_in, 4 * 16)

        def split_hi(act, c, m=0):
            if c >= N_CHUNKS:
                return
            act.wait_ge(raw_in[c % RAW], m * 16 + 16 * (c // RAW + 1))
            if c >= SPLIT:
                act.wait_ge(chunk_used, m * RAW + (c - SPLIT + 1))
            act.copy(whi[:, c % SPLIT, :], raw[:, c % RAW, :]).then_inc(hi_made, 1)

        def split_lo(dve, c, m=0):
            if c >= N_CHUNKS:
                return
            dve.wait_ge(hi_made, m * RAW + (c + 1))
            if c >= SPLIT:
                dve.wait_ge(chunk_used, m * RAW + (c - SPLIT + 1))
            dve.tensor_tensor(wlo[:, c % SPLIT, :], raw[:, c % RAW, :], whi[:, c % SPLIT, :].bitcast(f32),
                              ALU.subtract).then_inc(lo_made, 1)

        @block.tensor
        def _(pe):
            def three(o, l1, l2, r1, r2, start, stop, **kw):
                pe.matmul(o, l1, r1, start=start, stop=False, **kw)
                pe.matmul(o, l1, r2, start=False, stop=False, **kw)
                return pe.matmul(o, l2, r1, start=False, stop=stop, **kw)

            def gemm(c, b, x_need=None, tokens_out=False, m=0):
                pe.wait_ge(lo_made, m * RAW + (c + 1))
                wh, wl = whi[:, c % SPLIT, :], wlo[:, c % SPLIT, :]
                outs = [bank(b)[:, t * 256:t * 256 + 256] for t in range(2)]
                if x_need is not None:
                    for k in range(NT):
                        if k % 2 == 0:
                            pe.wait_ge(x_made, 4 * x_need + k // 2 + 1)
                        for t in range(2):
                            w = slice(k * 256 + t * 128, k * 256 + t * 128 + 128)
                            mm = three(outs[t], wh[:, w], wl[:, w], xhi[:, k, :], xlo[:, k, :], k == 0 and t == 0,
                                       k == NT - 1, skip_group_check=True)
                    mm.then_inc(chunk_used, 1)
                    return
                for t in range(2):
                    for k in range(NT):
                        if tokens_out:
                            tok, w = slice(t * 128, t * 128 + 128), slice(k * 256, k * 256 + 256)
                            mm = three(outs[t], xhi[:, k, tok], xlo[:, k, tok], wh[:, w], wl[:, w], k == 0, k == NT - 1)
                        else:
                            w = slice(k * 256 + t * 128, k * 256 + t * 128 + 128)
                            mm = three(outs[t], wh[:, w], wl[:, w], xhi[:, k, :], xlo[:, k, :], k == 0, k == NT - 1)
                mm.then_inc(chunk_used, 1)

            def down(c, s, m=0, last=False):
                pe.wait_ge(lo_made, m * RAW + (c + 1))
                for k in range(2):
                    for t in range(NT):
                        w = slice(k * D + t * 128, k * D + t * 128 + 128)
                        mm = three(acc[:, t, :], whi[:, c % SPLIT, w], wlo[:, c % SPLIT, w], hhi[:, s, k, :],
                                   hlo[:, s, k, :], False, False, skip_group_check=True)
                        if last and k == 1 and t % 2 and t < NT - 1:
                            mm.then_inc(acc_done, 1)
                mm.then_inc(chunk_used, 1)

            def sums(src, made, base, o, done):
                for t in range(NT):
                    if t % 2 == 0:
                        pe.wait_ge(made, base + t // 2 + 1)
                    mm = pe.matmul(o, ones, src[:, t, :], start=(t == 0), stop=(t == NT - 1))
                mm.then_inc(done, 1)

            def layer_norm(n):
                sums(y, y_made, 4 * n, bank(0)[:, 0:S], mean_done)
                sums(sq, sq_made, 4 * n, bank(1)[:, 0:S], var_done)

            def squares_sum(n, o):
                sums(sq, sq_made, 4 * (4 + n), o, var_done)

            def ple_projection(c, L):
                pe.wait_ge(lo_made, c + 1)
                pe.wait_ge(p_lo, L + 1)
                for j in range(4):
                    pe.wait_ge(y_made, 4 * (6 + 3 * L) + j + 1)
                    for k in range(2):
                        for t in (2 * j, 2 * j + 1):
                            w = slice(k * D + t * 128, k * D + t * 128 + 128)
                            mm = three(acc[:, t, :], whi[:, c % SPLIT, w], wlo[:, c % SPLIT, w], hhi[:, 2, k, :],
                                       hlo[:, 2, k, :], k == 0 and t % 2 == 0, k == 1, skip_group_check=True)
                mm.then_inc(chunk_used, 1)

            def product(c, x_need):
                for j in range(4):
                    gemm(c + j, j, x_need if j == 0 else None)

            def wide_product(c, n, free, x_need, tokens, between):
                for j in range(n):
                    if j >= 4:
                        pe.wait_ge(gemm_free, free + j - 3)
                    gemm(c + j, j % 4, x_need if j == 0 else None, j in tokens)
                    if j in between:
                        between[j]()
                pe.wait_ge(gemm_free, free + n)

            def mlp(n, x_need):
                c0, free, h0 = C_MLP[n], FREE[f"mlp{n}"], N_UP * n
                gemm(c0, 0, x_need)
                pe.wait_ge(acc_zero, ZERO[f"mlp{n}"] + 1)
                with pe.Fori(0, (N_UP - 1) // 3) as m:
                    for i in range(1, 4):
                        cu = c0 + 2 * i - 1
                        pe.wait_ge(gemm_free, m * 3 + (free + i - 2))
                        gemm(cu, i % 3, m=m)
                        pe.wait_ge(hid_lo, m * 3 + (h0 + i))
                        down(cu + 1, (i - 1) % 3, m=m)
                pe.wait_ge(hid_lo, h0 + N_UP)
                down(c0 + 2 * N_UP - 1, (N_UP - 1) % 3, last=True)

            def ffn(L, x_need):
                c0, b = C_FFN[L], N_FF * L
                gemm(c0, 0, x_need)
                squares_sum(3 * L + 1, bank(3)[:, 0:S])
                gemm(c0 + 1, 1)
                pe.wait_ge(acc_zero, ZERO[f"ffn{L}"] + 1)
                pe.wait_ge(rs_made, 4 + 3 * L + 2)
                with pe.Fori(0, (N_FF - 1) // 2) as m:
                    for i in range(1, 3):
                        ca = c0 + 3 * i - 1
                        pe.wait_ge(a_copied, m * 2 + (b + i))
                        gemm(ca, 2 * (i % 2), m=m)
                        pe.wait_ge(prod_made, m * 2 + (b + i))
                        gemm(ca + 1, 2 * (i % 2) + 1, m=m)
                        pe.wait_ge(prod_lo, m * 2 + (b + i))
                        down(ca + 2, (i - 1) % 2, m=m)
                pe.wait_ge(prod_lo, b + N_FF)
                down(c0 + 3 * N_FF - 1, (N_FF - 1) % 2, last=True)

            def head(h):
                return slice(64 * (h % 2), 64 * (h % 2) + 64)

            def scores(b, l, r):
                pe.matmul(b[:, 0:256], l[:, 0:128], r, start=True, stop=False, skip_group_check=True)
                return pe.matmul(b[:, 256:384], l[:, 128:256], r[:, 128:256], start=False, stop=False,
                                 skip_group_check=True)

            def values(t, h, col, W):
                o = acc[head(h), t, :]
                pe.matmul(o, v[:, 0, col:col + 64], W[:, 0:256], start=True, stop=False, skip_group_check=True)
                return pe.matmul(o[:, 128:256], v[:, 1, col:col + 64], W[:, 256:384], start=False, stop=True,
                                 skip_group_check=True)

            def gate_input():
                pe.wait_ge(x_in, 16)
                pe.wait_ge(par_in, 5 * 16)
                pe.wait_ge(const_in, 16)
                for k in range(NT):
                    mm = pe.matmul(acc[0:16, 0, :], wa1_sb[:, k, :], hT[:, k, :], start=(k == 0), stop=(k == NT - 1))
                mm.then_inc(a1_done, 1)

            def gate_logits():
                pe.wait_ge(a1_copied, 1)
                for h in range(GLA_H):
                    mm = pe.matmul(acc[:, 2 + h, :], wa2_sb[:, h * 128:h * 128 + 128], a1_sb,
                                   start=(h % 2 == 0), stop=True, skip_group_check=True)
                mm.then_inc(gate_done, 1)

            wide_product(C_GLA_IN, 12, FREE["gla_in"], 0, range(4, 8), {0: gate_input, 1: gate_logits})
            for h in range(GLA_H):
                pe.wait_ge(g_kend, h + 1)
                for t in range(2):
                    mm = pe.transpose(ring[:, t, h * 128:h * 128 + 128], kT[:, 4 + h, t * 128:t * 128 + 128], ident)
            mm.then_inc(g_ktd, 1)
            pe.wait_ge(g_dec, 1)
            for t in range(2):
                tok = slice(t * 128, t * 128 + 128)
                for h in range(GLA_H):
                    mm = pe.matmul(ring[:, 2 + t, h * 128:h * 128 + 128], kT[:, h, tok], qT[:, h, tok],
                                   start=True, stop=True)
                mm.then_inc(g_attd, 1)
            pe.wait_ge(g_ktc, 1)
            keT = two(yf[:, 0:1024])
            for n in range(3):
                r = slice(64 * (n % 2), 64 * (n % 2) + 64)
                if n:
                    pe.wait_ge(g_st, n)
                for h in range(GLA_H):
                    mm = pe.matmul(ring[:, h // 2, (h % 2) * 256:(h % 2) * 256 + 256],
                                   keT[r, n // 2, h * 128:h * 128 + 128], v[r, n // 2, h * 256:h * 256 + 256],
                                   start=True, stop=True)
                mm.then_inc(g_ud, 1)
            pe.wait_ge(g_attm, 2)
            pe.wait_ge(g_st, 3)
            attm = two(sqf[:, 1024:2048])
            for h in range(GLA_H):
                for e in range(2):
                    ec = h * 256 + e * 128
                    for t in range(2):
                        pe.matmul(acc[:, 2 * h + e, t * 128:t * 128 + 128], v[:, t, ec:ec + 128],
                                  attm[:, t, h * 128:h * 128 + 128], start=True, stop=False, skip_group_check=True)
                        for n in (2 * t, 2 * t + 1):
                            if n:
                                sc = (n - 1) * 1024 + ec
                                mm = pe.matmul(acc[:, 2 * h + e, n * 64:n * 64 + 64], misc[:, sc:sc + 128],
                                               qT[:, h, n * 64:n * 64 + 64], start=False, stop=True,
                                               skip_group_check=True)
                mm.then_inc(g_od, 1)
            for h in range(GLA_H):
                pe.wait_ge(g_sq, h + 1)
                for e in range(2):
                    mm = pe.matmul(ring[:, 2 + h // 2, (h % 2) * 256:(h % 2) * 256 + 256], ones, sq[:, 2 * h + e, :],
                                   start=(e == 0), stop=(e == 1))
                if h % 2:
                    mm.then_inc(g_var, 1)
            product(C_GLA_O, 1)
            layer_norm(0)
            mlp(0, 2)
            layer_norm(1)

            wide_product(C_SB_IN, 12, FREE["sb_in"], 3, range(4, 8), {})
            for i in range(SB_H + 4):
                if i < SB_H:
                    h = i
                    if h >= 4:
                        pe.wait_ge(s_w, h - 3)
                    scores(bank(h % 4), kT[head(h), h // 2, :], qT[head(h), h // 2, :]).then_inc(s_z, 1)
                if 0 <= i - 2 < SB_H:
                    h = i - 2
                    b, L = bank(h % 4), yf[:, (h % 2) * 384:(h % 2) * 384 + 384]
                    pe.wait_ge(s_L, h + 1)
                    pe.matmul(b[:, 0:256], tri, L[:, 0:256], start=False, stop=False, skip_group_check=True)
                    pe.matmul(b[:, 128:256], neg, L[:, 256:384], start=False, stop=False, skip_group_check=True)
                    pe.matmul(b[:, 256:384], tri, L[:, 256:384], start=False, stop=True,
                              skip_group_check=True).then_inc(s_lw, 1)
                if 0 <= i - 4:
                    h = i - 4
                    pe.wait_ge(s_wm, h + 1)
                    values(h // 2, h, h * 64, sqf[:, (h % 3) * 384:(h % 3) * 384 + 384]).then_inc(s_o, 1)
            product(C_SB_O, 4)
            layer_norm(2)
            mlp(1, 5)
            layer_norm(3)

            for L in range(DEPTH):
                X = 6 + 4 * L

                def norm_and_forget():
                    squares_sum(3 * L, acc[:, 7, :])
                    if L == 0:
                        pe.wait_ge(wf_made, 1)
                    for k in range(NT):
                        mm = pe.matmul(acc[0:FOX_H, 0, :], wf_sb[:, L, k, :], hT[:, k, :], start=(k == 0),
                                       stop=(k == NT - 1))
                    mm.then_inc(f_log, 1)

                def scale_column():
                    pe.wait_ge(rs_made, 4 + 3 * L + 1)
                    for t in range(2):
                        mm = pe.matmul(acc[:, 4, t:t + 1], rs1[:, t * 128:t * 128 + 128], ident[:, 0:1],
                                       start=(t == 0), stop=True, skip_group_check=True)
                    mm.then_inc(r_col_done, 1)

                def rotate(n):
                    pe.wait_ge(gemm_free, FREE[f"in{L}"] + 8 + 2 * n)
                    if n == 0:
                        pe.wait_ge(r_col_copied, L + 1)
                    else:
                        pe.wait_ge(r_rdy, 2 * L + 1)
                    for t in range(4, NT):
                        mm = pe.matmul(acc[:, t, :], perm, (kT if n else qT)[:, t, :], start=(t % 2 == 0),
                                       stop=True, skip_group_check=True)
                    mm.then_inc(r_rot, 1)

                def fox_step(i):
                    done = FOX_H * L
                    if i < FOX_H:
                        h, b = i, bank(2)
                        if h == 0:
                            pe.wait_ge(f_cum, L + 1)
                            pe.wait_ge(gemm_free, FREE[f"in{L}"] + 4)
                        else:
                            pe.wait_ge(f_mx, done + h)
                        q, k, nc_h = qT[head(h), h // 2, :], kT[head(h), h // 2, :], y[0:FOX_H, h, :]
                        pe.matmul(b[:, 0:128], q[:, 0:128], k[:, 0:128], start=True, stop=False, skip_group_check=True)
                        pe.matmul(b[:, 128:384], q[:, 128:256], k, start=False, stop=False, skip_group_check=True)
                        pe.matmul(b[:, 0:128], ones[0:FOX_H, :], nc_h[:, 0:128], start=False, stop=False,
                                  skip_group_check=True)
                        pe.matmul(b[:, 128:384], ones[0:FOX_H, :], nc_h, start=False, stop=True,
                                  skip_group_check=True).then_inc(f_z, 1)
                    if 0 <= i - 1 < FOX_H:
                        h = i - 1
                        b, P = bank(3), sqf[:, (h % 3) * 384:(h % 3) * 384 + 384]
                        pe.wait_ge(f_p, done + h + 1)
                        if h >= 1:
                            pe.wait_ge(f_tc, done + h)
                        pe.transpose(b[:, 0:128], P[:, 0:128], ident)
                        pe.transpose(b[:, 128:256], P[:, 128:256], ident)
                        pe.transpose(b[:, 256:384], P[:, 256:384], ident).then_inc(f_td, 1)
                    if 0 <= i - 2:
                        h = i - 2
                        if h == 0:
                            pe.wait_ge(gemm_free, FREE[f"in{L}"] + 6)
                        pe.wait_ge(f_tc, done + h + 1)
                        values(h // 2, h, h * 64,
                               sqf[:, 1152 + (h % 2) * 384:1536 + (h % 2) * 384]).then_inc(f_o, 1)

                for j in range(14):
                    if j >= 4:
                        pe.wait_ge(gemm_free, FREE[f"in{L}"] + (j - 3 if j < 6 else j - 1))
                    gemm(C_IN[L] + j, in_bank(j), X if j == 0 else None, j in (4, 5, 10, 11))
                    if j == 0:
                        norm_and_forget()
                    if j == 2:
                        scale_column()
                    if j >= 4:
                        fox_step(j - 4)
                    if j in (8, 10):
                        rotate((j - 8) // 2)
                for i in range(RET_H + 2):
                    if i < RET_H:
                        h, t = i, 4 + i // 2
                        if h == 0:
                            pe.wait_ge(f_mx, FOX_H * (L + 1))
                            pe.wait_ge(r_rdy, 2 * L + 2)
                        if h == 1:
                            pe.wait_ge(f_tc, FOX_H * (L + 1))
                        if h == 2:
                            pe.wait_ge(gemm_free, FREE[f"in{L}"] + 14)
                        if h >= 4:
                            pe.wait_ge(r_m, RET_H * L + h - 3)
                        scores(bank((2 + h) % 4), kT[head(h), t, :], qT[head(h), t, :]).then_inc(r_s, 1)
                    if i >= 2:
                        h = i - 2
                        pe.wait_ge(r_m, RET_H * L + h + 1)
                        values(4 + h // 2, h, 512 + h * 64,
                               sqf[:, (h % 3) * 384:(h % 3) * 384 + 384]).then_inc(r_o, 1)
                for j in range(2):
                    pe.wait_ge(r_c, 2 * L + j + 1)
                    pe.matmul(acc_bank(2 + j), blk, yf[:, 1024 + j * 512:1536 + j * 512], start=True,
                              stop=True).then_inc(r_mean, 1)
                for j in range(4):
                    c = C_OUT[L] + j
                    pe.wait_ge(lo_made, c + 1)
                    pe.wait_ge(x_made, 4 * (X + 1) + j + 1)
                    for k in range(2):
                        for t in range(NT):
                            w = slice(k * D + t * 128, k * D + t * 128 + 128)
                            mm = three(bank(t // 2)[:, (t % 2) * 256:(t % 2) * 256 + 256], whi[:, c % SPLIT, w],
                                       wlo[:, c % SPLIT, w], xhi[:, 2 * j + k, :], xlo[:, 2 * j + k, :],
                                       j == 0 and k == 0 and t % 2 == 0, j == 3 and k == 1, skip_group_check=True)
                            if j == 3 and k == 1 and t % 2 and t < NT - 1:
                                mm.then_inc(out_done, 1)
                    mm.then_inc(chunk_used, 1)
                    if j == 0:
                        for e in range(2):
                            pe.wait_ge(r_sq, 2 * L + e + 1)
                            pe.matmul(acc_bank(2 + e), blk, sqf[:, e * 512:e * 512 + 512], start=True,
                                      stop=True).then_inc(r_var, 1)
                ffn(L, X + 2)
                ple_projection(C_PROJ[L], L)
                for j in range(4):
                    if j == 3:
                        pe.wait_ge(rs_made, 4 + 3 * L + 3)
                    gemm(C_GATE[L] + j, j, X + 3 if j == 0 else None)
                    if j == 0:
                        squares_sum(3 * L + 2, bank(3)[:, 0:S])
            squares_sum(6, bank(0)[:, 0:S])

        @block.scalar
        def _(act):
            own = Own(act, act_own)
            for dst, src in ((pv[:, :], params), (wa1_sb[:, :, :], wa1), (wa2_sb[:, :], wa2), (wf_sb[:, :, :, :], wf),
                             (fb_sb[:, :], fbias)):
                act.dma_start(dst, src).then_inc(par_in, 16)
            act.dma_start(cst[:, :], consts).then_inc(const_in, 16)

            def x_high(X, src, waits):
                for j in range(4):
                    act.wait_ge(*waits(j))
                    act.copy(pair(xhi, j), src(j)).then_inc(xh_made, 1)

            def from_h(X):
                return lambda j: (h_made, H_OF[X] + j + 1)

            def squares(n, src, made, base):
                for j in range(4):
                    act.wait_ge(made, base + j + 1)
                    act.activation(pair(sq, j), pair(src, j), ACT.Square).then_inc(sq_made, 1)

            def power(r, psum, scale, eps):
                own.sync(act.activation(r, psum, ACT.Ln, bias=eps_col[eps], scale=scale))
                return act.activation(r, r, ACT.Exp, scale=-0.5)

            def inverse_root(n, psum, eps):
                act.wait_ge(var_done, n + 1)
                power(rs1, psum, 1 / D, eps).then_inc(rs_made, 1)

            def ln_part(n):
                squares(n, y, yc_made, 4 * n)
                inverse_root(n, bank(1)[:, 0:S], LN_EPS)

            def weighted_high(n, w, i0, j):
                act.wait_ge(y_made, 4 * (4 + n) + j + 1)
                for t in (2 * j, 2 * j + 1):
                    ins = act.activation(xhi[:, t, :], hT[:, t, :], ACT.Copy, scale=par(w, i0 + t))
                ins.then_inc(xh_made, 1)

            def squares_of_h(n):
                squares(4 + n, hT, y_made, 4 * (4 + n))

            def evacuate(c, n, dest, between):
                for j in range(n):
                    split_hi(act, c + j + AHEAD)
                    act.wait_ge(chunk_used, c + j + 1)
                    d, func, scale = dest(j)
                    if func is None:
                        act.copy(d, two(bank(j % 4))).then_inc(gemm_free, 1)
                    else:
                        act.activation(d, two(bank(j % 4)), func, scale=scale).then_inc(gemm_free, 1)
                    if j in between:
                        between[j]()

            def v_part(j):
                return v[:, :, j * 256:j * 256 + 256]

            def ahead(c, n):
                for j in range(n):
                    split_hi(act, c + j + AHEAD)

            def mlp(n):
                c0, free, h0 = C_MLP[n], FREE[f"mlp{n}"], N_UP * n

                def hidden(c, i, m=0):
                    s = i % 3
                    act.wait_ge(chunk_used, m * RAW + (c + 1))
                    act.activation(pair(qT, s), two(bank(s)), ACT.Relu).then_inc(gemm_free, 1)
                    act.wait_ge(gemm_free, m * 3 + (free + i + 1))
                    act.activation(hhi[:, s, :, :], pair(qT, s), ACT.Square).then_inc(hid_hi, 1)

                split_hi(act, c0 + AHEAD)
                hidden(c0, 0)
                with act.Fori(0, (N_UP - 1) // 3) as m:
                    for i in range(1, 4):
                        cu = c0 + 2 * i - 1
                        split_hi(act, cu + AHEAD, m)
                        hidden(cu, i, m)
                        split_hi(act, cu + 1 + AHEAD, m)
                split_hi(act, c0 + 2 * N_UP - 1 + AHEAD)

            def ffn(L):
                c0, b = C_FFN[L], N_FF * L

                def gelu(i, m=0):
                    s = i % 2
                    act.wait_ge(conv_made, m * 2 + (b + i + 1))
                    act.activation(kf[:, 1024 + s * 512:1536 + s * 512], kf[:, s * 512:s * 512 + 512],
                                   ACT.Gelu).then_inc(gelu_made, 1)

                def high(i, m=0):
                    s = i % 2
                    act.wait_ge(prod_made, m * 2 + (b + i + 1))
                    act.copy(hhi[:, s, :, :], two(gf[:, s * 512:s * 512 + 512])).then_inc(prod_hi, 1)

                split_hi(act, c0 + AHEAD)
                inverse_root(4 + 3 * L + 1, bank(3)[:, 0:S], RMS_EPS)
                split_hi(act, c0 + 1 + AHEAD)
                gelu(0)
                high(0)
                with act.Fori(0, (N_FF - 1) // 2) as m:
                    for i in range(1, 3):
                        ca = c0 + 3 * i - 1
                        split_hi(act, ca + AHEAD, m)
                        split_hi(act, ca + 1 + AHEAD, m)
                        gelu(i, m)
                        split_hi(act, ca + 2 + AHEAD, m)
                        high(i, m)
                split_hi(act, c0 + 3 * N_FF - 1 + AHEAD)

            def load_exp_ln():
                act.preload_act_table_set("natural_log_exp_and_others")

            load_exp_ln()
            x_high(0, lambda j: pair(hT, j), lambda j: (x_in, 16))
            for c in range(AHEAD):
                split_hi(act, c)

            def a1_copy():
                act.wait_ge(a1_done, 1)
                act.copy(a1_sb, acc[0:16, 0, :]).then_inc(a1_copied, 1)

            def gate_ln():
                act.wait_ge(gate_done, 1)
                act.wait_ge(par_in, 5 * 16)
                for h in range(GLA_H):
                    n = own.mark(act.activation(sqf[:, h * 256:h * 256 + 256], acc[:, 2 + h, :], ACT.Abs,
                                                bias=par("b_a", h)))
                own.need(n)
                own.sync(act.activation(sqf[:, 0:1024], sqf[:, 0:1024], ACT.Exp, scale=-1.0))
                act.activation(sqf[:, 0:1024], sqf[:, 0:1024], ACT.Ln, bias=1.0).then_inc(g_ln, 1)

            def gate_exp():
                act.wait_ge(g_cum, 2)
                act.activation(yf[:, 0:1024], yf[:, 0:1024], ACT.Exp, scale=1 / 16).then_inc(g_exp, 1)
                act.activation(sqf[:, 0:1024], yf[:, 1024:2048], ACT.Exp, scale=1 / 16).then_inc(g_exp, 1)
                act.activation(sqf[:, 1024:2048], yf[:, 1024:2048], ACT.Exp, scale=-1 / 16).then_inc(g_exp, 1)

            def gla_dest(j):
                if j < 4:
                    return pair(qT if j < 2 else kT, j % 2), None, None
                if j < 8:
                    return v_part(j - 4), None, None
                return pair(gT, j - 8), ACT.Silu, 1.0

            evacuate(C_GLA_IN, 12, gla_dest, {0: a1_copy, 1: gate_ln, 4: gate_exp})
            load_exp_ln()
            act.wait_ge(g_ktd, 1)
            own.mark(act.copy(yf[:, 0:512], ring[:, 0, :]))
            act.copy(yf[:, 512:1024], ring[:, 1, :]).then_inc(g_ktc, 1)
            for t in range(2):
                act.wait_ge(g_attd, t + 1)
                act.copy(sqf[:, 1024 + t * 512:1536 + t * 512], ring[:, 2 + t, :]).then_inc(g_attc, 1)
            for h in range(GLA_H):
                act.wait_ge(g_od, h + 1 if h < 2 else GLA_H)
                act.activation(pair(sq, h), pair(acc, h), ACT.Square).then_inc(g_sq, 1)
            for j in range(2):
                act.wait_ge(g_var, j + 1)
                power(rs[:, j * 512:j * 512 + 512], bank(2 + j), 1 / 256, RMS_EPS).then_inc(g_rs, 1)
            x_high(1, lambda j: pair(y, j), from_h(1))
            ahead(C_GLA_O, 4)
            ln_part(0)
            x_high(2, lambda j: pair(hT, j), from_h(2))
            act.dma_start(misc[:, 0:2048], decay).then_inc(dec_in, 16)
            mlp(0)
            ln_part(1)
            x_high(3, lambda j: pair(hT, j), from_h(3))

            def sb_dest(j):
                if j < 4:
                    return pair(kT, j), None, None
                if j < 8:
                    return v_part(j - 4), None, None
                return pair(qT, j - 8), ACT.Copy, 0.125

            evacuate(C_SB_IN, 12, sb_dest, {})
            for i in range(SB_H + 2):
                if i < SB_H:
                    h = i
                    a, b = gf[:, (h % 2) * 384:(h % 2) * 384 + 384], bank(h % 4)[:, 0:384]
                    act.wait_ge(s_z, h + 1)
                    if h >= 2:
                        act.wait_ge(s_sp, h - 1)
                    own.sync(act.activation(a, b, ACT.Abs))
                    own.sync(act.activation(a, a, ACT.Exp, scale=-1.0))
                    act.activation(a, a, ACT.Ln, bias=1.0).then_inc(s_ln, 1)
                if i >= 2:
                    h = i - 2
                    act.wait_ge(s_lw, h + 1)
                    if h >= 3:
                        act.wait_ge(s_o, h - 2)
                    act.activation(sqf[:, (h % 3) * 384:(h % 3) * 384 + 384], bank(h % 4)[:, 0:384],
                                   ACT.Exp).then_inc(s_w, 1)
            x_high(4, lambda j: pair(acc, j), lambda j: (s_o, 4 * j + 4))
            ahead(C_SB_O, 4)
            ln_part(2)
            x_high(5, lambda j: pair(hT, j), from_h(5))
            mlp(1)
            ln_part(3)

            for L in range(DEPTH):
                X = 6 + 4 * L
                if L:
                    act.wait_ge(p_lo, L)
                act.dma_start(two(gf[:, 1024:1536]), pT[L]).then_inc(p_in, 16)
                if L == 0:
                    for j in range(4):
                        weighted_high(0, "attn_w", 0, j)
                squares_of_h(3 * L)
                split_hi(act, C_IN[L] + AHEAD)
                inverse_root(4 + 3 * L, acc[:, 7, :], RMS_EPS)
                split_hi(act, C_IN[L] + 1 + AHEAD)

                def forget_ln():
                    act.wait_ge(f_logit, L + 1)
                    own.sync(act.activation(cum[:, 0, :], cum[:, 1, :], ACT.Abs, bias=fb_sb[:, L:L + 1]))
                    own.sync(act.activation(cum[:, 0, :], cum[:, 0, :], ACT.Exp, scale=-1.0))
                    act.activation(cum[:, 0, :], cum[:, 0, :], ACT.Ln, bias=1.0).then_inc(f_ln, 1)

                def p_high():
                    act.wait_ge(p_in, 16 * (L + 1))
                    act.copy(hhi[:, 2, :, :], two(gf[:, 1024:1536])).then_inc(p_hi, 1)

                forget_ln()
                split_hi(act, C_IN[L] + 2 + AHEAD)
                act.wait_ge(r_col_done, L + 1)
                act.copy(r_col[:, :], acc[:, 4, 0:2]).then_inc(r_col_copied, 1)
                for j in (3, 4):
                    split_hi(act, C_IN[L] + j + AHEAD)

                def v_evacuate(j, part):
                    act.wait_ge(chunk_used, C_IN[L] + j + 1)
                    act.wait_ge(gemm_free, FREE[f"in{L}"] + j)
                    act.wait_ge(r_col_copied, L + 1)
                    dest, b = v_part(part), bank(in_bank(j))
                    own.mark(act.activation(dest[:, 0, :], b[:, 0:256], ACT.Copy, scale=r_col[:, 0:1]))
                    act.activation(dest[:, 1, :], b[:, 256:512], ACT.Copy, scale=r_col[:, 1:2]).then_inc(gemm_free, 1)

                for j in range(4, 14):
                    i = j - 4
                    if j in (4, 5, 10, 11):
                        v_evacuate(j, j - 4 if j < 6 else j - 8)
                    split_hi(act, C_IN[L] + j + 1 + AHEAD)
                    if 1 <= i <= FOX_H:
                        h = i - 1
                        act.wait_ge(f_td, FOX_H * L + h + 1)
                        if h >= 2:
                            act.wait_ge(f_o, FOX_H * L + h - 1)
                        act.copy(sqf[:, 1152 + (h % 2) * 384:1536 + (h % 2) * 384], bank(3)[:, 0:384]).then_inc(f_tc, 1)
                    if i < FOX_H:
                        h = i
                        P = sqf[:, (h % 3) * 384:(h % 3) * 384 + 384]
                        act.wait_ge(f_mx, FOX_H * L + h + 1)
                        act.activation(P[:, 0:128], P[:, 0:128], ACT.Exp, bias=stat[:, h % 4, 2:3],
                                       accum_out=stat[:, h % 4, 4:5])
                        act.activation(P[:, 128:384], P[:, 128:384], ACT.Exp, bias=stat[:, h % 4, 3:4],
                                       accum_out=stat[:, h % 4, 5:6]).then_inc(f_e, 1)
                    if j == 9:
                        p_high()
                    if j >= 12:
                        act.wait_ge(gemm_free, FREE[f"in{L}"] + j + 1)
                        act.activation(pair(gT, j - 12), pair(gT, j - 12), ACT.Silu).then_inc(silu_made, 1)
                load_exp_ln()
                act.wait_ge(chunk_used, C_IN[L] + 14)
                for j in range(2):
                    act.wait_ge(f_o, FOX_H * L + 4 * j + 4)
                    act.copy(pair(xhi, j), pair(acc, j)).then_inc(xh_made, 1)
                for j in range(2):
                    act.wait_ge(r_o, RET_H * L + 4 * j + 4)
                    act.copy(pair(y, 2 + j), pair(acc, 2 + j)).then_inc(r_c, 1)
                for j in range(2):
                    act.wait_ge(r_yc, 2 * L + j + 1)
                    act.activation(pair(sq, j), pair(y, 2 + j), ACT.Square).then_inc(r_sq, 1)
                for j in range(2):
                    act.wait_ge(r_var, 2 * L + j + 1)
                    power(rs[:, j * 512:j * 512 + 512], acc_bank(2 + j), 1 / 64, GN_EPS).then_inc(r_rs, 1)
                split_hi(act, C_OUT[L] + 1 + AHEAD)
                for j in range(2):
                    act.wait_ge(h_made, H_OF[X + 1] + j + 1)
                    act.copy(pair(xhi, 2 + j), pair(y, 2 + j)).then_inc(xh_made, 1)
                for j in (2, 3):
                    split_hi(act, C_OUT[L] + j + AHEAD)
                act.wait_ge(chunk_used, C_OUT[L] + 4)
                for j in range(4):
                    weighted_high(3 * L + 1, "ffn_w", 8 * L, j)
                squares_of_h(3 * L + 1)
                ffn(L)
                load_exp_ln()
                for j in range(4):
                    weighted_high(3 * L + 2, "ple_w", 8 * L, j)
                ahead(C_PROJ[L], 1)
                squares_of_h(3 * L + 2)
                split_hi(act, C_GATE[L] + AHEAD)
                inverse_root(4 + 3 * L + 2, bank(3)[:, 0:S], RMS_EPS)
                for j in range(4):
                    if 1 <= j < 3:
                        split_hi(act, C_GATE[L] + j + AHEAD)
                    if j == 3 and L + 1 < DEPTH:
                        act.wait_ge(chunk_used, C_GATE[L] + 4)
                        for i in range(2):
                            weighted_high(3 * L + 3, "attn_w", 8 * L + 8, i)
                    act.wait_ge(z_scaled, 4 * L + j + 1)
                    z = kf[:, j * 512:j * 512 + 512]
                    act.activation(z, z, ACT.Sigmoid).then_inc(sig_made, 1)
                if L + 1 < DEPTH:
                    for j in range(2, 4):
                        weighted_high(3 * L + 3, "attn_w", 8 * L + 8, j)
                load_exp_ln()
                split_hi(act, C_GATE[L] + 3 + AHEAD)
            squares_of_h(6)
            inverse_root(4 + 6, bank(0)[:, 0:S], RMS_EPS)

        @block.vector
        def _(dve):
            own = Own(dve, dve_own)

            def x_low(X, src, js=range(4)):
                for j in js:
                    dve.wait_ge(xh_made, 4 * X + j + 1)
                    dve.tensor_tensor(pair(xlo, j), src(j), pair(xhi, j).bitcast(f32), ALU.subtract).then_inc(x_made, 1)

            def ahead(c, n):
                for j in range(n):
                    split_lo(dve, c + j + AHEAD)

            def zero_acc(s, n):
                dve.wait_ge(s, n)
                dve.memset(acc[:, :, :], 0.0).then_inc(acc_zero, 1)

            def residual(j, psum):
                dve.scalar_tensor_tensor(pair(y, j), pair(hT, j), ALPHA, psum, ALU.mult, ALU.add).then_inc(y_made, 1)

            def layer_norm(n, X):
                dve.wait_ge(y_made, 4 * n + 4)
                dve.wait_ge(mean_done, n + 1)
                for j in range(4):
                    dve.scalar_tensor_tensor(pair(y, j), wide(bank(0)[:, 0:S], 2), -1 / D, pair(y, j), ALU.mult,
                                             ALU.add).then_inc(yc_made, 1)
                dve.wait_ge(yc_made, 4 * n + 4)
                dve.wait_ge(rs_made, n + 1)
                for j in range(4):
                    own.sync(dve.tensor_tensor(pair(y, j), pair(y, j), wide(rs1, 2), ALU.mult))
                    for t in (2 * j, 2 * j + 1):
                        ins = dve.tensor_scalar(hT[:, t, :], y[:, t, :], par("ln_g", 8 * n + t), par("ln_b", 8 * n + t),
                                                ALU.mult, ALU.add)
                    ins.then_inc(y_made if X is None else h_made, 1)
                    for i in ([j - 1] if j else []) + ([3] if j == 3 else []):
                        if X is None:
                            weighted_low(6, "attn_w", 0, [i])
                        else:
                            x_low(X, lambda i: pair(hT, i), [i])

            def weighted_low(X, w, i0, js=range(4)):
                for j in js:
                    dve.wait_ge(xh_made, 4 * X + j + 1)
                    for t in (2 * j, 2 * j + 1):
                        ins = dve.scalar_tensor_tensor(xlo[:, t, :], hT[:, t, :], par(w, i0 + t),
                                                       xhi[:, t, :].bitcast(f32), ALU.mult, ALU.subtract)
                    ins.then_inc(x_made, 1)

            def final_norm():
                dve.wait_ge(rs_made, 4 + 6 + 1)
                for j in range(4):
                    for t in (2 * j, 2 * j + 1):
                        ins = dve.scalar_tensor_tensor(y[:, t, :], hT[:, t, :], par("fin_w", t), rs1, ALU.mult, ALU.mult)
                    ins.then_inc(out_made, 1)

            def mlp(n):
                c0, free, h0 = C_MLP[n], FREE[f"mlp{n}"], N_UP * n

                def hidden(i, m=0):
                    s = i % 3
                    dve.wait_ge(gemm_free, m * 3 + (free + i + 1))
                    dve.tensor_tensor(pair(kT, s), pair(qT, s), pair(qT, s), ALU.mult).then_inc(hid_sq, 1)
                    dve.wait_ge(hid_sq, m * 3 + (h0 + i + 1))
                    dve.wait_ge(hid_hi, m * 3 + (h0 + i + 1))
                    dve.tensor_tensor(hlo[:, s, :, :], pair(kT, s), hhi[:, s, :, :].bitcast(f32),
                                      ALU.subtract).then_inc(hid_lo, 1)

                split_lo(dve, c0 + AHEAD)
                hidden(0)
                with dve.Fori(0, (N_UP - 1) // 3) as m:
                    for i in range(1, 4):
                        cu = c0 + 2 * i - 1
                        split_lo(dve, cu + AHEAD, m)
                        hidden(i, m)
                        split_lo(dve, cu + 1 + AHEAD, m)
                split_lo(dve, c0 + 2 * N_UP - 1 + AHEAD)

            def acc_ready(inst, c, j):
                if j < 3:
                    dve.wait_ge(acc_done, 3 * inst + j + 1)
                else:
                    dve.wait_ge(chunk_used, c + 1)

            def ffn(L):
                c0, b = C_FFN[L], N_FF * L
                pads = qf[:, 0:1032].rearrange("p (a s) -> p a s", a=4)[:, :, 0:2]
                own.sync(dve.memset(pads, 0.0))

                def a_part(c, i, m=0):
                    s = i % 2
                    dve.wait_ge(chunk_used, m * RAW + (c + 1))
                    pad = qf[:, s * 516:s * 516 + 516].rearrange("p (t s) -> p t s", t=2)
                    dve.tensor_tensor(pad[:, :, 2:258], two(bank(2 * s)), wide(rs1, 2), ALU.mult).then_inc(a_copied, 1)

                def conv(i, m=0):
                    s = i % 2
                    dve.wait_ge(a_copied, m * 2 + (b + i + 1))
                    for step in range(3):
                        for t in range(2):
                            o = kf[:, s * 512 + t * 256:s * 512 + t * 256 + 256]
                            at = s * 516 + t * 258 + 2 - step
                            tile = m * 4 + (2 * i + t)
                            w = pv[:, bass.ds(tile + (PV["conv_w"] + (3 * L + 2 - step) * FT), 1)]
                            if step == 0:
                                bias = pv[:, bass.ds(tile + (PV["conv_b"] + L * FT), 1)]
                                ins = dve.tensor_scalar(o, qf[:, at:at + 256], w, bias, ALU.mult, ALU.add)
                            else:
                                ins = dve.scalar_tensor_tensor(o, qf[:, at:at + 256], w, o, ALU.mult, ALU.add)
                        ins.then_inc(conv_step if step < 2 else conv_made, 1)
                        if step < 2:
                            dve.wait_ge(conv_step, m * 4 + (2 * (b + i) + step + 1))

                def gated(c, i, m=0):
                    s = i % 2
                    dve.wait_ge(gelu_made, m * 2 + (b + i + 1))
                    a = two(kf[:, 1024 + s * 512:1536 + s * 512])
                    dve.tensor_tensor(a, a, wide(rs1, 2), ALU.mult).then_inc(gelu_scaled, 1)
                    dve.wait_ge(gelu_scaled, m * 2 + (b + i + 1))
                    dve.wait_ge(chunk_used, m * RAW + (c + 1))
                    dve.tensor_tensor(gf[:, s * 512:s * 512 + 512], kf[:, 1024 + s * 512:1536 + s * 512],
                                      bank(2 * s + 1), ALU.mult).then_inc(prod_made, 1)

                def low(i, m=0):
                    s = i % 2
                    dve.wait_ge(prod_made, m * 2 + (b + i + 1))
                    dve.wait_ge(prod_hi, m * 2 + (b + i + 1))
                    dve.tensor_tensor(hlo[:, s, :, :], two(gf[:, s * 512:s * 512 + 512]), hhi[:, s, :, :].bitcast(f32),
                                      ALU.subtract).then_inc(prod_lo, 1)

                split_lo(dve, c0 + AHEAD)
                dve.wait_ge(rs_made, 4 + 3 * L + 2)
                a_part(c0, 0)
                conv(0)
                split_lo(dve, c0 + 1 + AHEAD)
                gated(c0 + 1, 0)
                low(0)
                with dve.Fori(0, (N_FF - 1) // 2) as m:
                    for i in range(1, 3):
                        ca = c0 + 3 * i - 1
                        split_lo(dve, ca + AHEAD, m)
                        a_part(ca, i, m)
                        conv(i, m)
                        split_lo(dve, ca + 1 + AHEAD, m)
                        gated(ca + 1, i, m)
                        split_lo(dve, ca + 2 + AHEAD, m)
                        low(i, m)
                split_lo(dve, c0 + 3 * N_FF - 1 + AHEAD)

            x_low(0, lambda j: pair(hT, j))
            for c in range(AHEAD + 2):
                split_lo(dve, c)
            b4 = yf[:, 1024:2048]
            dve.wait_ge(g_ln, 1)
            dve.wait_ge(par_in, 5 * 16)
            dve.wait_ge(const_in, 16)
            for L in range(DEPTH):
                w = pv[:, PV["attn_w"] + 8 * L:PV["attn_w"] + 8 * L + 8].unsqueeze(2).to_broadcast([128, NT, FOX_H])
                ins = dve.tensor_tensor(wf_sb[:, L, :, :], wf_sb[:, L, :, :], w, ALU.mult)
            ins.then_inc(wf_made, 1)
            for h in range(GLA_H):
                n = own.mark(dve.tensor_scalar(yf[:, h * 256:h * 256 + 256], acc[:, 2 + h, :], par("b_a", h), 0.0,
                                               ALU.add, ALU.min))
            own.need(n)
            own.sync(dve.tensor_tensor(yf[:, 0:1024], yf[:, 0:1024], sqf[:, 0:1024], ALU.subtract))
            split_lo(dve, 2 + AHEAD)
            for h in range(GLA_H):
                s = slice(h * 256, h * 256 + 256)
                last = dve.tensor_tensor_scan(b4[:, s], scanm, yf[:, s], 0.0, ALU.mult, ALU.add)
            last.then_inc(g_cum, 1)
            dve.wait_ge(g_cum, 1)
            b3 = b4.rearrange("p (a c) -> p a c", c=64)
            dve.tensor_tensor(yf[:, 0:1024].rearrange("p (a c) -> p a c", c=64), b3[:, :, 63:64].to_broadcast([128, 16, 64]),
                              b3, ALU.subtract).then_inc(g_cum, 1)
            for c in (3, 4, 5):
                split_lo(dve, c + AHEAD)
            dve.wait_ge(gemm_free, 4)
            dve.wait_ge(g_exp, 1)
            for h in range(GLA_H):
                dve.tensor_tensor(kT[:, 4 + h, :], kT[:, h, :], y[:, h, :], ALU.mult).then_inc(g_kend, 1)
            split_lo(dve, 6 + AHEAD)
            dve.wait_ge(g_exp, 3)
            dve.wait_ge(g_kend, GLA_H)
            own.mark(dve.scalar_tensor_tensor(qf[:, 0:1024], qf[:, 0:1024], GLA_SCALE, sqf[:, 0:1024], ALU.mult, ALU.mult))
            dve.tensor_tensor(kf[:, 0:1024], kf[:, 0:1024], sqf[:, 1024:2048], ALU.mult).then_inc(g_dec, 1)
            for c in range(7, 12):
                split_lo(dve, c + AHEAD)
            for n in range(3):
                dve.wait_ge(g_ud, n + 1)
                for h in range(GLA_H):
                    u = ring[:, h // 2, (h % 2) * 256:(h % 2) * 256 + 256]
                    at = n * 1024 + h * 256
                    if n == 0:
                        ins = dve.tensor_copy(misc[:, at:at + 256], u)
                    else:
                        d = sqf[:, h * 256 + n * 64 + 63:h * 256 + n * 64 + 64]
                        ins = dve.scalar_tensor_tensor(misc[:, at:at + 256], misc[:, at - 1024:at - 768], d, u,
                                                       ALU.mult, ALU.add)
                ins.then_inc(g_st, 1)
                dve.wait_ge(g_st, n + 1)
            for j in range(2):
                dve.wait_ge(g_rs, j + 1)
                for h in (2 * j, 2 * j + 1):
                    own.sync(dve.tensor_tensor(pair(y, h), pair(acc, h), wide(rs[:, h * 256:h * 256 + 256], 2), ALU.mult))
                    for e in range(2):
                        t = 2 * h + e
                        ins = dve.scalar_tensor_tensor(y[:, t, :], y[:, t, :], par("gla_g", e), gT[:, t, :],
                                                       ALU.mult, ALU.mult)
                    ins.then_inc(h_made, 1)
                    x_low(1, lambda i: pair(y, i), [h])
            zero_acc(x_made, 8)

            def after_product(c, n):
                for j in range(4):
                    split_lo(dve, c + j + AHEAD)
                    dve.wait_ge(chunk_used, c + j + 1)
                    residual(j, two(bank(j)))

            def after_mlp(n):
                for j in range(4):
                    acc_ready(ZERO[f"mlp{n}"], C_MLP[n] + 2 * N_UP - 1, j)
                    residual(j, pair(acc, j))

            dve.wait_ge(x_made, 8)
            after_product(C_GLA_O, 0)
            layer_norm(0, 2)
            mlp(0)
            after_mlp(0)
            layer_norm(1, 3)

            ahead(C_SB_IN, 12)
            for h in range(SB_H):
                s = (h % 2) * 384
                dve.wait_ge(s_ln, h + 1)
                if h >= 2:
                    dve.wait_ge(s_lw, h - 1)
                dve.scalar_tensor_tensor(yf[:, s:s + 384], bank(h % 4)[:, 0:384], 0.0, gf[:, s:s + 384], ALU.max,
                                         ALU.add).then_inc(s_sp, 1)
            x_low(4, lambda j: pair(acc, j))
            zero_acc(x_made, 20)
            after_product(C_SB_O, 2)
            layer_norm(2, 5)
            mlp(1)
            after_mlp(1)
            layer_norm(3, None)

            def add_to_h(j, psum):
                dve.tensor_tensor(pair(hT, j), pair(hT, j), psum, ALU.add).then_inc(y_made, 1)

            for L in range(DEPTH):
                X = 6 + 4 * L
                if L:
                    weighted_low(X, "attn_w", 8 * L, (2, 3))
                    split_lo(dve, C_IN[L] - 1 + AHEAD)
                split_lo(dve, C_IN[L] + AHEAD)
                split_lo(dve, C_IN[L] + 1 + AHEAD)
                dve.wait_ge(rs_made, 4 + 3 * L + 1)
                dve.wait_ge(f_log, L + 1)
                dve.tensor_tensor(cum[:, 1, :], acc[0:FOX_H, 0, :], rs1[0:FOX_H, :], ALU.mult).then_inc(f_logit, 1)

                def scaled(j, dest, scale=1.0):
                    dve.wait_ge(chunk_used, C_IN[L] + j + 1)
                    if j in (6, 12):
                        dve.wait_ge(gemm_free, FREE[f"in{L}"] + j)
                    dve.scalar_tensor_tensor(dest, two(bank(in_bank(j))), scale, wide(rs1, 2), ALU.mult,
                                             ALU.mult).then_inc(gemm_free, 1)

                scaled(0, pair(qT, 0), 0.125)
                dve.wait_ge(f_ln, L + 1)
                own.sync(dve.tensor_scalar(cum[:, 1, :], cum[:, 1, :], fb_sb[:, L:L + 1], 0.0, ALU.add, ALU.min))
                own.sync(dve.tensor_tensor(cum[:, 1, :], cum[:, 1, :], cum[:, 0, :], ALU.subtract))
                own.sync(dve.tensor_tensor_scan(cum[:, 2, :], cst[0:FOX_H, CONST["ones"]:CONST["ones"] + S], cum[:, 1, :],
                                                0.0, ALU.mult, ALU.add))
                dve.scalar_tensor_tensor(y[0:FOX_H, :, :], wide(cum[:, 2, :], FOX_H), -1.0,
                                         ident[0:FOX_H, 0:FOX_H].unsqueeze(2).to_broadcast([FOX_H, FOX_H, S]),
                                         ALU.mult, ALU.mult).then_inc(f_cum, 1)
                scaled(1, pair(qT, 1), 0.125)
                for j in (2, 3):
                    split_lo(dve, C_IN[L] + j + AHEAD)
                    scaled(j, pair(kT, j - 2))
                split_lo(dve, C_IN[L] + 4 + AHEAD)

                def rotary(n):
                    t, turned = (kT if n else qT)[:, 4:8, :], gT[:, 0:4, :]
                    dve.wait_ge(r_rot, 2 * L + n + 1)
                    own.mark(dve.tensor_tensor(t, t, wide(cosT, 4), ALU.mult))
                    own.sync(dve.tensor_tensor(turned, acc[:, 4:8, :], wide(sinT, 4), ALU.mult))
                    dve.tensor_tensor(t, t, turned, ALU.add).then_inc(r_rdy, 1)

                for j in range(4, 14):
                    h, st = j - 4, stat[:, (j - 4) % 4, :]
                    P = sqf[:, (h % 3) * 384:(h % 3) * 384 + 384]
                    if 6 <= j < 8:
                        scaled(j, pair(qT, j - 4))
                    elif 8 <= j < 10:
                        scaled(j, pair(kT, j - 6), 0.125)
                    elif j >= 12:
                        dve.wait_ge(r_rdy, 2 * L + 2)
                        scaled(j, pair(gT, j - 12))
                    if h < FOX_H:
                        b = bank(2)
                        dve.wait_ge(f_z, FOX_H * L + h + 1)
                        if h >= 3:
                            dve.wait_ge(f_td, FOX_H * L + h - 2)
                        own.mark(dve.tensor_tensor_reduce(P[:, 0:128], b[:, 0:128], maskadd[:, 0:128], 1.0, -3.0e38,
                                                          ALU.add, ALU.max, st[:, 0:1]))
                        own.sync(dve.tensor_tensor_reduce(P[:, 128:384], b[:, 128:384], maskadd[:, 128:384], 1.0, -3.0e38,
                                                          ALU.add, ALU.max, st[:, 1:2]))
                        dve.tensor_scalar(st[:, 2:4], st[:, 0:2], -1.0, None, ALU.mult).then_inc(f_mx, 1)
                    if j < 13:
                        split_lo(dve, C_IN[L] + j + 1 + AHEAD)
                    if h < FOX_H:
                        dve.wait_ge(f_e, FOX_H * L + h + 1)
                        own.sync(dve.reciprocal(st[:, 6:8], st[:, 4:6]))
                        dve.tensor_scalar(P[:, 0:128], P[:, 0:128], st[:, 6:7], None, ALU.mult)
                        dve.tensor_scalar(P[:, 128:384], P[:, 128:384], st[:, 7:8], None, ALU.mult).then_inc(f_p, 1)
                    if j in (8, 10):
                        rotary((j - 8) // 2)
                    if j == 9:
                        dve.wait_ge(p_hi, L + 1)
                        dve.tensor_tensor(hlo[:, 2, :, :], two(gf[:, 1024:1536]), hhi[:, 2, :, :].bitcast(f32),
                                          ALU.subtract).then_inc(p_lo, 1)
                dve.wait_ge(dec_in, 16)
                for h in range(RET_H):
                    s, b = (h % 3) * 384, bank((2 + h) % 4)
                    dve.wait_ge(r_s, RET_H * L + h + 1)
                    if h >= 3:
                        dve.wait_ge(r_o, RET_H * L + h - 2)
                    dve.tensor_tensor(sqf[:, s:s + 256], b[:, 0:256], dec[:, h, :], ALU.mult)
                    dve.tensor_tensor(sqf[:, s + 256:s + 384], b[:, 256:384], dec[:, h, 0:128],
                                      ALU.mult).then_inc(r_m, 1)
                    if h == 2:
                        split_lo(dve, C_OUT[L] + AHEAD)
                    if h in (3, 5):
                        x_low(X + 1, lambda j: pair(acc, j), [(h - 3) // 2])
                for j in range(2):
                    dve.wait_ge(r_mean, 2 * L + j + 1)
                    dve.scalar_tensor_tensor(pair(y, 2 + j), pair(acc, 2 + j), -1 / 64, pair(y, 2 + j), ALU.mult,
                                             ALU.add).then_inc(r_yc, 1)
                dve.wait_ge(r_yc, 2 * L + 2)
                for j in range(2):
                    r, t = rs[:, j * 512:j * 512 + 512], yf[:, 1024 + j * 512:1536 + j * 512]
                    dve.wait_ge(r_rs, 2 * L + j + 1)
                    own.sync(dve.tensor_tensor(t, t, r, ALU.mult))
                    dve.wait_ge(silu_made, 2 * L + j + 1)
                    dve.tensor_tensor(t, t, gf[:, j * 512:j * 512 + 512], ALU.mult).then_inc(h_made, 1)
                    x_low(X + 1, lambda i: pair(y, i), [2 + j])
                split_lo(dve, C_OUT[L] + 1 + AHEAD)
                zero_acc(x_made, 4 * (X + 1) + 4)
                split_lo(dve, C_OUT[L] + 2 + AHEAD)
                for j in range(4):
                    if j < 3:
                        dve.wait_ge(out_done, 3 * L + j + 1)
                    else:
                        dve.wait_ge(chunk_used, C_OUT[L] + 4)
                    add_to_h(j, two(bank(j)))
                weighted_low(X + 2, "ffn_w", 8 * L)
                split_lo(dve, C_OUT[L] + 3 + AHEAD)
                ffn(L)
                for j in range(4):
                    acc_ready(ZERO[f"ffn{L}"], C_FFN[L] + 3 * N_FF - 1, j)
                    add_to_h(j, pair(acc, j))
                weighted_low(X + 3, "ple_w", 8 * L)
                split_lo(dve, C_PROJ[L] + AHEAD)
                for j in range(4):
                    if j < 3:
                        split_lo(dve, C_GATE[L] + j + AHEAD)
                    if j == 0:
                        dve.wait_ge(rs_made, 4 + 3 * L + 3)
                    dve.wait_ge(chunk_used, C_GATE[L] + j + 1)
                    dve.tensor_tensor(pair(kT, j), two(bank(j)), wide(rs1, 2), ALU.mult).then_inc(z_scaled, 1)
                    if j == 3 and L + 1 < DEPTH:
                        weighted_low(X + 4, "attn_w", 8 * L + 8, (0, 1))
                    dve.wait_ge(sig_made, 4 * L + j + 1)
                    own.sync(dve.tensor_tensor(pair(kT, j), pair(kT, j), pair(acc, j), ALU.mult))
                    add_to_h(j, pair(kT, j))
            final_norm()

        @block.gpsimd
        def _(pool):
            own = Own(pool, pool_own)
            for t in range(2):
                pool.wait_ge(g_attc, t + 1)
                a = sqf[:, 1024 + t * 512:1536 + t * 512]
                own.sync(pool.affine_select(out=a, in_=a, compare_op=ALU.is_ge, fill=0.0, base=0,
                                            pattern=[[0, 4], [1, 128]], channel_multiplier=-1))
                b = a.rearrange("p (h c) -> p h c", h=4)[:, :, 64:128]
                pool.affine_select(out=b, in_=b, compare_op=ALU.is_ge, fill=0.0, base=-64,
                                   pattern=[[0, 4], [0, 64]], channel_multiplier=1).then_inc(g_attm, 1)

            def strict(buf):
                d = buf.rearrange("p (b s) -> p b s", b=3)[:, 0:3:2, :]
                return pool.affine_select(out=d, in_=d, compare_op=ALU.is_gt, fill=0.0, base=0,
                                          pattern=[[0, 2], [1, 128]], channel_multiplier=-1)

            for i in range(SB_H + 2):
                if i < SB_H:
                    pool.wait_ge(s_sp, i + 1)
                    strict(yf[:, (i % 2) * 384:(i % 2) * 384 + 384]).then_inc(s_L, 1)
                if i >= 2:
                    h = i - 2
                    pool.wait_ge(s_w, h + 1)
                    strict(sqf[:, (h % 3) * 384:(h % 3) * 384 + 384]).then_inc(s_wm, 1)


def _tiles(a, n=None):
    return np.ascontiguousarray(a.reshape(-1, 128, a.shape[-1]).transpose(1, 0, 2))


def _cols(w):
    n = w.shape[1] // 256
    return w.reshape(NT, 128, n, 256).transpose(2, 1, 0, 3).reshape(n, 128, CW)


def _rows(w):
    n = w.shape[0] // 256
    return w.reshape(n, 2, 128, D).transpose(0, 2, 1, 3).reshape(n, 128, CW)


def _stream(i):
    w = i["gla_w_in"][0]
    parts = [_cols(w[:, 0:3072]), _cols(i["gla_w_o"][0])]

    def mlp(n):
        up, down = _cols(i["mlp_w_up"][n]), _rows(i["mlp_w_down"][n])
        parts.append(up[0:1])
        for s in range(1, N_UP):
            parts.extend([up[s:s + 1], down[s - 1:s]])
        parts.append(down[N_UP - 1:])

    mlp(0)
    parts.extend([_cols(i["kv_w"]), _cols(i["sb_w_q"][0]), _cols(i["sb_w_o"][0])])
    mlp(1)
    for n in range(DEPTH):
        w = i["w_in_2"][n]
        fq, fk, fv, rq, rk, rv, rg = (w[:, a:a + 512] for a in (0, 512, 1024, 1544, 2056, 2568, 3080))
        parts.extend(_cols(p) for p in (fq, fk, fv, rq, rk, rv, rg))
        parts.append(_rows(i["w_out_2"][n]))
        up, down = i["w_up_2"][n], _rows(i["w_down_2"][n])
        a, g = _cols(up[:, :FF2]), _cols(up[:, FF2:])
        parts.extend([a[0:1], g[0:1]])
        for s in range(1, N_FF):
            parts.extend([a[s:s + 1], g[s:s + 1], down[s - 1:s]])
        parts.append(down[N_FF - 1:])
        parts.extend([_rows(i["w_ple_proj_2"][n]), _cols(i["w_ple_gate_2"][n])])
    return np.concatenate(parts, axis=0)


def _params(i):
    def c(a):
        return np.asarray(a).reshape(-1, 128).T

    return np.ascontiguousarray(np.concatenate([
        c(i["ln_g"]), c(i["ln_b"]), c(i["gla_b_a"]), c(i["gla_norm_g"]), c(i["attn_norm_w_2"]), c(i["ffn_norm_w_2"]),
        c(i["ple_norm_w_2"]), c(i["final_norm_w_2"]), c(i["conv_w_2"]), c(i["conv_b_2"])], axis=1))


def _constants():
    p, f = np.arange(128)[:, None], np.arange(128)[None, :]
    causal = np.where(f > p, -3.0e38, 0.0)
    d = p % 64
    source = np.where(d < 32, p + 32, p - 32)
    perm = np.where(f == source, np.where(d < 32, -1.0, 1.0), 0.0).T
    inv = (np.float32(10000.0) ** (-np.arange(0, 64, 2, dtype=np.float32) / np.float32(64))).astype(np.float32)
    ang = (np.arange(S, dtype=np.float32)[None, :] * inv[np.arange(128) % 32][:, None]).astype(np.float32)
    scan = np.where(np.arange(S) % 64 == 0, 0.0, 1.0)[None, :] * np.ones((128, 1))
    parts = dict(ident=p == f, ones=np.ones((128, 256)), blk=p // 64 == f // 64, tri=-(p >= f).astype(float),
                 neg=-np.ones((128, 128)), perm=perm, scan=scan,
                 mask=np.concatenate([causal, np.zeros((128, 128)), causal], axis=1), cos=np.cos(ang), sin=np.sin(ang),
                 eps=np.tile([LN_EPS, RMS_EPS], (128, 1)))
    assert list(parts) == list(CONST)
    return np.concatenate([np.asarray(a, np.float32) for a in parts.values()], axis=1)


def _decays():
    gamma = 1.0 - np.exp2(-5.0 - np.arange(RET_H))
    i, j = np.arange(S)[None, None, :], np.arange(128)[:, None, None]
    lg = np.log1p(-np.exp2(-5.0 - np.arange(RET_H)))[None, :, None]
    t = np.where(i >= j, np.exp(lg * np.maximum(i - j, 0)), 0.0)
    return t.reshape(128, RET_H * S).astype(np.float32)


def kernel(**inputs):
    import concourse.bacc as bacc
    from concourse.bass_utils import run_bass_kernel_spmd

    i = {k: np.asarray(a) for k, a in inputs.items()}
    arrays = dict(
        xT=_tiles(i["x"][0].T),
        wstream=_stream(i),
        wa1=_tiles(i["gla_w_in"][0][:, 3072:3088]),
        wa2=np.ascontiguousarray(i["gla_w_a2"][0]),
        wf=np.ascontiguousarray(np.stack([_tiles(i["w_in_2"][n][:, 1536:1544]) for n in range(DEPTH)], axis=1)),
        fbias=np.ascontiguousarray(i["forget_bias_2"].T),
        pT=np.stack([_tiles(i["p_2"][n, 0].T) for n in range(DEPTH)]),
        params=_params(i),
        consts=_constants(),
        decay=_decays(),
    )
    nc = bacc.Bacc("TRN2", target_bir_lowering=False, num_devices=1)
    aps = {n: nc.dram_tensor(n, a.shape, mybir.dt.from_np(a.dtype), kind="ExternalInput").ap() for n, a in arrays.items()}
    aps["out"] = nc.dram_tensor("out", (128, NT, S), mybir.dt.float32, kind="ExternalOutput").ap()
    build_program(nc, **aps)
    got = run_bass_kernel_spmd(nc, [arrays], core_ids=[0]).results[0]["out"]
    return np.ascontiguousarray(got.transpose(2, 1, 0).reshape(1, S, D))
```
